# Optimizing a Trainium2 kernel written in Bass

```python
import jax, jax.numpy as jnp
from jax import lax
import numpy as np

D_MODEL = 1024
BATCH = 1
SEQ = 256
DEPTH = 2

PLE_DIM = 256
D_MIX = D_MODEL
CONV_WIDTH = D_MIX // 4
CONV_GROUPS = 4
CONV_KERNEL = 31
SSD_WIDTH = D_MIX // 2
SSD_HEADDIM = 64
SSD_HEADS = SSD_WIDTH // SSD_HEADDIM
SSD_NGROUPS = 2
SSD_STATE = 128
SSD_CONV = 4
SSD_CHUNK = 128
MLA_HEADS = 4
MLA_NOPE_DIM = 64
MLA_ROPE_DIM = 32
MLA_V_DIM = D_MIX // 4 // MLA_HEADS
MLA_WIDTH = MLA_HEADS * MLA_V_DIM
MLA_Q_RANK = D_MODEL // 4
MLA_KV_RANK = D_MODEL // 8
ROPE_BASE = 10000.0
Q_BLOCK = 128
D_FF = 7 * D_MODEL // 2
N_EXPERTS = 8
TOP_K = 2
MOE_BLOCK = 128
N_DENSE = (DEPTH + 1) // 2
N_MOE = DEPTH // 2
CONV_IN = 2 * CONV_WIDTH
SSD_XBC = SSD_WIDTH + 2 * SSD_NGROUPS * SSD_STATE
IN_COLS = CONV_IN + SSD_WIDTH + SSD_XBC + SSD_HEADS + MLA_Q_RANK + MLA_KV_RANK + MLA_ROPE_DIM
RMS_EPS = 1e-6
LN_EPS = 1e-5

kernel_name = 'hybrid_conv_ssd_mla_moe_ple_trunk'

def rms_norm(x, g):
    xf = x.astype(jnp.float32)
    y = xf * lax.rsqrt(jnp.mean(xf * xf, axis=-1, keepdims=True) + RMS_EPS)
    return (y * g.astype(jnp.float32)).astype(x.dtype)

def causal_depthwise_conv(x, w, b):
    k, c = w.shape
    y = lax.conv_general_dilated(x, w.astype(x.dtype)[:, None, :], window_strides=(1,),
                                 padding=((k - 1, 0),), dimension_numbers=('NWC', 'WIO', 'NWC'),
                                 feature_group_count=c)
    return y + b.astype(x.dtype)

def split_in(u):
    sizes = (CONV_IN, SSD_WIDTH, SSD_XBC, SSD_HEADS, MLA_Q_RANK, MLA_KV_RANK, MLA_ROPE_DIM)
    points = np.cumsum(sizes)[:-1].tolist()
    return jnp.split(u, points, axis=-1)

def conformer_conv(u, dw_w, dw_b, ln_g, ln_b):
    val, gate = jnp.split(u, 2, axis=-1)
    h = causal_depthwise_conv(val * jax.nn.sigmoid(gate), dw_w, dw_b)
    b, s, c = h.shape
    hg = h.astype(jnp.float32).reshape(b, s, CONV_GROUPS, c // CONV_GROUPS)
    mu = jnp.mean(hg, axis=-1, keepdims=True)
    var = jnp.mean(jnp.square(hg - mu), axis=-1, keepdims=True)
    hn = ((hg - mu) * lax.rsqrt(var + LN_EPS)).reshape(b, s, c)
    hn = hn * ln_g.astype(jnp.float32) + ln_b.astype(jnp.float32)
    return jax.nn.silu(hn).astype(u.dtype)

def ssd_chunked(x, dt, a, bm, cm):
    b, s, h, pd = x.shape
    g, n = bm.shape[2], bm.shape[3]
    r = h // g
    c, L = s // SSD_CHUNK, SSD_CHUNK
    xd = (x * dt[..., None]).reshape(b, c, L, g, r, pd)
    adt = (dt * a).reshape(b, c, L, g, r).transpose(0, 3, 4, 1, 2)
    a_cs = jnp.cumsum(adt, axis=-1)
    bc = bm.reshape(b, c, L, g, n)
    cc = cm.reshape(b, c, L, g, n)
    causal = jnp.tril(jnp.ones((L, L), dtype=bool))
    seg = a_cs[..., :, None] - a_cs[..., None, :]
    decay = jnp.exp(jnp.where(causal, seg, -jnp.inf))
    cb = jnp.einsum('bclgn,bcsgn->bgcls', cc, bc)
    mix = cb[:, :, None] * decay
    y_diag = jnp.einsum('bgrcls,bcsgrp->bclgrp', mix, xd)
    decay_states = jnp.exp(a_cs[..., -1:] - a_cs)
    states = jnp.einsum('bclgn,bgrcl,bclgrp->cbgrpn', bc, decay_states, xd)
    chunk_decay = jnp.moveaxis(jnp.exp(a_cs[..., -1]), -1, 0)

    def step(carry, inp):
        st, dec = inp
        return carry * dec[..., None, None] + st, carry

    init = jnp.zeros((b, g, r, pd, n), jnp.float32)
    _, prev = lax.scan(step, init, (states, chunk_decay))
    y_off = jnp.einsum('bclgn,cbgrpn,bgrcl->bclgrp', cc, prev, jnp.exp(a_cs))
    return (y_diag + y_off).reshape(b, s, h, pd)

def ssd_mixer(z, xbc, dt_raw, conv_w, conv_b, dt_bias, a_log, d_skip, norm_g):
    b, s, _ = xbc.shape
    xbc = jax.nn.silu(causal_depthwise_conv(xbc, conv_w, conv_b)).astype(jnp.float32)
    gn = SSD_NGROUPS * SSD_STATE
    xs = xbc[..., :SSD_WIDTH].reshape(b, s, SSD_HEADS, SSD_HEADDIM)
    bm = xbc[..., SSD_WIDTH:SSD_WIDTH + gn].reshape(b, s, SSD_NGROUPS, SSD_STATE)
    cm = xbc[..., SSD_WIDTH + gn:].reshape(b, s, SSD_NGROUPS, SSD_STATE)
    dt = jax.nn.softplus(dt_raw.astype(jnp.float32) + dt_bias.astype(jnp.float32))
    a = -jnp.exp(a_log.astype(jnp.float32))
    y = ssd_chunked(xs, dt, a, bm, cm) + d_skip.astype(jnp.float32)[:, None] * xs
    yg = (y.reshape(b, s, SSD_WIDTH) * jax.nn.silu(z.astype(jnp.float32)))
    yg = yg.reshape(b, s, SSD_NGROUPS, SSD_WIDTH // SSD_NGROUPS)
    yg = yg * lax.rsqrt(jnp.mean(yg * yg, axis=-1, keepdims=True) + RMS_EPS)
    return (yg.reshape(b, s, SSD_WIDTH) * norm_g.astype(jnp.float32)).astype(z.dtype)

def rope_tables(positions, dtype):
    inv = ROPE_BASE ** (-jnp.arange(0, MLA_ROPE_DIM, 2, dtype=jnp.float32) / MLA_ROPE_DIM)
    ang = positions.astype(jnp.float32)[..., None] * inv
    return jnp.cos(ang).astype(dtype), jnp.sin(ang).astype(dtype)

def apply_rope(x, cos, sin):
    half = x.shape[-1] // 2
    x1, x2 = x[..., :half], x[..., half:]
    return jnp.concatenate([x1 * cos - x2 * sin, x1 * sin + x2 * cos], axis=-1)

def mla_mixer(c_q, c_kv, k_rope, q_norm_g, w_uq, kv_norm_g, w_ukv, cos, sin):
    b, s, _ = c_q.shape
    q = (rms_norm(c_q, q_norm_g) @ w_uq).reshape(b, s, MLA_HEADS, MLA_NOPE_DIM + MLA_ROPE_DIM)
    q_nope, q_pe = q[..., :MLA_NOPE_DIM], q[..., MLA_NOPE_DIM:]
    kv = (rms_norm(c_kv, kv_norm_g) @ w_ukv).reshape(b, s, MLA_HEADS, MLA_NOPE_DIM + MLA_V_DIM)
    k_nope, v = kv[..., :MLA_NOPE_DIM], kv[..., MLA_NOPE_DIM:]
    q_pe = apply_rope(q_pe, cos[:, :, None, :], sin[:, :, None, :])
    k_pe = apply_rope(k_rope, cos, sin)
    scale = (MLA_NOPE_DIM + MLA_ROPE_DIM) ** -0.5
    outs = []
    for blk in range(s // Q_BLOCK):
        q0, q1 = blk * Q_BLOCK, (blk + 1) * Q_BLOCK
        sc = (jnp.einsum('bqhd,bkhd->bhqk', q_nope[:, q0:q1], k_nope[:, :q1])
              + jnp.einsum('bqhd,bkd->bhqk', q_pe[:, q0:q1], k_pe[:, :q1])).astype(jnp.float32) * scale
        mask = (q0 + jnp.arange(Q_BLOCK))[:, None] >= jnp.arange(q1)[None, :]
        pr = jax.nn.softmax(jnp.where(mask, sc, -jnp.inf), axis=-1).astype(v.dtype)
        outs.append(jnp.einsum('bhqk,bkhd->bqhd', pr, v[:, :q1]))
    return jnp.concatenate(outs, axis=1).reshape(b, s, MLA_WIDTH)

def swiglu(h, wg, wu, wd):
    return (jax.nn.silu(h @ wg) * (h @ wu)) @ wd

def moe_top2(h, router, wg, wu, wd):
    b, s, d = h.shape
    t = b * s
    hf = h.reshape(t, d)
    logits = (hf @ router).astype(jnp.float32)
    top_val, top_idx = lax.top_k(logits, TOP_K)
    gates = jax.nn.softmax(top_val, axis=-1)
    e_flat = top_idx.reshape(-1)
    tok_flat = jnp.arange(t * TOP_K, dtype=jnp.int32) // TOP_K
    g_flat = gates.reshape(-1)
    order = jnp.argsort(e_flat)
    e_sorted = e_flat[order]
    counts = jnp.zeros((N_EXPERTS,), jnp.int32).at[e_flat].add(1)
    padded = ((counts + MOE_BLOCK - 1) // MOE_BLOCK) * MOE_BLOCK
    starts = jnp.cumsum(counts) - counts
    pends = jnp.cumsum(padded)
    pstarts = pends - padded
    dest = pstarts[e_sorted] + (jnp.arange(t * TOP_K, dtype=jnp.int32) - starts[e_sorted])
    n_blocks = -(-(t * TOP_K) // MOE_BLOCK) + N_EXPERTS
    n_slots = n_blocks * MOE_BLOCK
    slot_tok = jnp.full((n_slots,), t, jnp.int32).at[dest].set(tok_flat[order])
    slot_gate = jnp.zeros((n_slots,), jnp.float32).at[dest].set(g_flat[order])
    block_exp = jnp.minimum(jnp.searchsorted(pends, jnp.arange(n_blocks) * MOE_BLOCK, side='right'),
                            N_EXPERTS - 1)
    x_pad = jnp.concatenate([hf, jnp.zeros((1, d), hf.dtype)], axis=0)
    xb = x_pad[slot_tok].reshape(n_blocks, MOE_BLOCK, d)

    def expert_block(args):
        xblk, e = args
        return swiglu(xblk, wg[e], wu[e], wd[e])

    yb = lax.map(expert_block, (xb, block_exp))
    ys = yb.reshape(n_slots, d) * slot_gate[:, None].astype(h.dtype)
    y = jnp.zeros((t + 1, d), h.dtype).at[slot_tok].add(ys)[:t]
    return y.reshape(b, s, d)

def setup_inputs(seed: int = 0) -> dict:
    key = jax.random.key(seed)
    ks = jax.random.split(key, 40)
    f32 = jnp.float32

    def nrm(k, shape, scale):
        return jax.random.normal(k, shape, f32) * scale

    def gain(k, shape):
        return 1.0 + 0.05 * jax.random.normal(k, shape, f32)

    dt = jnp.exp(jax.random.uniform(ks[11], (DEPTH, SSD_HEADS), f32)
                 * (jnp.log(0.1) - jnp.log(0.001)) + jnp.log(0.001))
    return {
        'x': nrm(ks[0], (BATCH, SEQ, D_MODEL), 1.0),
        'p': nrm(ks[1], (DEPTH, BATCH, SEQ, PLE_DIM), 1.0),
        'positions': jnp.arange(SEQ, dtype=jnp.int32)[None, :]
                     + jax.random.randint(ks[2], (BATCH, 1), 0, 1024, dtype=jnp.int32),
        'attn_norm_g': gain(ks[3], (DEPTH, D_MODEL)),
        'w_in': nrm(ks[4], (DEPTH, D_MODEL, IN_COLS), D_MODEL ** -0.5),
        'conv_dw_w': nrm(ks[5], (DEPTH, CONV_KERNEL, CONV_WIDTH), CONV_KERNEL ** -0.5),
        'conv_dw_b': nrm(ks[6], (DEPTH, CONV_WIDTH), 0.02),
        'conv_ln_g': gain(ks[7], (DEPTH, CONV_WIDTH)),
        'conv_ln_b': nrm(ks[8], (DEPTH, CONV_WIDTH), 0.02),
        'ssd_conv_w': nrm(ks[9], (DEPTH, SSD_CONV, SSD_XBC), SSD_CONV ** -0.5),
        'ssd_conv_b': nrm(ks[10], (DEPTH, SSD_XBC), 0.02),
        'ssd_dt_bias': dt + jnp.log(-jnp.expm1(-dt)),
        'ssd_a_log': jnp.log(jax.random.uniform(ks[12], (DEPTH, SSD_HEADS), f32, 1.0, 16.0)),
        'ssd_d': gain(ks[13], (DEPTH, SSD_HEADS)),
        'ssd_norm_g': gain(ks[14], (DEPTH, SSD_WIDTH)),
        'mla_q_norm_g': gain(ks[15], (DEPTH, MLA_Q_RANK)),
        'mla_w_uq': nrm(ks[16], (DEPTH, MLA_Q_RANK, MLA_HEADS * (MLA_NOPE_DIM + MLA_ROPE_DIM)), MLA_Q_RANK ** -0.5),
        'mla_kv_norm_g': gain(ks[17], (DEPTH, MLA_KV_RANK)),
        'mla_w_ukv': nrm(ks[18], (DEPTH, MLA_KV_RANK, MLA_HEADS * (MLA_NOPE_DIM + MLA_V_DIM)), MLA_KV_RANK ** -0.5),
        'w_out': nrm(ks[19], (DEPTH, D_MIX, D_MODEL), D_MIX ** -0.5),
        'ffn_norm_g': gain(ks[20], (DEPTH, D_MODEL)),
        'dense_w_gate': nrm(ks[21], (N_DENSE, D_MODEL, D_FF), D_MODEL ** -0.5),
        'dense_w_up': nrm(ks[22], (N_DENSE, D_MODEL, D_FF), D_MODEL ** -0.5),
        'dense_w_down': nrm(ks[23], (N_DENSE, D_FF, D_MODEL), D_FF ** -0.5),
        'moe_router': nrm(ks[24], (N_MOE, D_MODEL, N_EXPERTS), D_MODEL ** -0.5),
        'moe_w_gate': nrm(ks[25], (N_MOE, N_EXPERTS, D_MODEL, D_FF), D_MODEL ** -0.5),
        'moe_w_up': nrm(ks[26], (N_MOE, N_EXPERTS, D_MODEL, D_FF), D_MODEL ** -0.5),
        'moe_w_down': nrm(ks[27], (N_MOE, N_EXPERTS, D_FF, D_MODEL), D_FF ** -0.5),
        'ple_norm_g': gain(ks[28], (DEPTH, D_MODEL)),
        'ple_w_gate': nrm(ks[29], (DEPTH, D_MODEL, D_MODEL), D_MODEL ** -0.5),
        'ple_w_proj': nrm(ks[30], (DEPTH, PLE_DIM, D_MODEL), PLE_DIM ** -0.5),
        'final_norm_g': gain(ks[31], (D_MODEL,)),
    }

def reference(x, p, positions, attn_norm_g, w_in, conv_dw_w, conv_dw_b, conv_ln_g, conv_ln_b,
              ssd_conv_w, ssd_conv_b, ssd_dt_bias, ssd_a_log, ssd_d, ssd_norm_g,
              mla_q_norm_g, mla_w_uq, mla_kv_norm_g, mla_w_ukv, w_out, ffn_norm_g,
              dense_w_gate, dense_w_up, dense_w_down, moe_router, moe_w_gate, moe_w_up, moe_w_down,
              ple_norm_g, ple_w_gate, ple_w_proj, final_norm_g):
    h = x
    cos, sin = rope_tables(positions, x.dtype)
    for i in range(DEPTH):
        u = rms_norm(h, attn_norm_g[i]) @ w_in[i]
        u_conv, z, xbc, dt_raw, c_q, c_kv, k_rope = split_in(u)
        y_conv = conformer_conv(u_conv, conv_dw_w[i], conv_dw_b[i], conv_ln_g[i], conv_ln_b[i])
        y_ssd = ssd_mixer(z, xbc, dt_raw, ssd_conv_w[i], ssd_conv_b[i], ssd_dt_bias[i],
                          ssd_a_log[i], ssd_d[i], ssd_norm_g[i])
        y_mla = mla_mixer(c_q, c_kv, k_rope, mla_q_norm_g[i], mla_w_uq[i], mla_kv_norm_g[i],
                          mla_w_ukv[i], cos, sin)
        h = h + jnp.concatenate([y_conv, y_ssd, y_mla], axis=-1) @ w_out[i]
        hn = rms_norm(h, ffn_norm_g[i])
        if i % 2 == 0:
            j = i // 2
            h = h + swiglu(hn, dense_w_gate[j], dense_w_up[j], dense_w_down[j])
        else:
            j = i // 2
            h = h + moe_top2(hn, moe_router[j], moe_w_gate[j], moe_w_up[j], moe_w_down[j])
        gate = jax.nn.sigmoid(rms_norm(h, ple_norm_g[i]) @ ple_w_gate[i])
        h = h + (p[i] @ ple_w_proj[i]) * gate
    return rms_norm(h, final_norm_g)


_drawn_inputs = setup_inputs


def setup_inputs(seed=0):
    import zlib

    import numpy as np

    out = dict(_drawn_inputs(seed))
    spreads = {}
    factors = {'conv_ln_b': 4.714, 'mla_q_norm_g': 4.522, 'mla_kv_norm_g': 2.946, 'ple_norm_g': 2.964}
    for name, (base, spread) in spreads.items():
        noise = np.random.default_rng([zlib.crc32(name.encode()), seed]).standard_normal(out[name].shape)
        drawn = base * np.exp(spread * noise) if base else spread * noise
        out[name] = __import__('jax').numpy.asarray(drawn.astype(out[name].dtype))
    for name, factor in factors.items():
        out[name] = (out[name] * factor).astype(out[name].dtype)
    return out
```

```python
from contextlib import ExitStack

import numpy as np
import concourse.bass as bass
from concourse import mybir

F32 = mybir.dt.float32
I32 = mybir.dt.int32
U32 = mybir.dt.uint32
ALU = mybir.AluOpType
ACT = mybir.ActivationFunctionType
AX = mybir.AxisListType

P = 128
D = 1024
KT = D // P
SEQ = 256
NT = SEQ // P
DEPTH = 2
PLE = 256
CONVW = 256
CK = 31
SSDW = 512
SH = 8
SHD = SSDW // SH
SG = 2
SN = 128
SCONV = 4
XBC = SSDW + 2 * SG * SN
XT = XBC // P
MH = 4
NOPE = 64
ROPE = 32
HR = ROPE // 2
VD = 64
QD = NOPE + ROPE
QRANK = 256
KVRANK = 128
FF = 3584
FB = 512
NCB = FF // FB
FKT = FF // P
NE = 8
RMS_EPS = 1e-6
LN_EPS = 1e-5
C_CONV, C_Z, C_XBC = 0, 2 * CONVW, 2 * CONVW + SSDW
C_SM = C_XBC + XBC
SMW = SH + QRANK + KVRANK + ROPE
IN_COLS = C_SM + SMW
S_CQ, S_CKV, S_KR = SH, SH + QRANK, SH + QRANK + KVRANK
B_SIZE = NT * SMW + 2 * NT * SSDW + 2 * NT * MH * QD + NT * MH * VD + 2 * MH * SEQ + 3 * SEQ
SLOTS = 7
SLOT = 4096
EXPERT_CHUNKS = 3 * NCB
assert EXPERT_CHUNKS % SLOTS == 0
NEG = -1e30


def layout(parts):
    at, out = 0, {}
    for name, n in parts:
        out[name] = at
        at += n
    return out, at


CONST_PARTS = [("ident", P), ("tri", P), ("ones", P), ("group", P), ("iota", P), ("mask", 2 * P), ("inv", HR)]
LAYER_PARTS = [("g_attn", KT), ("g_ffn", KT), ("g_ple", KT), ("cw", 2 * CK), ("cb", 2), ("lng", 2), ("lnb", 2),
               ("sw", XT * SCONV), ("sb", XT), ("dtb", SH), ("alog", SH), ("dskip", SH), ("sng", SSDW // P),
               ("qg", 2), ("kvg", 1)]
CONST_AT, CONST_N = layout(CONST_PARTS)
LAYER_AT, LAYER_N = layout(LAYER_PARTS)


def trunk(nc, params, x, p, positions, w_in, w_uq, w_ukv, w_out, dense_g, dense_u, dense_d, router,
          moe_g, moe_u, moe_d, ple_g, ple_p, final_g, out):
    with ExitStack() as ctx:
        def sb(name, n, dt=F32):
            return ctx.enter_context(nc.sbuf_tensor(name, [P, n], dt))

        def sem(name):
            return ctx.enter_context(nc.semaphore(name))

        ring = sb("ring", SLOTS * SLOT)
        h_b = sb("h", NT * D)
        xs_b = sb("xs", NT * D)
        xT_b = sb("xT", NT * D)
        arena_a = sb("arena_a", FKT * SEQ)
        arena_b = sb("arena_b", B_SIZE)
        par = sb("par", CONST_N + DEPTH * LAYER_N)
        wq_b = sb("wq", 2 * MH * QD)
        wkv_b = sb("wkv", MH * (NOPE + VD))
        rt = sb("rt", KT * NE)
        pos_i = sb("pos_i", NT, I32)
        trig = sb("trig", 5 * NT * HR)
        tiny = sb("tiny", 560)
        tinyi = sb("tinyi", 2 * 8, U32)
        flag = sb("flag", 2, I32)
        psum = ctx.enter_context(nc.psum_tensor("psum", [P, 8, 512], F32))

        h = h_b[:, :].rearrange("p (t d) -> p t d", t=NT)
        xs = xs_b[:, :].rearrange("p (t d) -> p t d", t=NT)
        xT = xT_b[:, :].rearrange("p (k s) -> p k s", k=KT)

        def const(name, n=P):
            return par[:, CONST_AT[name]:CONST_AT[name] + n]

        def lp(L, name, i=0, n=1):
            a = CONST_N + L * LAYER_N + LAYER_AT[name] + i
            return par[:, a:a + n]

        ident, tri, ones, group, iota = (const(n) for n in ("ident", "tri", "ones", "group", "iota"))
        mask = const("mask", 2 * P)

        class View:

            def __init__(self, buf, at, end):
                self.buf, self.at, self.end = buf, at, end

            def __call__(self, n):
                a, self.at = self.at, self.at + n
                assert self.at <= self.end, (self.at, self.end)
                return self.buf[:, a:a + n]

        va = View(arena_a, 0, FKT * SEQ)
        cpad_f = va(2 * (CK - 1 + SEQ))
        cpad = cpad_f.rearrange("p (m s) -> p m s", m=2)
        xpad_f = va(XT * (SCONV - 1 + SEQ))
        xpad = xpad_f.rearrange("p (m s) -> p m s", m=XT)
        xbcT = va(XT * SEQ).rearrange("p (m s) -> p m s", m=XT)
        z = va(NT * SSDW).rearrange("p (t c) -> p t c", t=NT)
        cacc = va(2 * SEQ).rearrange("p (m s) -> p m s", m=2)
        csq = va(2 * SEQ).rearrange("p (m s) -> p m s", m=2)
        ctmp = va(4 * NT * HR)
        hT = arena_a[:, :].rearrange("p (k s) -> p k s", k=FKT)
        dec = xpad_f[:, 0:NT * SH * P].rearrange("p (t h l) -> p t h l", t=NT, h=SH)
        cbm = cpad_f[:, 0:NT * SG * P].rearrange("p (t g l) -> p t g l", t=NT, g=SG)
        vb = View(arena_b, 0, B_SIZE)
        sm_f = vb(NT * SMW)
        sm = sm_f.rearrange("p (t c) -> p t c", t=NT)
        xd = vb(NT * SSDW).rearrange("p (t c) -> p t c", t=NT)
        dx = vb(NT * SSDW).rearrange("p (t c) -> p t c", t=NT)
        st = sm_f[:, 0:SSDW]
        qk_f = vb(2 * NT * MH * QD)
        qf = qk_f[:, 0:NT * MH * QD].rearrange("p (t h d) -> p t h d", t=NT, h=MH)
        kf = qk_f[:, NT * MH * QD:].rearrange("p (t h d) -> p t h d", t=NT, h=MH)
        sc_f = [qk_f[:, 0:MH * P], qk_f[:, MH * P:3 * MH * P]]
        sc = [s.rearrange("p (h k) -> p h k", h=MH) for s in sc_f]
        vs = vb(NT * MH * VD).rearrange("p (t h d) -> p t h d", t=NT, h=MH)
        qT = vb(MH * SEQ).rearrange("p (h s) -> p h s", h=MH)
        kT = vb(MH * SEQ).rearrange("p (h s) -> p h s", h=MH)
        cqT = vb(2 * SEQ).rearrange("p (k s) -> p k s", k=2)
        ckvT = vb(SEQ)
        YW = SSDW + MH * VD
        ytok = xs_b[:, 0:NT * YW].rearrange("p (t c) -> p t c", t=NT)
        xdd = xs_b[:, NT * YW:NT * YW + SSDW]
        yT = xT
        btok = xT_b[:, 0:SG * SN].rearrange("p (g n) -> p g n", g=SG)
        prT_f = xT_b[:, 2 * SEQ:2 * SEQ + 3 * MH * P]
        prT = [prT_f[:, 0:MH * P].rearrange("p (h b q) -> p h b q", h=MH, b=1),
               prT_f[:, MH * P:].rearrange("p (h b q) -> p h b q", h=MH, b=2)]
        vf = View(arena_b, 0, B_SIZE)
        sg = vf(2 * FB).rearrange("p (t c) -> p t c", t=2)
        hs = vf(2 * FB).rearrange("p (t c) -> p t c", t=2)
        ysb = vf(D)
        xg = vf(KT * P).rearrange("p (k s) -> p k s", k=KT)
        sel = vf(NT * P).rearrange("p (t s) -> p t s", t=NT)
        selg = vf(NT * P).rearrange("p (t s) -> p t s", t=NT)
        selgT = vf(NT * P).rearrange("p (t s) -> p t s", t=NT)
        ptok = vf(NT * PLE).rearrange("p (t c) -> p t c", t=NT)
        pT = vf(2 * SEQ).rearrange("p (k s) -> p k s", k=2)
        gfin = vf(D)
        wq = wq_b[:, :].rearrange("p (k n) -> p k n", k=2)
        rt_v = rt[:, :].rearrange("p (k n) -> p k n", k=KT)

        cos_t, sin_t, tr0, tr1, tr2 = (trig[:, i * NT * HR:(i + 1) * NT * HR] for i in range(5))

        vt = View(tiny, 0, 560)
        ss = vt(2)
        ms = vt(2)
        rms = vt(2)
        rstd = vt(2)
        dtx, dtn, dte, dtu, dtl, dtc, dt, adt = (vt(NT * SH) for _ in range(8))
        nega = vt(SH)
        acs = vt(3 * SH)
        ea, dst = vt(SH), vt(SH)
        lss, lms, lrm, lrs = (vt(4) for _ in range(4))
        gss, gms, grm, grs = (vt(4) for _ in range(4))
        nm, den, rden = vt(8), vt(8), vt(8)
        posf = vt(NT)
        logits = vt(NT * NE)
        top = vt(NT * 8)
        topi = vt(NT * 2)
        dv, ev, g1, g2 = (vt(NT) for _ in range(4))
        o1, o2 = vt(NT * NE), vt(NT * NE)
        chosen = vt(NT * NE)
        rank = vt(NT * NE)
        STEPS = 2 * NE
        slot_of = vt(NT * (STEPS + 1)).rearrange("p (t e) -> p t e", t=NT)
        gate_of = vt(NT * (STEPS + 1)).rearrange("p (t e) -> p t e", t=NT)
        cnt = vt(NE)
        mx = vt(1)

        loaded = [sem(f"loaded{s}") for s in range(SLOTS)]
        down_used = sem("down_used")
        moe_down_used = sem("moe_down_used")
        params_in, x_in, pos_in, wsmall_in = (sem(n) for n in ("params_in", "x_in", "pos_in", "wsmall_in"))
        ptok_in, gfin_in, out_ready, out_done = (sem(n) for n in ("ptok_in", "gfin_in", "out_ready", "out_done"))
        h_ready, sumsq, ms_ready, rms_ready, xs_ready = (sem(n) for n in (
            "h_ready", "sumsq", "ms_ready", "rms_ready", "xs_ready"))
        conv_ready, csq_ready, crms_ready, chn_ready = (sem(n) for n in (
            "conv_ready", "csq_ready", "crms_ready", "chn_ready"))
        (xtap_ready, xbc_ready, pads_ready) = (sem(n) for n in ("xtap_ready", "xbc_ready", "pads_ready"))
        (dtn_ready, dte_ready, dtu_ready, dtl_ready, nega_ready, adt_ready, acsd_ready, ea_ready, triadt_ready,
         dec_ready, mix_ready, xdd_ready, ygz_ready, gss_ready, gms_ready, grm_ready, ytok_ready) = (
             sem(n) for n in ("dtn_ready", "dte_ready", "dtu_ready", "dtl_ready", "nega_ready", "adt_ready",
                              "acsd_ready", "ea_ready", "triadt_ready", "dec_ready", "mix_ready", "xdd_ready",
                              "ygz_ready", "gss_ready", "gms_ready", "grm_ready", "ytok_ready"))
        (lss_ready, lms_ready, lrm_ready, cn_ready, qk_ready, score_ready, prob_ready, yT_ready) = (
            sem(n) for n in ("lss_ready", "lms_ready", "lrm_ready", "cn_ready", "qk_ready", "score_ready",
                             "prob_ready", "yT_ready"))
        (chosen_ready, dv_ready, ev_ready, flag_ready, sel_ready, selg_ready) = (sem(n) for n in (
            "chosen_ready", "dv_ready", "ev_ready", "flag_ready", "sel_ready", "selg_ready"))
        trig_arg, trig_ready = sem("trig_arg"), sem("trig_ready")
        dve_step = sem("dve_step")

        class Banks:

            def __init__(self):
                self.full = [sem(f"full{b}") for b in range(8)]
                self.free = [sem(f"free{b}") for b in range(8)]
                self.count = [0] * 8
                self.uses = {}

            def fill(self, pe, name, b):
                if self.count[b]:
                    pe.wait_ge(self.free[b], self.count[b])
                self.count[b] += 1
                self.uses[name] = (b, self.count[b])
                return psum[:, b, :]

            def is_full(self, name):
                return self.full[self.uses[name][0]]

            def filled(self, eng, name):
                b, n = self.uses[name]
                eng.wait_ge(self.full[b], n)
                return psum[:, b, :]

            def is_free(self, name):
                return self.free[self.uses[name][0]]

            def taken(self, name):
                b, n = self.uses[name]
                return self.free[b], n

        banks = Banks()
        moe_full = [sem(f"moe_full{b}") for b in range(8)]
        moe_free = [sem(f"moe_free{b}") for b in range(8)]
        MOE_FILLS = [NCB, NCB, NCB + 1, 2, 2, 1, 1, 2]

        def cols(w, c0, n, k=KT):
            return w.rearrange("(k p) n -> p k n", p=P)[:, :, c0:c0 + n], k, n

        def layer_front(L):
            wi, wo = w_in[L], w_out[L]
            return [cols(wi, C_CONV, 512), cols(wi, C_XBC, 512), cols(wi, C_XBC + 512, 512),
                    cols(wi, C_SM, SMW), cols(wi, C_Z, 512), cols(wo, 0, 512), cols(wo, 512, 512)]

        def layer_ple(L):
            return [cols(ple_g[L], 0, 512), cols(ple_g[L], 512, 512), cols(ple_p[L], 0, D, 2)]

        def swiglu_chunk(g, u, d, k):
            if k < 2 * NCB:
                return cols(g if k % 2 == 0 else u, (k // 2) * FB, FB)
            j = k - 2 * NCB
            return d.rearrange("(k p) n -> p k n", p=P)[:, 4 * j:4 * j + 4, :], 4, D

        before_moe = layer_front(0) + [swiglu_chunk(dense_g[0], dense_u[0], dense_d[0], k)
                                       for k in range(EXPERT_CHUNKS)] + layer_ple(0) + layer_front(1)
        after_moe = layer_ple(1)
        N0 = len(before_moe)
        last_reader = []

        def slot_view(s, k, n):
            return ring[:, s * SLOT:s * SLOT + k * n].rearrange("p (k n) -> p k n", k=k)

        def loads_before(g, s=None):
            return g // SLOTS + 1

        block = ctx.enter_context(nc.Block())

        @block.tensor
        def _(pe):
            mm, tr = nc.tensor.matmul, nc.tensor.transpose
            chunk_no = [0]

            def chunk(k, n):
                g = chunk_no[0]
                chunk_no[0] += 1
                pe.wait_ge(loaded[g % SLOTS], 16 * loads_before(g))
                return slot_view(g % SLOTS, k, n)

            def chunk_read(name):
                b, n = banks.uses[name]
                last_reader.append((banks.full[b], n))

            def transpose_x(key):
                for b in range(4):
                    o = banks.fill(pe, (key, b), b)
                    for q in range(2):
                        for t in range(NT):
                            kt = 2 * b + q
                            last = tr(o[:, q * SEQ + t * P:q * SEQ + t * P + P], xs[:, t, kt * P:kt * P + P], ident)
                    last.then_inc(banks.is_full((key, b)), 1)

            def wait_xT(key):
                for b in range(4):
                    pe.wait_ge(*banks.taken((key, b)))

            def tokens_by_cols(key, lhs, k, w, n, c0, b, t):
                o = banks.fill(pe, key, b)
                for kt in range(k):
                    last = mm(o[:, 0:n], lhs[:, kt, t * P:t * P + P], w[:, kt, c0:c0 + n],
                              start=kt == 0, stop=kt == k - 1)
                last.then_inc(banks.is_full(key), 1)

            def mixers(L):
                w = chunk(KT, 512)
                for m in range(4):
                    key = ("conv", L, m // 2)
                    if m % 2 == 0:
                        o = banks.fill(pe, key, 4 + m // 2)
                    for kt in range(KT):
                        last = mm(o[:, (m % 2) * SEQ:(m % 2) * SEQ + SEQ], w[:, kt, m * P:m * P + P], xT[:, kt, :],
                                  start=kt == 0, stop=kt == KT - 1)
                    if m % 2:
                        last.then_inc(banks.is_full(key), 1)
                chunk_read(key)
                for c in range(2):
                    w = chunk(KT, 512)
                    for m in range(4):
                        key = ("xbc", L, 2 * c + m // 2)
                        if m % 2 == 0:
                            o = banks.fill(pe, key, [6, 7, 0, 1][2 * c + m // 2])
                        for kt in range(KT):
                            last = mm(o[:, (m % 2) * SEQ:(m % 2) * SEQ + SEQ], w[:, kt, m * P:m * P + P],
                                      xT[:, kt, :], start=kt == 0, stop=kt == KT - 1)
                        if m % 2:
                            last.then_inc(banks.is_full(key), 1)
                    chunk_read(key)
                w = chunk(KT, SMW)
                for t in range(NT):
                    tokens_by_cols(("sm", L, t), xT, KT, w, SMW, 0, 2 + t, t)
                chunk_read(key := ("sm", L, 1))
                w = chunk(KT, 512)
                for t in range(NT):
                    tokens_by_cols(("z", L, t), xT, KT, w, 512, 0, 6 + t, t)
                chunk_read(("z", L, 1))
                pe.wait_ge(cn_ready, L + 1)
                o = banks.fill(pe, ("cqT", L), 4)
                for k in range(2):
                    for t in range(NT):
                        last = tr(o[:, k * SEQ + t * P:k * SEQ + t * P + P],
                                  sm[:, t, S_CQ + k * P:S_CQ + k * P + P], ident)
                last.then_inc(banks.is_full(("cqT", L)), 1)
                o = banks.fill(pe, ("ckvT", L), 5)
                for t in range(NT):
                    last = tr(o[:, t * P:t * P + P], sm[:, t, S_CKV:S_CKV + KVRANK], ident)
                last.then_inc(banks.is_full(("ckvT", L)), 1)
                pe.wait_ge(*banks.taken(("cqT", L)))
                pe.wait_ge(*banks.taken(("ckvT", L)))
                pe.wait_ge(wsmall_in, 16 * (2 * L + 3))
                for t in range(NT):
                    tokens_by_cols(("q", L, t), cqT, 2, wq, MH * QD, 0, 0 + t, t)
                for t in range(NT):
                    o = banks.fill(pe, ("kv", L, t), 2 + t)
                    mm(o, ckvT[:, t * P:t * P + P], wkv_b[:, :], start=True, stop=True).then_inc(
                        banks.is_full(("kv", L, t)), 1)
                pe.wait_ge(xbc_ready, XT * (L + 1))
                for t in range(NT):
                    o = banks.fill(pe, ("xtok", L, t), 4 + t)
                    for m in range(4):
                        last = tr(o[:, m * P:m * P + P], xbcT[:, m, t * P:t * P + P], ident)
                    last.then_inc(banks.is_full(("xtok", L, t)), 1)
                o = banks.fill(pe, ("btok", L), 6)
                for g in range(SG):
                    last = tr(o[:, g * P:g * P + P], xbcT[:, 4 + g, 0:P], ident)
                last.then_inc(banks.is_full(("btok", L)), 1)
                o = banks.fill(pe, ("cb", L), 7)
                for t in range(NT):
                    for g in range(SG):
                        c0 = (t * SG + g) * P
                        last = mm(o[:, c0:c0 + P], xbcT[:, 4 + g, t * P:t * P + P], xbcT[:, 6 + g, t * P:t * P + P],
                                  start=True, stop=True)
                last.then_inc(banks.is_full(("cb", L)), 1)
                pe.wait_ge(qk_ready, L + 1)
                for t in range(NT):
                    pe.wait_ge(*banks.taken(("kv", L, t)))
                for n, (buf, name) in enumerate(((qf, "qT"), (kf, "kT"))):
                    for t in range(NT):
                        o = banks.fill(pe, (name, L, t), 2 * n + t)
                        for hd in range(MH):
                            last = tr(o[0:QD, hd * P:hd * P + P], buf[:, t, hd, :], ident)
                        last.then_inc(banks.is_full((name, L, t)), 1)
                pe.wait_ge(adt_ready, L + 1)
                o = banks.fill(pe, ("acs", L), 6)
                for t in range(NT):
                    mm(o[:, t * SH:t * SH + SH], tri, adt[:, t * SH:t * SH + SH], start=True, stop=True)
                mm(o[:, 2 * SH:3 * SH], ones, adt[:, 0:SH], start=True, stop=True).then_inc(
                    banks.is_full(("acs", L)), 1)
                for t in range(NT):
                    for g in range(SG):
                        pe.wait_ge(triadt_ready, 4 * L + 2 * t + g + 1)
                        key = ("seg", L, t, g)
                        o = banks.fill(pe, key, [4, 5, 7, 6][2 * t + g])
                        mm(o, ones, dec[:, t, 4 * g:4 * g + 4, :].rearrange("p h l -> p (h l)"),
                           start=True, stop=True).then_inc(banks.is_full(key), 1)
                for name in ("qT", "kT"):
                    for t in range(NT):
                        pe.wait_ge(*banks.taken((name, L, t)))
                o = banks.fill(pe, ("sc", L, 0), 0)
                for hd in range(MH):
                    last = mm(o[:, hd * P:hd * P + P], qT[0:QD, hd, 0:P], kT[0:QD, hd, 0:P], start=True, stop=True)
                last.then_inc(banks.is_full(("sc", L, 0)), 1)
                for j in range(2):
                    key = ("sc", L, 1 + j)
                    o = banks.fill(pe, key, 1 + j)
                    for i in range(2):
                        hd = 2 * j + i
                        last = mm(o[:, i * SEQ:i * SEQ + SEQ], qT[0:QD, hd, P:SEQ], kT[0:QD, hd, :],
                                  start=True, stop=True)
                    last.then_inc(banks.is_full(key), 1)
                pe.wait_ge(conv_ready, L + 1)
                o = banks.fill(pe, ("mean", L), 3)
                mm(o, group, cacc.rearrange("p m s -> p (m s)"), start=True, stop=True).then_inc(
                    banks.is_full(("mean", L)), 1)
                pe.wait_ge(*banks.taken(("btok", L)))
                pe.wait_ge(xdd_ready, L + 1)
                o = banks.fill(pe, ("st", L), 4)
                for g in range(SG):
                    last = mm(o[:, g * SEQ:g * SEQ + SEQ], btok[:, g, :], xdd[:, g * SEQ:g * SEQ + SEQ],
                              start=True, stop=True)
                last.then_inc(banks.is_full(("st", L)), 1)
                pe.wait_ge(csq_ready, L + 1)
                o = banks.fill(pe, ("var", L), 3)
                mm(o, group, csq.rearrange("p m s -> p (m s)"), start=True, stop=True).then_inc(
                    banks.is_full(("var", L)), 1)
                for t in range(NT):
                    pe.wait_ge(*banks.taken(("xtok", L, t)))
                    key = ("yd", L, t)
                    o = banks.fill(pe, key, 5 + t)
                    for hd in range(SH):
                        if hd % 4 == 0:
                            pe.wait_ge(mix_ready, 4 * L + 2 * t + hd // 4 + 1)
                        last = mm(o[:, hd * SHD:hd * SHD + SHD], dec[:, t, hd, :], xd[:, t, hd * SHD:hd * SHD + SHD],
                                  start=True, stop=True)
                    last.then_inc(banks.is_full(key), 1)
                pe.wait_ge(*banks.taken(("st", L)))
                o = banks.fill(pe, ("yo", L), 7)
                for g in range(SG):
                    last = mm(o[:, g * SEQ:g * SEQ + SEQ], xbcT[:, 6 + g, P:SEQ], st[:, g * SEQ:g * SEQ + SEQ],
                              start=True, stop=True)
                last.then_inc(banks.is_full(("yo", L)), 1)
                pe.wait_ge(prob_ready, 8 * L + 4)
                o = banks.fill(pe, ("prT", L, 0), 0)
                for hd in range(MH):
                    last = tr(o[:, hd * P:hd * P + P], sc[0][:, hd, :], ident)
                last.then_inc(banks.is_full(("prT", L, 0)), 1)
                pe.wait_ge(prob_ready, 8 * L + 8)
                for j in range(2):
                    key = ("prT", L, 1 + j)
                    o = banks.fill(pe, key, 1 + j)
                    for i in range(2):
                        for b in range(2):
                            last = tr(o[:, (2 * i + b) * P:(2 * i + b) * P + P], sc[1][:, 2 * j + i, b * P:b * P + P],
                                      ident)
                    last.then_inc(banks.is_full(key), 1)
                for j in range(3):
                    pe.wait_ge(*banks.taken(("prT", L, j)))
                o = banks.fill(pe, ("pv", L), 4)
                for t in range(NT):
                    for hd in range(MH):
                        c0 = (t * MH + hd) * VD
                        for b in range(t + 1):
                            last = mm(o[:, c0:c0 + VD], prT[t][:, hd, b, :], vs[:, b, hd, :], start=b == 0, stop=b == t)
                last.then_inc(banks.is_full(("pv", L)), 1)
                pe.wait_ge(*banks.taken(("pv", L)))
                pe.wait_ge(ytok_ready, L + 1)
                for j in range(3):
                    key = ("yT", L, j)
                    o = banks.fill(pe, key, [0, 1, 2][j])
                    for q in range(2):
                        m = 2 * j + q
                        for t in range(NT):
                            last = tr(o[:, q * SEQ + t * P:q * SEQ + t * P + P], ytok[:, t, m * P:m * P + P], ident)
                    last.then_inc(banks.is_full(key), 1)
                pe.wait_ge(yT_ready, L + 1)
                for j in range(3):
                    pe.wait_ge(*banks.taken(("yT", L, j)))
                for half in range(2):
                    w = chunk(KT, 512)
                    for t in range(NT):
                        tokens_by_cols(("o", L, half, t), yT, KT, w, 512, 0, 4 + 2 * half + t, t)
                    chunk_read(("o", L, half, 1))

            def hidden_T(key, b, t, cb):
                o = banks.fill(pe, key, b)
                for q in range(4):
                    last = tr(o[:, q * P:q * P + P], hs[:, t, q * P:q * P + P], ident)
                last.then_inc(banks.is_full(key), 1)

            def dense():
                for cb in range(NCB):
                    wg = chunk(KT, FB)
                    for t in range(NT):
                        tokens_by_cols(("g", cb, t), xT, KT, wg, FB, 0, t, t)
                    chunk_read(("g", cb, 1))
                    if cb:
                        for t in range(NT):
                            pe.wait_ge(*banks.taken(("u", cb - 1, t)))
                            hidden_T(("hT", cb - 1, t), 4 + t, t, cb - 1)
                    wu = chunk(KT, FB)
                    for t in range(NT):
                        tokens_by_cols(("u", cb, t), xT, KT, wu, FB, 0, 2 + t, t)
                    chunk_read(("u", cb, 1))
                keys = [(t, half) for t in range(NT) for half in range(2)]
                acc = {key: banks.fill(pe, ("d", *key), b) for key, b in zip(keys, (6, 7, 0, 1))}
                for j in range(NCB):
                    w = chunk(4, D)
                    if j == 1:
                        for t in range(NT):
                            pe.wait_ge(*banks.taken(("u", NCB - 1, t)))
                            hidden_T(("hT", NCB - 1, t), 4 + t, t, NCB - 1)
                    for t in range(NT):
                        pe.wait_ge(*banks.taken(("hT", j, t)))
                    for key in keys:
                        t, half = key
                        for q in range(4):
                            kt = 4 * j + q
                            last = mm(acc[key], hT[:, kt, t * P:t * P + P], w[:, q, half * 512:half * 512 + 512],
                                      start=kt == 0, stop=kt == FKT - 1)
                        if j == NCB - 1:
                            last.then_inc(banks.is_full(("d", *key)), 1)
                    if j < NCB - 1:
                        last.then_inc(down_used, 1)
                        last_reader.append((down_used, j + 1))
                    else:
                        chunk_read(("d", 1, 1))

            def ple(L, wait_chunk):
                pe.wait_ge(ptok_in, 16 * (L + 1))
                o = banks.fill(pe, ("pT", L), 7)
                for k in range(2):
                    for t in range(NT):
                        last = tr(o[:, k * SEQ + t * P:k * SEQ + t * P + P], ptok[:, t, k * P:k * P + P], ident)
                last.then_inc(banks.is_full(("pT", L)), 1)
                pe.wait_ge(xs_ready, 2 * (3 * L + 3))
                transpose_x(("n", 3 * L + 2))
                wait_xT(("n", 3 * L + 2))
                for half in range(2):
                    w = wait_chunk(KT, 512)
                    for t in range(NT):
                        tokens_by_cols(("pg", L, half, t), xT, KT, w, 512, 0, 4 + t if half == 0 else 0 + t, t)
                    chunk_read(("pg", L, half, 1))
                pe.wait_ge(*banks.taken(("pT", L)))
                w = wait_chunk(2, D)
                for half in range(2):
                    for t in range(NT):
                        tokens_by_cols(("pp", L, half, t), pT, 2, w, 512, half * 512,
                                       [6, 7, 2, 3][2 * half + t], t)
                chunk_read(("pp", L, 1, 1))

            pe.wait_ge(params_in, 16)
            for L in range(DEPTH):
                pe.wait_ge(xs_ready, 2 * (3 * L + 1))
                transpose_x(("n", 3 * L))
                wait_xT(("n", 3 * L))
                mixers(L)
                pe.wait_ge(xs_ready, 2 * (3 * L + 2))
                transpose_x(("n", 3 * L + 1))
                wait_xT(("n", 3 * L + 1))
                if L == 0:
                    dense()
                    ple(0, chunk)

            for t in range(NT):
                o = banks.fill(pe, ("lg", t), 4 + t)
                for kt in range(KT):
                    last = mm(o[:, 0:NE], xT[:, kt, t * P:t * P + P], rt_v[:, kt, :], start=kt == 0, stop=kt == KT - 1)
                last.then_inc(banks.is_full(("lg", t)), 1)
            pe.wait_ge(chosen_ready, 1)
            o = banks.fill(pe, ("rank",), 6)
            mm(o[:, 0:NE], tri, chosen[:, 0:NE], start=True, stop=True)
            mm(o[:, NE:2 * NE], tri, chosen[:, NE:2 * NE], start=True, stop=False)
            mm(o[:, NE:2 * NE], ones, chosen[:, 0:NE], start=False, stop=True)
            mm(o[:, 2 * NE:3 * NE], ones, chosen[:, 0:NE], start=True, stop=False)
            mm(o[:, 2 * NE:3 * NE], ones, chosen[:, NE:2 * NE], start=False, stop=True).then_inc(
                banks.is_full(("rank",)), 1)

            for b in range(8):
                pe.wait_ge(banks.free[b], banks.count[b])
            pe.wait_ge(flag_ready, 1)
            n_steps = pe.value_load(flag[0:1, 0:1], min_val=NE, max_val=2 * NE)

            def gather(step):
                pe.wait_ge(sel_ready, step + 1)
                for half in range(2):
                    pe.wait_ge(moe_free[5 + half], step + 1)
                    o = psum[:, 5 + half, :]
                    for q in range(4):
                        kt = 4 * half + q
                        for t in range(NT):
                            last = mm(o[:, q * P:q * P + P], xs[:, t, kt * P:kt * P + P], sel[:, t, :],
                                      start=t == 0, stop=t == NT - 1)
                    last.then_inc(moe_full[5 + half], 1)

            for b in range(8):
                pe.sem_inc(moe_free[b], 1)
            gather(0)
            with pe.Fori(0, n_steps) as e:
                def moe_chunk(c, k, n):
                    g = N0 + c
                    pe.wait_ge(loaded[g % SLOTS], e * (16 * EXPERT_CHUNKS // SLOTS) + 16 * loads_before(g))
                    return slot_view(g % SLOTS, k, n)

                def hidden(cb):
                    pe.wait_ge(moe_free[1], e * NCB + cb + 2)
                    pe.wait_ge(moe_free[2], e * (NCB + 1) + cb + 2)
                    for q in range(4):
                        last = tr(psum[:, 2, q * P:q * P + P], hs[:, cb % 2, q * P:q * P + P], ident)
                    last.then_inc(moe_full[2], 1)

                pe.wait_ge(moe_free[5], e + 2)
                pe.wait_ge(moe_free[6], e + 2)
                for cb in range(NCB):
                    for u in range(2):
                        w = moe_chunk(2 * cb + u, KT, FB)
                        pe.wait_ge(moe_free[u], e * NCB + cb + 1)
                        for kt in range(KT):
                            last = mm(psum[:, u, :], xg[:, kt, :], w[:, kt, :], start=kt == 0, stop=kt == KT - 1)
                        last.then_inc(moe_full[u], 1)
                        if u == 0 and cb == 0:
                            pe.wait_ge(selg_ready, e + 1)
                            pe.wait_ge(moe_free[2], e * (NCB + 1) + 1)
                            for t in range(NT):
                                last = tr(psum[:, 2, t * P:t * P + P], selg[:, t, :], ident)
                            last.then_inc(moe_full[2], 1)
                        elif u == 0:
                            hidden(cb - 1)
                for half in range(2):
                    pe.wait_ge(moe_free[3 + half], e * 2 + 1)
                for j in range(NCB):
                    w = moe_chunk(2 * NCB + j, 4, D)
                    if j == 1:
                        hidden(NCB - 1)
                    pe.wait_ge(moe_free[2], e * (NCB + 1) + j + 3)
                    for half in range(2):
                        for q in range(4):
                            kt = 4 * j + q
                            last = mm(psum[:, 3 + half, :], hT[:, kt, 0:P], w[:, q, half * 512:half * 512 + 512],
                                      start=kt == 0, stop=kt == FKT - 1)
                        if j == NCB - 1:
                            last.then_inc(moe_full[3 + half], 1)
                    if j < NCB - 1:
                        last.then_inc(moe_down_used, 1)
                gather(e + 1)
                pe.wait_ge(moe_free[3], e * 2 + 2)
                pe.wait_ge(moe_free[4], e * 2 + 2)
                for i, (b, n) in enumerate(((7, 0), (3, 1), (4, 1), (7, 1))):
                    t, half = divmod(i, 2)
                    pe.wait_ge(moe_free[b], e * 2 + n + 1)
                    mm(psum[:, b, :], selgT[:, t, :], ysb[:, half * 512:half * 512 + 512],
                       start=True, stop=True).then_inc(moe_full[b], 1)
            for b in range(8):
                extra = 2 if b in (5, 6) else 1
                pe.wait_ge(moe_free[b], n_steps * MOE_FILLS[b] + extra)

            def chunk_after(k, n):
                g = N0 + chunk_after_no[0]
                chunk_after_no[0] += 1
                pe.wait_ge(loaded[g % SLOTS], n_steps * (16 * EXPERT_CHUNKS // SLOTS) + 16 * loads_before(g))
                return slot_view(g % SLOTS, k, n)
            chunk_after_no = [0]
            ple(1, chunk_after)

        @block.sync
        def _(sp):
            def load(g, src, k, n):
                sp.dma_start(slot_view(g % SLOTS, k, n), src).then_inc(loaded[g % SLOTS], 16)

            sp.dma_start(h, x[0].rearrange("(t p) d -> p t d", p=P)).then_inc(x_in, 16)
            for g, (src, k, n) in enumerate(before_moe):
                if g >= SLOTS:
                    sp.wait_ge(*last_reader[g - SLOTS])
                load(g, src, k, n)

            def expert(e, weights, prior):
                for c in range(EXPERT_CHUNKS):
                    if c < SLOTS:
                        prior(c)
                    else:
                        r = c - SLOTS
                        sp.wait_ge(moe_full[r % 2], e * NCB + r // 2 + 1)
                    load(N0 + c, *swiglu_chunk(*weights, c))

            expert(0, (moe_g[0, 0], moe_u[0, 0], moe_d[0, 0]), lambda c: sp.wait_ge(*last_reader[N0 + c - SLOTS]))
            sp.wait_ge(flag_ready, 1)
            n_steps = sp.value_load(flag[0:1, 0:1], min_val=NE, max_val=2 * NE)

            def prior_in_loop(e):
                def wait(c):
                    if c < SLOTS - 1:
                        sp.wait_ge(moe_down_used, e * (NCB - 1) + c + 1 - (NCB - 1))
                    else:
                        sp.wait_ge(moe_full[4], e * 2 - 1)
                return wait

            last_step = sp.value_load(flag[0:1, 1:2], min_val=NE - 1, max_val=2 * NE - 1)
            with sp.Fori(1, n_steps) as e:
                ex = sp.snap(e % NE)

                def pick(w):
                    return w[0, bass.ds(ex, 1)].rearrange("a k n -> (a k) n")
                expert(e, (pick(moe_g), pick(moe_u), pick(moe_d)), prior_in_loop(e))
            for c, (src, k, n) in enumerate(after_moe):
                sp.wait_ge(moe_down_used, last_step * (NCB - 1) + c + 1)
                load(N0 + c, src, k, n)
            for t in range(NT):
                sp.wait_ge(out_ready, t + 1)
                sp.dma_start(out[0, t * P:t * P + P, :], xs[:, t, :]).then_inc(out_done, 16)
            sp.wait_ge(out_done, 16 * NT)

        @block.gpsimd
        def _(pool):
            pool.dma_start(par[:, :], params).then_inc(params_in, 16)
            pool.dma_start(pos_i[:, :], positions).then_inc(pos_in, 16)
            for L in range(DEPTH):
                if L:
                    banks.filled(pool, ("kv", L - 1, 1))
                pool.dma_start(wq, w_uq[L].rearrange("(k p) n -> p k n", p=P)).then_inc(wsmall_in, 16)
                pool.dma_start(wkv_b[:, :], w_ukv[L]).then_inc(wsmall_in, 16)
                if L == 0:
                    pool.dma_start(rt_v, router[0].rearrange("(k p) n -> p k n", p=P)).then_inc(wsmall_in, 16)
                pool.wait_ge(*banks.taken(("o", L, 1, 1)))
                pool.dma_start(ptok, p[L, 0].rearrange("(t p) c -> p t c", p=P)).then_inc(ptok_in, 16)
            pool.dma_start(gfin, final_g.rearrange("(a n) -> a n", a=1).to_broadcast([P, D])).then_inc(gfin_in, 16)

        def dense_hT(act, A, cb):
            for t in range(NT):
                o = banks.filled(act, ("hT", cb, t))
                A(hT[:, 4 * cb:4 * cb + 4, t * P:t * P + P], o.rearrange("p (k s) -> p k s", k=4),
                  ACT.Copy).then_inc(banks.is_free(("hT", cb, t)), 1)

        @block.scalar
        def _(act):
            A = nc.scalar.activation
            def norm(k, h_done):
                act.wait_ge(*h_done)
                for t in range(NT):
                    A(xs[:, t, :], h[:, t, :], ACT.Square, accum_out=ss[:, t:t + 1]).then_inc(sumsq, 1)
                act.wait_ge(ms_ready, k + 1)
                A(rms, ms, ACT.Sqrt).then_inc(rms_ready, 1)

            def take_xT(k, L, gain):
                for b in (1, 3):
                    o = banks.filled(act, (("n", k), b))
                    for q in range(2):
                        kt = 2 * b + q
                        last = A(xT[:, kt, :], o[:, q * SEQ:q * SEQ + SEQ], ACT.Copy, scale=lp(L, gain, kt))
                    last.then_inc(banks.is_free((("n", k), b)), 1)

            def mixers(L):
                o = banks.filled(act, ("conv", L, 1))
                A(csq.rearrange("p m s -> p (m s)"), o, ACT.Sigmoid).then_inc(banks.is_free(("conv", L, 1)), 1)
                act.wait_ge(pads_ready, L + 1)
                for j in range(4):
                    o = banks.filled(act, ("xbc", L, j))
                    A(xpad[:, 2 * j:2 * j + 2, SCONV - 1:], o.rearrange("p (m s) -> p m s", m=2), ACT.Copy).then_inc(
                        banks.is_free(("xbc", L, j)), 1)
                for t in range(NT):
                    o = banks.filled(act, ("sm", L, t))
                    A(sm[:, t, :], o[:, 0:SMW], ACT.Copy).then_inc(banks.is_free(("sm", L, t)), 1)
                    act.wait_ge(*banks.taken(("sm", L, t)))
                    A(sq_junk(QRANK), sm[:, t, S_CQ:S_CQ + QRANK], ACT.Square, accum_out=lss[:, t:t + 1]).then_inc(lss_ready, 1)
                    act.wait_ge(lss_ready, 4 * L + 2 * t + 1)
                    A(sq_junk(KVRANK), sm[:, t, S_CKV:S_CKV + KVRANK], ACT.Square,
                      accum_out=lss[:, 2 + t:3 + t]).then_inc(lss_ready, 1)
                    act.wait_ge(lss_ready, 4 * L + 2 * t + 2)
                act.wait_ge(lms_ready, L + 1)
                A(lrm, lms, ACT.Sqrt).then_inc(lrm_ready, 1)
                act.wait_ge(dtn_ready, L + 1)
                A(dte, dtn, ACT.Exp).then_inc(dte_ready, 1)
                A(nega, lp(L, "alog", 0, SH), ACT.Exp).then_inc(nega_ready, 1)
                act.wait_ge(dtu_ready, L + 1)
                A(dtl, dtu, ACT.Ln).then_inc(dtl_ready, 1)
                for m in range(XT):
                    act.wait_ge(xtap_ready, XT * L + m + 1)
                    A(xbcT[:, m, :], xbcT[:, m, :], ACT.Silu, bias=lp(L, "sb", m)).then_inc(xbc_ready, 1)
                for t in range(NT):
                    o = banks.filled(act, ("z", L, t))
                    A(z[:, t, :], o, ACT.Silu).then_inc(banks.is_free(("z", L, t)), 1)
                o = banks.filled(act, ("cqT", L))
                for k in range(2):
                    last = A(cqT[:, k, :], o[:, k * SEQ:k * SEQ + SEQ], ACT.Copy, scale=lp(L, "qg", k))
                last.then_inc(banks.is_free(("cqT", L)), 1)
                o = banks.filled(act, ("ckvT", L))
                A(ckvT, o[:, 0:SEQ], ACT.Copy, scale=lp(L, "kvg")).then_inc(banks.is_free(("ckvT", L)), 1)
                for t in range(NT):
                    o = banks.filled(act, ("q", L, t))
                    A(qf[:, t, :, :], o[:, 0:MH * QD].rearrange("p (h d) -> p h d", h=MH), ACT.Copy).then_inc(
                        banks.is_free(("q", L, t)), 1)
                for t in range(NT):
                    o = banks.filled(act, ("kv", L, t)).rearrange("p (h d) -> p h d", h=MH)
                    A(kf[:, t, :, 0:NOPE], o[:, :, 0:NOPE], ACT.Copy)
                    A(vs[:, t, :, :], o[:, :, NOPE:], ACT.Copy).then_inc(banks.is_free(("kv", L, t)), 1)
                o = banks.filled(act, ("btok", L))
                A(btok.rearrange("p g n -> p (g n)"), o[:, 0:SG * SN], ACT.Copy).then_inc(
                    banks.is_free(("btok", L)), 1)
                for name, buf in (("qT", qT), ("kT", kT)):
                    for t in range(NT):
                        o = banks.filled(act, (name, L, t))
                        A(buf[0:QD, :, t * P:t * P + P], o[0:QD, :].rearrange("p (h s) -> p h s", h=MH),
                          ACT.Copy).then_inc(banks.is_free((name, L, t)), 1)
                act.wait_ge(acsd_ready, L + 1)
                A(dst, dst, ACT.Exp)
                A(ea, acs[:, SH:2 * SH], ACT.Exp).then_inc(ea_ready, 1)
                for t in range(NT):
                    for g in range(SG):
                        act.wait_ge(*banks.taken(("seg", L, t, g)))
                        v = dec[:, t, 4 * g:4 * g + 4, :].rearrange("p h l -> p (h l)")
                        A(v, v, ACT.Exp).then_inc(dec_ready, 1)
                for t in range(NT):
                    act.wait_ge(score_ready, 2 * L + t + 1)
                    for hd in range(MH):
                        i = t * MH + hd
                        A(sc[t][:, hd, :], sc[t][:, hd, :], ACT.Exp, bias=nm[:, i:i + 1],
                          accum_out=den[:, i:i + 1]).then_inc(prob_ready, 1)
                act.wait_ge(*banks.taken(("mean", L)))
                A(csq.rearrange("p m s -> p (m s)"), cacc.rearrange("p m s -> p (m s)"), ACT.Square).then_inc(
                    csq_ready, 1)
                o = banks.filled(act, ("st", L))
                A(st, o, ACT.Copy).then_inc(banks.is_free(("st", L)), 1)
                act.wait_ge(*banks.taken(("var", L)))
                c2 = csq.rearrange("p m s -> p (m s)")
                A(c2, c2, ACT.Sqrt).then_inc(crms_ready, 1)
                for j in range(3):
                    o = banks.filled(act, ("prT", L, j))
                    A(prT_f[:, j * 512:(j + 1) * 512], o, ACT.Copy).then_inc(banks.is_free(("prT", L, j)), 1)
                act.wait_ge(chn_ready, L + 1)
                for m in range(2):
                    last = A(yT[:, m, :], cacc[:, m, :], ACT.Silu, scale=lp(L, "lng", m), bias=lp(L, "lnb", m))
                last.then_inc(yT_ready, 1)
                act.wait_ge(ygz_ready, L + 1)
                for t in range(NT):
                    for g in range(SG):
                        A(dx[:, t, g * SEQ:g * SEQ + SEQ], ytok[:, t, g * SEQ:g * SEQ + SEQ], ACT.Square,
                          accum_out=gss[:, 2 * t + g:2 * t + g + 1]).then_inc(gss_ready, 1)
                act.wait_ge(gms_ready, L + 1)
                A(grm, gms, ACT.Sqrt).then_inc(grm_ready, 1)

            def sq_junk(n):
                return xd.rearrange("p t c -> p (t c)")[:, 0:n]

            act.wait_ge(trig_arg, 1)
            A(sin_t, tr0, ACT.Sin)
            A(cos_t, tr1, ACT.Sin).then_inc(trig_ready, 1)
            for L in range(DEPTH):
                norm(3 * L, (h_ready, L) if L else (x_in, 16))
                take_xT(3 * L, L, "g_attn")
                mixers(L)
                norm(3 * L + 1, banks.taken(("o", L, 1, 1)))
                take_xT(3 * L + 1, L, "g_ffn")
                if L == 0:
                    h_done = banks.taken(("d", 1, 1))
                    for cb in range(NCB):
                        for t in range(NT):
                            o = banks.filled(act, ("g", cb, t))
                            if cb:
                                act.wait_ge(*banks.taken(("u", cb - 1, t)))
                            A(sg[:, t, :], o, ACT.Silu).then_inc(banks.is_free(("g", cb, t)), 1)
                        if cb:
                            dense_hT(act, A, cb - 1)
                    dense_hT(act, A, NCB - 1)
                else:
                    act.wait_ge(dv_ready, 1)
                    A(ev, dv, ACT.Exp).then_inc(ev_ready, 1)
                    act.wait_ge(flag_ready, 1)
                    n_steps = act.value_load(flag[0:1, 0:1], min_val=NE, max_val=2 * NE)

                    def take_xg(stepno):
                        act.wait_ge(moe_full[6], stepno + 1)
                        for q in range(4):
                            last = A(xg[:, 4 + q, :], psum[:, 6, q * P:q * P + P], ACT.Copy,
                                     scale=lp(1, "g_ffn", 4 + q))
                        last.then_inc(moe_free[6], 1)

                    take_xg(0)
                    with act.Fori(0, n_steps) as e:
                        for cb in range(NCB + 1):
                            if cb < NCB:
                                act.wait_ge(moe_full[0], e * NCB + cb + 1)
                                if cb >= 2:
                                    act.wait_ge(moe_free[1], e * NCB + cb)
                                A(sg[:, cb % 2, :], psum[:, 0, :], ACT.Silu).then_inc(moe_free[0], 1)
                            act.wait_ge(moe_full[2], e * (NCB + 1) + cb + 1)
                            if cb == 0:
                                A(selgT.rearrange("p t s -> p (t s)"), psum[:, 2, 0:NT * P], ACT.Copy).then_inc(
                                    moe_free[2], 1)
                            else:
                                A(hT[:, 4 * cb - 4:4 * cb, 0:P], psum[:, 2, :].rearrange("p (k s) -> p k s", k=4),
                                  ACT.Copy).then_inc(moe_free[2], 1)
                        take_xg(e + 1)
                    h_done = (moe_free[7], n_steps * MOE_FILLS[7] + 1)
                o = banks.filled(act, ("pT", L))
                A(pT.rearrange("p k s -> p (k s)"), o, ACT.Copy).then_inc(banks.is_free(("pT", L)), 1)
                norm(3 * L + 2, h_done)
                take_xT(3 * L + 2, L, "g_ple")
                for half in range(2):
                    for t in range(NT):
                        o = banks.filled(act, ("pg", L, half, t))
                        buf = sg if half == 0 else hs
                        A(buf[:, t, :], o, ACT.Sigmoid).then_inc(banks.is_free(("pg", L, half, t)), 1)
            norm(3 * DEPTH, (h_ready, DEPTH))

        @block.vector
        def _(dve):
            V = nc.vector
            steps = [0]

            def step(ins):
                steps[0] += 1
                ins.then_inc(dve_step, 1)
                dve.wait_ge(dve_step, steps[0])

            def norm(k):
                dve.wait_ge(sumsq, NT * (k + 1))
                V.tensor_scalar(ms, ss, 1.0 / D, RMS_EPS, ALU.mult, ALU.add).then_inc(ms_ready, 1)
                dve.wait_ge(rms_ready, k + 1)
                step(V.reciprocal(rstd, rms))
                for t in range(NT):
                    V.tensor_scalar(xs[:, t, :], h[:, t, :], rstd[:, t:t + 1], None, ALU.mult).then_inc(xs_ready, 1)

            def take_xT(k, L, gain):
                for b in (0, 2):
                    o = banks.filled(dve, (("n", k), b))
                    for q in range(2):
                        kt = 2 * b + q
                        last = V.tensor_scalar(xT[:, kt, :], o[:, q * SEQ:q * SEQ + SEQ], lp(L, gain, kt), None,
                                               ALU.mult)
                    last.then_inc(banks.is_free((("n", k), b)), 1)

            def bc(v, n):
                return v.unsqueeze(len(v.shape)).to_broadcast(list(v.shape) + [n])

            def heads(v, n=SH):
                return v.rearrange("p (h d) -> p h d", h=n)

            def rotate(x1, x2, c, s, t1, t2, t3, t4):
                V.tensor_tensor(t1, x1, c, ALU.mult)
                V.tensor_tensor(t2, x2, s, ALU.mult)
                V.tensor_tensor(t3, x1, s, ALU.mult)
                step(V.tensor_tensor(t4, x2, c, ALU.mult))
                V.tensor_tensor(x1, t1, t2, ALU.subtract)
                return V.tensor_tensor(x2, t3, t4, ALU.add)

            def mixers(L):
                V.memset(cpad[:, :, 0:CK - 1], 0.0)
                V.memset(xpad[:, :, 0:SCONV - 1], 0.0).then_inc(pads_ready, 1)
                dve.wait_ge(pads_ready, L + 1)
                dve.wait_ge(*banks.taken(("conv", L, 1)))
                o = banks.filled(dve, ("conv", L, 0))
                V.tensor_tensor(cpad[:, :, CK - 1:], o.rearrange("p (m s) -> p m s", m=2),
                                csq, ALU.mult).then_inc(banks.is_free(("conv", L, 0)), 1)
                dve.wait_ge(*banks.taken(("conv", L, 0)))

                def conv_taps(j0, j1):
                    for j in range(j0, j1):
                        for m in range(2):
                            src, w = cpad[:, m, j:j + SEQ], lp(L, "cw", m * CK + j)
                            if j == 0:
                                ins = V.tensor_scalar(cacc[:, m, :], src, w, lp(L, "cb", m), ALU.mult, ALU.add)
                            else:
                                ins = V.scalar_tensor_tensor(out=cacc[:, m, :], in0=src, scalar=w,
                                                             in1=cacc[:, m, :], op0=ALU.mult, op1=ALU.add)
                            if j == CK - 1 and m == 1:
                                ins.then_inc(conv_ready, 1)
                            elif m == 1:
                                step(ins)

                conv_taps(0, 12)
                for j in range(4):
                    dve.wait_ge(*banks.taken(("xbc", L, j)))
                    for i in range(SCONV):
                        for m in (2 * j, 2 * j + 1):
                            src, w = xpad[:, m, i:i + SEQ], lp(L, "sw", m * SCONV + i)
                            if i == 0:
                                ins = V.tensor_scalar(xbcT[:, m, :], src, w, None, ALU.mult)
                            else:
                                ins = V.scalar_tensor_tensor(out=xbcT[:, m, :], in0=src, scalar=w,
                                                             in1=xbcT[:, m, :], op0=ALU.mult, op1=ALU.add)
                            if i == SCONV - 1:
                                ins.then_inc(xtap_ready, 1)
                            elif m % 2:
                                step(ins)
                dve.wait_ge(lss_ready, 4 * (L + 1))
                V.tensor_scalar(lms[:, 0:2], lss[:, 0:2], 1.0 / QRANK, RMS_EPS, ALU.mult, ALU.add)
                V.tensor_scalar(lms[:, 2:4], lss[:, 2:4], 1.0 / KVRANK, RMS_EPS, ALU.mult, ALU.add).then_inc(
                    lms_ready, 1)
                for t in range(NT):
                    ins = V.tensor_tensor(dtx[:, t * SH:t * SH + SH], sm[:, t, 0:SH], lp(L, "dtb", 0, SH), ALU.add)
                step(ins)
                V.scalar_tensor_tensor(out=dtn, in0=dtx, scalar=-1.0, in1=dtx, op0=ALU.mult, op1=ALU.min).then_inc(
                    dtn_ready, 1)
                dve.wait_ge(dte_ready, L + 1)
                V.tensor_scalar(dtu, dte, 1.0, None, ALU.add).then_inc(dtu_ready, 1)
                dve.wait_ge(lrm_ready, L + 1)
                step(V.reciprocal(lrs, lrm))
                for t in range(NT):
                    V.tensor_scalar(sm[:, t, S_CQ:S_CQ + QRANK], sm[:, t, S_CQ:S_CQ + QRANK], lrs[:, t:t + 1],
                                    None, ALU.mult)
                    last = V.tensor_scalar(sm[:, t, S_CKV:S_CKV + KVRANK], sm[:, t, S_CKV:S_CKV + KVRANK],
                                           lrs[:, 2 + t:3 + t], None, ALU.mult)
                last.then_inc(cn_ready, 1)
                step(V.scalar_tensor_tensor(out=dtc, in0=dtu, scalar=-1.0, in1=dte, op0=ALU.add, op1=ALU.subtract))
                step(V.reciprocal(dtn, dtu))
                step(V.tensor_tensor(dtc, dtc, dtn, ALU.mult))
                dve.wait_ge(dtl_ready, L + 1)
                step(V.tensor_tensor(dtc, dtl, dtc, ALU.subtract))
                step(V.scalar_tensor_tensor(out=dt, in0=dtx, scalar=0.0, in1=dtc, op0=ALU.max, op1=ALU.add))
                dve.wait_ge(nega_ready, L + 1)
                for t in range(NT):
                    last = V.scalar_tensor_tensor(out=adt[:, t * SH:t * SH + SH], in0=dt[:, t * SH:t * SH + SH],
                                                  scalar=-1.0, in1=nega, op0=ALU.mult, op1=ALU.mult)
                last.then_inc(adt_ready, 1)
                dve.wait_ge(adt_ready, L + 1)
                dve.wait_ge(xtap_ready, XT * (L + 1))
                for t in range(NT):
                    for g in range(SG):
                        for hd in range(4 * g, 4 * g + 4):
                            last = V.tensor_scalar(dec[:, t, hd, :], tri, adt[:, t * SH + hd:t * SH + hd + 1], None,
                                                   ALU.mult)
                        last.then_inc(triadt_ready, 1)
                conv_taps(12, CK)
                if L == 0:
                    dve.wait_ge(trig_ready, 1)
                c3 = cos_t.rearrange("p (t r) -> p t r", t=NT)
                s3 = sin_t.rearrange("p (t r) -> p t r", t=NT)
                tmp = [ctmp[:, i * NT * HR:(i + 1) * NT * HR].rearrange("p (t r) -> p t r", t=NT) for i in range(4)]
                step(rotate(sm[:, :, S_KR:S_KR + HR], sm[:, :, S_KR + HR:S_KR + ROPE], c3, s3, *tmp))
                for t in range(NT):
                    for hd in range(MH):
                        V.tensor_copy(kf[:, t, hd, NOPE:], sm[:, t, S_KR:S_KR + ROPE])
                for t in range(NT):
                    dve.wait_ge(*banks.taken(("q", L, t)))
                    ct = c3[:, t:t + 1, :].to_broadcast([P, MH, HR])
                    s_ = s3[:, t:t + 1, :].to_broadcast([P, MH, HR])
                    tmp = [xdd[:, i * MH * HR:(i + 1) * MH * HR].rearrange("p (h r) -> p h r", h=MH)
                           for i in range(4)]
                    last = rotate(qf[:, t, :, NOPE:NOPE + HR], qf[:, t, :, NOPE + HR:], ct, s_, *tmp)
                    if t < NT - 1:
                        step(last)
                last.then_inc(qk_ready, 1)
                for t in range(NT):
                    o = banks.filled(dve, ("xtok", L, t))
                    V.tensor_tensor(heads(xd[:, t, :]), heads(o), bc(dt[:, t * SH:t * SH + SH], SHD), ALU.mult)
                    V.tensor_tensor(heads(dx[:, t, :]), heads(o), bc(lp(L, "dskip", 0, SH), SHD),
                                    ALU.mult).then_inc(banks.is_free(("xtok", L, t)), 1)
                    dve.wait_ge(*banks.taken(("xtok", L, t)))
                o = banks.filled(dve, ("acs", L))
                V.tensor_copy(acs, o[:, 0:3 * SH]).then_inc(banks.is_free(("acs", L)), 1)
                dve.wait_ge(*banks.taken(("acs", L)))
                V.tensor_tensor(dst, acs[:, 2 * SH:], acs[:, 0:SH], ALU.subtract).then_inc(acsd_ready, 1)
                o = banks.filled(dve, ("cb", L))
                V.tensor_tensor(cbm.rearrange("p t g l -> p (t g) l"), o.rearrange("p (a l) -> p a l", l=P),
                                tri.unsqueeze(1).to_broadcast([P, NT * SG, P]), ALU.mult).then_inc(
                                    banks.is_free(("cb", L)), 1)
                for t in range(NT):
                    for g in range(SG):
                        o = banks.filled(dve, ("seg", L, t, g))
                        for i in range(4):
                            hd = 4 * g + i
                            c = t * SH + hd
                            last = V.tensor_scalar(dec[:, t, hd, :], o[:, i * P:i * P + P], acs[:, c:c + 1], 0.0,
                                                   ALU.subtract, ALU.min)
                        last.then_inc(banks.is_free(("seg", L, t, g)), 1)
                dve.wait_ge(ea_ready, L + 1)
                V.tensor_tensor(heads(xdd), heads(xd[:, 0, :]), bc(dst, SHD), ALU.mult).then_inc(xdd_ready, 1)
                scale = float(QD) ** -0.5
                o = banks.filled(dve, ("sc", L, 0))
                step(V.scalar_tensor_tensor(out=sc[0], in0=heads(o, MH), scalar=scale,
                                            in1=mask[:, P:].unsqueeze(1).to_broadcast([P, MH, P]),
                                            op0=ALU.mult, op1=ALU.add))
                V.tensor_reduce(rden[:, 0:4], sc[0], AX.X, ALU.max).then_inc(banks.is_free(("sc", L, 0)), 1)
                dve.wait_ge(*banks.taken(("sc", L, 0)))
                V.tensor_scalar(nm[:, 0:4], rden[:, 0:4], -1.0, None, ALU.mult).then_inc(score_ready, 1)
                for j in range(2):
                    o = banks.filled(dve, ("sc", L, 1 + j))
                    v = sc[1][:, 2 * j:2 * j + 2, :]
                    step(V.scalar_tensor_tensor(out=v, in0=heads(o, 2), scalar=scale,
                                                in1=mask.unsqueeze(1).to_broadcast([P, 2, SEQ]),
                                                op0=ALU.mult, op1=ALU.add))
                    V.tensor_reduce(rden[:, 4 + 2 * j:6 + 2 * j], v, AX.X, ALU.max).then_inc(
                        banks.is_free(("sc", L, 1 + j)), 1)
                    dve.wait_ge(*banks.taken(("sc", L, 1 + j)))
                V.tensor_scalar(nm[:, 4:8], rden[:, 4:8], -1.0, None, ALU.mult).then_inc(score_ready, 1)
                o = banks.filled(dve, ("mean", L))
                c2 = cacc.rearrange("p m s -> p (m s)")
                q2 = csq.rearrange("p m s -> p (m s)")
                V.tensor_tensor(c2, c2, o, ALU.subtract).then_inc(banks.is_free(("mean", L)), 1)
                for t in range(NT):
                    for g in range(SG):
                        dve.wait_ge(dec_ready, 4 * L + 2 * t + g + 1)
                        v = dec[:, t, 4 * g:4 * g + 4, :]
                        V.tensor_tensor(v, v, cbm[:, t, g:g + 1, :].to_broadcast([P, 4, P]), ALU.mult).then_inc(
                            mix_ready, 1)
                o = banks.filled(dve, ("var", L))
                V.tensor_scalar(q2, o, LN_EPS, None, ALU.add).then_inc(banks.is_free(("var", L)), 1)
                dve.wait_ge(crms_ready, L + 1)
                step(V.reciprocal(q2, q2))
                V.tensor_tensor(c2, c2, q2, ALU.mult).then_inc(chn_ready, 1)
                o0 = banks.filled(dve, ("yd", L, 0))
                V.tensor_tensor(ytok[:, 0, 0:SSDW], o0, dx[:, 0, :], ALU.add).then_inc(banks.is_free(("yd", L, 0)), 1)
                o1_ = banks.filled(dve, ("yd", L, 1))
                V.tensor_tensor(ytok[:, 1, 0:SSDW], o1_, dx[:, 1, :], ALU.add).then_inc(banks.is_free(("yd", L, 1)), 1)
                oo = banks.filled(dve, ("yo", L))
                V.tensor_tensor(heads(xdd), heads(oo), bc(ea, SHD), ALU.mult).then_inc(banks.is_free(("yo", L)), 1)
                dve.wait_ge(*banks.taken(("yo", L)))
                step(V.tensor_tensor(ytok[:, 1, 0:SSDW], ytok[:, 1, 0:SSDW], xdd, ALU.add))
                for t in range(NT):
                    dve.wait_ge(*banks.taken(("z", L, t)))
                V.tensor_tensor(ytok[:, :, 0:SSDW], ytok[:, :, 0:SSDW], z, ALU.mult).then_inc(ygz_ready, 1)
                dve.wait_ge(prob_ready, 8 * (L + 1))
                step(V.reciprocal(rden, den))
                o = banks.filled(dve, ("pv", L))
                for t in range(NT):
                    last = V.tensor_tensor(heads(ytok[:, t, SSDW:], MH), heads(o[:, t * 256:t * 256 + 256], MH),
                                           bc(rden[:, 4 * t:4 * t + 4], VD), ALU.mult)
                last.then_inc(banks.is_free(("pv", L)), 1)
                dve.wait_ge(gss_ready, 4 * (L + 1))
                V.tensor_scalar(gms, gss, SG / SSDW, RMS_EPS, ALU.mult, ALU.add).then_inc(gms_ready, 1)
                dve.wait_ge(grm_ready, L + 1)
                step(V.reciprocal(grs, grm))
                for t in range(NT):
                    for g in range(SG):
                        v = ytok[:, t, g * SEQ:g * SEQ + SEQ]
                        last = V.tensor_scalar(v, v, grs[:, 2 * t + g:2 * t + g + 1], None, ALU.mult)
                last.then_inc(ytok_ready, 1)
                for j in range(3):
                    o = banks.filled(dve, ("yT", L, j))
                    for q in range(2):
                        m = 2 * j + q
                        src = o[:, q * SEQ:q * SEQ + SEQ]
                        if j < 2:
                            last = V.tensor_scalar(yT[:, 2 + m, :], src, lp(L, "sng", m), None, ALU.mult)
                        else:
                            last = V.tensor_copy(yT[:, 2 + m, :], src)
                    last.then_inc(banks.is_free(("yT", L, j)), 1)
                for half in range(2):
                    for t in range(NT):
                        o = banks.filled(dve, ("o", L, half, t))
                        v = h[:, t, half * 512:half * 512 + 512]
                        V.tensor_tensor(v, v, o, ALU.add).then_inc(banks.is_free(("o", L, half, t)), 1)

            def embed(L):
                for half in range(2):
                    buf = sg if half == 0 else hs
                    for t in range(NT):
                        dve.wait_ge(*banks.taken(("pg", L, half, t)))
                        o = banks.filled(dve, ("pp", L, half, t))
                        V.tensor_tensor(buf[:, t, :], o, buf[:, t, :], ALU.mult).then_inc(
                            banks.is_free(("pp", L, half, t)), 1)
                        dve.wait_ge(*banks.taken(("pp", L, half, t)))
                        v = h[:, t, half * 512:half * 512 + 512]
                        last = V.tensor_tensor(v, v, buf[:, t, :], ALU.add)
                last.then_inc(h_ready, 1)

            def experts():
                for t in range(NT):
                    o = banks.filled(dve, ("lg", t))
                    V.tensor_copy(logits[:, t * NE:t * NE + NE], o[:, 0:NE]).then_inc(banks.is_free(("lg", t)), 1)
                    dve.wait_ge(*banks.taken(("lg", t)))
                    lt, tt = logits[:, t * NE:t * NE + NE], top[:, t * 8:t * 8 + 8]
                    step(V.max(out=tt, in_=lt))
                    step(V.max_index(out=tinyi[:, t * 8:t * 8 + 8], in_max=tt, in_values=lt))
                    V.tensor_copy(topi[:, 2 * t:2 * t + 2], tinyi[:, t * 8:t * 8 + 2])
                    step(V.tensor_tensor(dv[:, t:t + 1], tt[:, 1:2], tt[:, 0:1], ALU.subtract))
                V.tensor_copy(g2, dv).then_inc(dv_ready, 1)
                dve.wait_ge(ev_ready, 1)
                step(V.tensor_scalar(g1, ev, 1.0, None, ALU.add))
                step(V.reciprocal(g1, g1))
                step(V.tensor_tensor(g2, ev, g1, ALU.mult))
                for t in range(NT):
                    c = slice(t * NE, t * NE + NE)
                    V.tensor_scalar(o1[:, c], iota[:, 0:NE], topi[:, 2 * t:2 * t + 1], None, ALU.is_equal)
                    step(V.tensor_scalar(o2[:, c], iota[:, 0:NE], topi[:, 2 * t + 1:2 * t + 2], None, ALU.is_equal))
                V.tensor_tensor(chosen, o1, o2, ALU.add).then_inc(chosen_ready, 1)
                for t in range(NT):
                    c = slice(t * NE, t * NE + NE)
                    step(V.tensor_scalar(gate_of[:, t, 0:NE], o1[:, c], g1[:, t:t + 1], None, ALU.mult))
                    step(V.scalar_tensor_tensor(out=gate_of[:, t, 0:NE], in0=o2[:, c], scalar=g2[:, t:t + 1],
                                                in1=gate_of[:, t, 0:NE], op0=ALU.mult, op1=ALU.add))
                    V.tensor_copy(gate_of[:, t, NE:2 * NE], gate_of[:, t, 0:NE])
                V.memset(slot_of[:, :, STEPS:], -1.0)
                step(V.memset(gate_of[:, :, STEPS:], 0.0))
                o = banks.filled(dve, ("rank",))
                V.tensor_copy(cnt, o[:, 2 * NE:3 * NE])
                V.tensor_tensor(rank, o[:, 0:NT * NE], chosen, ALU.mult).then_inc(banks.is_free(("rank",)), 1)
                dve.wait_ge(*banks.taken(("rank",)))
                r3 = rank.rearrange("p (t e) -> p t e", t=NT)
                V.tensor_scalar(slot_of[:, :, 0:NE], r3, -1.0, None, ALU.add)
                V.tensor_scalar(slot_of[:, :, NE:2 * NE], r3, -1.0 - P, None, ALU.add)
                step(V.tensor_reduce(mx, cnt, AX.X, ALU.max))
                step(V.tensor_scalar(mx, mx, P + 0.5, float(NE), ALU.is_gt, ALU.mult))
                V.tensor_scalar(flag[:, 0:1], mx, float(NE), None, ALU.add)
                V.tensor_scalar(flag[:, 1:2], mx, NE - 1.0, None, ALU.add).then_inc(flag_ready, 1)
                dve.wait_ge(flag_ready, 1)
                n_steps = dve.value_load(flag[0:1, 0:1], min_val=NE, max_val=2 * NE)

                def build_sel(stepno):
                    for t in range(NT):
                        col = slot_of[:, t, bass.ds(stepno, 1)] if not isinstance(stepno, int) else slot_of[:, t, 0:1]
                        last = V.tensor_scalar(sel[:, t, :], iota, col, None, ALU.is_equal)
                    last.then_inc(sel_ready, 1)

                def take_xg(stepno):
                    dve.wait_ge(moe_full[5], stepno + 1)
                    for q in range(4):
                        last = V.tensor_scalar(xg[:, q, :], psum[:, 5, q * P:q * P + P], lp(1, "g_ffn", q), None,
                                               ALU.mult)
                    last.then_inc(moe_free[5], 1)

                build_sel(0)
                take_xg(0)
                with dve.Fori(0, n_steps) as e:
                    for t in range(NT):
                        last = V.tensor_scalar(selg[:, t, :], iota, slot_of[:, t, bass.ds(e, 1)],
                                               gate_of[:, t, bass.ds(e, 1)], ALU.is_equal, ALU.mult)
                    last.then_inc(selg_ready, 1)
                    dve.wait_ge(moe_full[6], e + 1)
                    build_sel(e + 1)
                    for cb in range(NCB):
                        dve.wait_ge(moe_free[0], e * NCB + cb + 2)
                        if cb >= 2:
                            dve.wait_ge(moe_full[2], e * (NCB + 1) + cb)
                        dve.wait_ge(moe_full[1], e * NCB + cb + 1)
                        V.tensor_tensor(hs[:, cb % 2, :], psum[:, 1, :], sg[:, cb % 2, :], ALU.mult).then_inc(
                            moe_free[1], 1)
                    for half in range(2):
                        dve.wait_ge(moe_full[3 + half], e * 2 + 1)
                        V.tensor_copy(ysb[:, half * 512:half * 512 + 512], psum[:, 3 + half, :]).then_inc(
                            moe_free[3 + half], 1)
                    take_xg(e + 1)
                    for i, (b, n) in enumerate(((7, 1), (3, 2), (4, 2), (7, 2))):
                        t, half = divmod(i, 2)
                        dve.wait_ge(moe_full[b], e * 2 + n)
                        v = h[:, t, half * 512:half * 512 + 512]
                        V.tensor_tensor(v, v, psum[:, b, :], ALU.add).then_inc(moe_free[b], 1)
                dve.wait_ge(moe_free[7], n_steps * MOE_FILLS[7] + 1)

            dve.wait_ge(params_in, 16)
            dve.wait_ge(pos_in, 16)
            step(V.tensor_copy(posf, pos_i[:, :]))
            for t in range(NT):
                last = V.tensor_scalar(tr0[:, t * HR:t * HR + HR], const("inv", HR), posf[:, t:t + 1], None, ALU.mult)
            step(last)
            two_pi = 2 * np.pi
            big = 1.5 * 2 ** 23
            step(V.tensor_scalar(tr1, tr0, 1 / two_pi, big, ALU.mult, ALU.add))
            step(V.tensor_scalar(tr1, tr1, -big, None, ALU.add))
            c1 = 6.28125
            c2 = float(np.floor((two_pi - c1) * 2 ** 17) / 2 ** 17)
            c3 = float(np.floor((two_pi - c1 - c2) * 2 ** 28) / 2 ** 28)
            c4 = float(np.float32(two_pi - c1 - c2 - c3))
            for c in (c1, c2, c3, c4):
                step(V.scalar_tensor_tensor(out=tr0, in0=tr1, scalar=-c, in1=tr0, op0=ALU.mult, op1=ALU.add))
            pi = 3.1415925
            step(V.tensor_scalar(tr0, tr0, pi, -pi, ALU.min, ALU.max))
            step(V.scalar_tensor_tensor(out=tr2, in0=tr0, scalar=-1.0, in1=tr0, op0=ALU.mult, op1=ALU.min))
            V.tensor_scalar(tr1, tr2, float(np.pi / 2), None, ALU.add).then_inc(trig_arg, 1)

            for L in range(DEPTH):
                if L == 0:
                    dve.wait_ge(x_in, 16)
                norm(3 * L)
                take_xT(3 * L, L, "g_attn")
                mixers(L)
                norm(3 * L + 1)
                take_xT(3 * L + 1, L, "g_ffn")
                if L == 0:
                    for cb in range(NCB):
                        for t in range(NT):
                            if cb:
                                banks.filled(dve, ("hT", cb - 1, t))
                            dve.wait_ge(*banks.taken(("g", cb, t)))
                            o = banks.filled(dve, ("u", cb, t))
                            V.tensor_tensor(hs[:, t, :], o, sg[:, t, :], ALU.mult).then_inc(
                                banks.is_free(("u", cb, t)), 1)
                    for t in range(NT):
                        for half in range(2):
                            o = banks.filled(dve, ("d", t, half))
                            v = h[:, t, half * 512:half * 512 + 512]
                            V.tensor_tensor(v, v, o, ALU.add).then_inc(banks.is_free(("d", t, half)), 1)
                else:
                    experts()
                norm(3 * L + 2)
                take_xT(3 * L + 2, L, "g_ple")
                embed(L)
            k = 3 * DEPTH
            dve.wait_ge(sumsq, NT * (k + 1))
            V.tensor_scalar(ms, ss, 1.0 / D, RMS_EPS, ALU.mult, ALU.add).then_inc(ms_ready, 1)
            dve.wait_ge(rms_ready, k + 1)
            step(V.reciprocal(rstd, rms))
            dve.wait_ge(gfin_in, 16)
            for t in range(NT):
                V.scalar_tensor_tensor(out=xs[:, t, :], in0=h[:, t, :], scalar=rstd[:, t:t + 1], in1=gfin,
                                       op0=ALU.mult, op1=ALU.mult).then_inc(out_ready, 1)


def _constants():
    i = np.arange(P)
    group = (i[:, None] // 64 == i[None, :] // 64) / np.float32(64)
    mask = np.zeros((P, 2 * P))
    mask[:, P:] = np.where(i[:, None] >= i[None, :], 0.0, NEG)
    inv = np.float32(10000.0) ** (-np.arange(0, ROPE, 2, dtype=np.float32) / np.float32(ROPE))
    parts = [np.eye(P), i[:, None] <= i[None, :], np.ones((P, P)), group, np.tile(i, (P, 1)), mask,
             np.tile(inv, (P, 1))]
    return [a.astype(np.float32) for a in parts]


def _by_partition(a):
    a = np.asarray(a)
    return np.moveaxis(a.reshape(a.shape[:-1] + (-1, P)), -1, 0)


def _spread(a):
    return np.broadcast_to(np.asarray(a)[None], (P,) + np.asarray(a).shape)


def kernel(**inputs):
    import concourse.bacc as bacc
    from concourse.bass_utils import run_bass_kernel_spmd

    v = {k: np.asarray(a) for k, a in inputs.items()}
    parts = _constants()
    for L in range(DEPTH):
        parts += [_by_partition(v["attn_norm_g"][L]), _by_partition(v["ffn_norm_g"][L]),
                  _by_partition(v["ple_norm_g"][L]),
                  _by_partition(v["conv_dw_w"][L]).transpose(0, 2, 1).reshape(P, -1),
                  _by_partition(v["conv_dw_b"][L]), _by_partition(v["conv_ln_g"][L]),
                  _by_partition(v["conv_ln_b"][L]),
                  _by_partition(v["ssd_conv_w"][L]).transpose(0, 2, 1).reshape(P, -1),
                  _by_partition(v["ssd_conv_b"][L]), _spread(v["ssd_dt_bias"][L]), _spread(v["ssd_a_log"][L]),
                  _spread(v["ssd_d"][L]), _by_partition(v["ssd_norm_g"][L]), _by_partition(v["mla_q_norm_g"][L]),
                  _by_partition(v["mla_kv_norm_g"][L])]
    params = np.ascontiguousarray(np.concatenate(parts, axis=1))
    v["positions"] = v["positions"].reshape(NT, P).T
    names = ["x", "p", "positions", "w_in", "mla_w_uq", "mla_w_ukv", "w_out", "dense_w_gate", "dense_w_up",
             "dense_w_down", "moe_router", "moe_w_gate", "moe_w_up", "moe_w_down", "ple_w_gate", "ple_w_proj",
             "final_norm_g"]
    arrays = {"params": params, **{n: np.ascontiguousarray(v[n]) for n in names}}
    nc = bacc.Bacc("TRN2", target_bir_lowering=False, num_devices=1)
    args = [nc.dram_tensor("in_" + n, a.shape, mybir.dt.from_np(a.dtype), kind="ExternalInput").ap()
            for n, a in arrays.items()]
    out = nc.dram_tensor("out", (1, SEQ, D), F32, kind="ExternalOutput").ap()
    trunk(nc, *args, out)
    r = run_bass_kernel_spmd(nc, [{"in_" + n: a for n, a in arrays.items()}], core_ids=[0])
    return r.results[0]["out"]
```

```python
from contextlib import ExitStack

import numpy as np
import concourse.bass as bass
from concourse import mybir

F32 = mybir.dt.float32
F32R = mybir.dt.float32r
I32 = mybir.dt.int32
U32 = mybir.dt.uint32
ALU = mybir.AluOpType
ACT = mybir.ActivationFunctionType
AX = mybir.AxisListType

P = 128
D = 1024
KT = D // P
SEQ = 256
NT = SEQ // P
DEPTH = 2
PLE = 256
CONVW = 256
CK = 31
SSDW = 512
SH = 8
SHD = SSDW // SH
SG = 2
SN = 128
SCONV = 4
XBC = SSDW + 2 * SG * SN
XT = XBC // P
MH = 4
NOPE = 64
ROPE = 32
HR = ROPE // 2
VD = 64
QD = NOPE + ROPE
QRANK = 256
KVRANK = 128
FF = 3584
FB = 512
NCB = FF // FB
FKT = FF // P
NE = 8
RMS_EPS = 1e-6
LN_EPS = 1e-5
C_CONV, C_Z, C_XBC = 0, 2 * CONVW, 2 * CONVW + SSDW
C_SM = C_XBC + XBC
SMW = SH + QRANK + KVRANK + ROPE
IN_COLS = C_SM + SMW
S_CQ, S_CKV, S_KR = SH, SH + QRANK, SH + QRANK + KVRANK
B_SIZE = NT * SMW + 2 * NT * SSDW + 2 * NT * MH * QD + NT * MH * VD + 2 * MH * SEQ + 3 * SEQ
SLOTS = 7
UNIT = 2048
SPLITS = 3
HALF_K = KT // 2
EXPERT_UNITS = 6 * NCB
DOWN_UNITS = 2 * NCB
assert EXPERT_UNITS % SLOTS == 0 and EXPERT_UNITS % SPLITS == 0
NEG = -1e30


def layout(parts):
    at, out = 0, {}
    for name, n in parts:
        out[name] = at
        at += n
    return out, at


CONST_PARTS = [("ident", P), ("tri", P), ("ones", P), ("group", P), ("iota", P), ("mask", 2 * P), ("inv", HR)]
LAYER_PARTS = [("g_attn", KT), ("g_ffn", KT), ("g_ple", KT), ("cw", 2 * CK), ("cb", 2), ("lng", 2), ("lnb", 2),
               ("sw", XT * SCONV), ("sb", XT), ("dtb", SH), ("alog", SH), ("dskip", SH), ("sng", SSDW // P),
               ("qg", 2), ("kvg", 1)]
CONST_AT, CONST_N = layout(CONST_PARTS)
LAYER_AT, LAYER_N = layout(LAYER_PARTS)


def trunk(nc, params, x, p, positions, w_in, w_uq, w_ukv, w_out, dense_g, dense_u, dense_d, router,
          moe_g, moe_u, moe_d, ple_g, ple_p, final_g, out):
    with ExitStack() as ctx:
        def sb(name, n, dt=F32):
            return ctx.enter_context(nc.sbuf_tensor(name, [P, n], dt))

        def sem(name):
            return ctx.enter_context(nc.semaphore(name))

        def shared(name, n, over, n_over):
            at = -(-nc.sbuf_base // 32) * 32
            buf = sb(name, n)
            return buf, nc.alloc_sbuf_tensor_at(over, [P, n_over], F32R, offset=at)

        ring = sb("ring", SLOTS * UNIT)
        w_hi = sb("w_hi", SPLITS * UNIT, F32R)
        w_lo = sb("w_lo", SPLITS * UNIT, F32R)
        h_b = sb("h", NT * D)
        xs_b = sb("xs", NT * D)
        xT_b, xT_r = shared("xT", 2 * NT * D, "xT_parts", 2 * NT * D)
        arena_a, arena_a_r = shared("arena_a", FKT * SEQ, "hidden_a", FKT * SEQ)
        arena_b, arena_b_r = shared("arena_b", B_SIZE, "hidden_b", FKT * SEQ)
        par = sb("par", CONST_N + DEPTH * LAYER_N)
        wq_b = sb("wq", 2 * MH * QD)
        wkv_b = sb("wkv", MH * (NOPE + VD))
        rt = sb("rt", KT * NE)
        rt_r = sb("rt_parts", 2 * KT * NE, F32R)
        pos_i = sb("pos_i", NT, I32)
        trig = sb("trig", 5 * NT * HR)
        tiny = sb("tiny", 560)
        tinyi = sb("tinyi", 2 * 8, U32)
        flag = sb("flag", 1, I32)
        psum = ctx.enter_context(nc.psum_tensor("psum", [P, 8, 512], F32))

        h = h_b[:, :].rearrange("p (t d) -> p t d", t=NT)
        xs = xs_b[:, :].rearrange("p (t d) -> p t d", t=NT)
        xT_hi = xT_r[:, 0:NT * D].rearrange("p (k s) -> p k s", k=KT)
        xT_lo = xT_r[:, NT * D:].rearrange("p (k s) -> p k s", k=KT)

        def const(name, n=P):
            return par[:, CONST_AT[name]:CONST_AT[name] + n]

        def lp(L, name, i=0, n=1):
            a = CONST_N + L * LAYER_N + LAYER_AT[name] + i
            return par[:, a:a + n]

        ident, tri, ones, group, iota = (const(n) for n in ("ident", "tri", "ones", "group", "iota"))
        mask = const("mask", 2 * P)

        class View:

            def __init__(self, buf, at, end):
                self.buf, self.at, self.end = buf, at, end

            def __call__(self, n):
                a, self.at = self.at, self.at + n
                assert self.at <= self.end, (self.at, self.end)
                return self.buf[:, a:a + n]

        va = View(arena_a, 0, FKT * SEQ)
        cpad_f = va(2 * (CK - 1 + SEQ))
        cpad = cpad_f.rearrange("p (m s) -> p m s", m=2)
        xpad_f = va(XT * (SCONV - 1 + SEQ))
        xpad = xpad_f.rearrange("p (m s) -> p m s", m=XT)
        xbcT = va(XT * SEQ).rearrange("p (m s) -> p m s", m=XT)
        z = va(NT * SSDW).rearrange("p (t c) -> p t c", t=NT)
        cacc = va(2 * SEQ).rearrange("p (m s) -> p m s", m=2)
        csq = va(2 * SEQ).rearrange("p (m s) -> p m s", m=2)
        ctmp = va(4 * NT * HR)
        hT_hi = arena_a_r[:, :].rearrange("p (k s) -> p k s", k=FKT)
        hT_lo = arena_b_r[:, :].rearrange("p (k s) -> p k s", k=FKT)
        ehT_hi = arena_a_r[:, 0:FKT * P].rearrange("p (k s) -> p k s", k=FKT)
        ehT_lo = arena_a_r[:, FKT * P:].rearrange("p (k s) -> p k s", k=FKT)
        dec = xpad_f[:, 0:NT * SH * P].rearrange("p (t h l) -> p t h l", t=NT, h=SH)
        cbm = cpad_f[:, 0:NT * SG * P].rearrange("p (t g l) -> p t g l", t=NT, g=SG)
        vb = View(arena_b, 0, B_SIZE)
        sm_f = vb(NT * SMW)
        sm = sm_f.rearrange("p (t c) -> p t c", t=NT)
        xd = vb(NT * SSDW).rearrange("p (t c) -> p t c", t=NT)
        dx = vb(NT * SSDW).rearrange("p (t c) -> p t c", t=NT)
        st = sm_f[:, 0:SSDW]
        qk_f = vb(2 * NT * MH * QD)
        qf = qk_f[:, 0:NT * MH * QD].rearrange("p (t h d) -> p t h d", t=NT, h=MH)
        kf = qk_f[:, NT * MH * QD:].rearrange("p (t h d) -> p t h d", t=NT, h=MH)
        sc_f = [qk_f[:, 0:MH * P], qk_f[:, MH * P:3 * MH * P]]
        sc = [s.rearrange("p (h k) -> p h k", h=MH) for s in sc_f]
        vs = vb(NT * MH * VD).rearrange("p (t h d) -> p t h d", t=NT, h=MH)
        qT = vb(MH * SEQ).rearrange("p (h s) -> p h s", h=MH)
        kT = vb(MH * SEQ).rearrange("p (h s) -> p h s", h=MH)
        cqT = vb(2 * SEQ).rearrange("p (k s) -> p k s", k=2)
        ckvT = vb(SEQ)
        YW = SSDW + MH * VD
        ytok = xs_b[:, 0:NT * YW].rearrange("p (t c) -> p t c", t=NT)
        xdd = xs_b[:, NT * YW:NT * YW + SSDW]
        yT_hi, yT_lo = xT_hi, xT_lo
        btok = xT_b[:, 2 * SEQ:2 * SEQ + SG * SN].rearrange("p (g n) -> p g n", g=SG)
        prT_f = xT_b[:, NT * D + 2 * SEQ:NT * D + 2 * SEQ + 3 * MH * P]
        prT = [prT_f[:, 0:MH * P].rearrange("p (h b q) -> p h b q", h=MH, b=1),
               prT_f[:, MH * P:].rearrange("p (h b q) -> p h b q", h=MH, b=2)]
        dsg = xs_b[:, 0:NT * FB].rearrange("p (t c) -> p t c", t=NT)
        dhs = xs_b[:, NT * FB:].rearrange("p (t c) -> p t c", t=NT)
        xg_hi = arena_b_r[:, 0:KT * P].rearrange("p (k s) -> p k s", k=KT)
        xg_lo = arena_b_r[:, KT * P:2 * KT * P].rearrange("p (k s) -> p k s", k=KT)
        vf = View(arena_b, 2 * KT * P, B_SIZE)
        sg = vf(2 * FB).rearrange("p (t c) -> p t c", t=2)
        hs = vf(2 * FB).rearrange("p (t c) -> p t c", t=2)
        ysb = vf(D)
        sel = vf(NT * P).rearrange("p (t s) -> p t s", t=NT)
        selg = vf(NT * P).rearrange("p (t s) -> p t s", t=NT)
        selgT = vf(NT * P).rearrange("p (t s) -> p t s", t=NT)
        vp = View(arena_b, FKT * SEQ, B_SIZE)
        ptok = vp(NT * PLE).rearrange("p (t c) -> p t c", t=NT)
        pT_hi = arena_a_r[:, 0:2 * SEQ].rearrange("p (k s) -> p k s", k=2)
        pT_lo = arena_a_r[:, 2 * SEQ:4 * SEQ].rearrange("p (k s) -> p k s", k=2)
        gfin = arena_a[:, 4 * SEQ:4 * SEQ + D]
        wq = wq_b[:, :].rearrange("p (k n) -> p k n", k=2)
        rt_v = rt[:, :].rearrange("p (k n) -> p k n", k=KT)
        rt_hi = rt_r[:, 0:KT * NE].rearrange("p (k n) -> p k n", k=KT)
        rt_lo = rt_r[:, KT * NE:].rearrange("p (k n) -> p k n", k=KT)

        cos_t, sin_t, tr0, tr1, tr2 = (trig[:, i * NT * HR:(i + 1) * NT * HR] for i in range(5))

        vt = View(tiny, 0, 560)
        ss = vt(2)
        ms = vt(2)
        rms = vt(2)
        rstd = vt(2)
        dtx, dtn, dte, dtu, dtl, dtc, dt, adt = (vt(NT * SH) for _ in range(8))
        nega = vt(SH)
        acs = vt(3 * SH)
        ea, dst = vt(SH), vt(SH)
        lss, lms, lrm, lrs = (vt(4) for _ in range(4))
        gss, gms, grm, grs = (vt(4) for _ in range(4))
        nm, den, rden = vt(8), vt(8), vt(8)
        posf = vt(NT)
        logits = vt(NT * NE)
        top = vt(NT * 8)
        topi = vt(NT * 2)
        dv, ev, g1, g2 = (vt(NT) for _ in range(4))
        o1, o2 = vt(NT * NE), vt(NT * NE)
        chosen = vt(NT * NE)
        rank = vt(NT * NE)
        STEPS = 2 * NE
        slot_of = vt(NT * (STEPS + 1)).rearrange("p (t e) -> p t e", t=NT)
        gate_of = vt(NT * (STEPS + 1)).rearrange("p (t e) -> p t e", t=NT)
        cnt = vt(NE)
        mx = vt(1)

        loaded = [sem(f"loaded{s}") for s in range(SLOTS)]
        hi_ready, lo_ready, unit_used = sem("hi_ready"), sem("lo_ready"), sem("unit_used")
        x_hi_ready, y_hi_ready, conv_hi_ready, h_hi_ready, p_hi_ready, rt_ready = (sem(n) for n in (
            "x_hi_ready", "y_hi_ready", "conv_hi_ready", "h_hi_ready", "p_hi_ready", "rt_ready"))
        moe_x_hi, moe_h_hi = sem("moe_x_hi"), sem("moe_h_hi")
        params_in, x_in, pos_in, wsmall_in = (sem(n) for n in ("params_in", "x_in", "pos_in", "wsmall_in"))
        ptok_in, gfin_in, out_ready, out_done = (sem(n) for n in ("ptok_in", "gfin_in", "out_ready", "out_done"))
        h_ready, sumsq, ms_ready, rms_ready, xs_ready = (sem(n) for n in (
            "h_ready", "sumsq", "ms_ready", "rms_ready", "xs_ready"))
        conv_ready, csq_ready, crms_ready, chn_ready = (sem(n) for n in (
            "conv_ready", "csq_ready", "crms_ready", "chn_ready"))
        (xtap_ready, xbc_ready, pads_ready) = (sem(n) for n in ("xtap_ready", "xbc_ready", "pads_ready"))
        (dtn_ready, dte_ready, dtu_ready, dtl_ready, nega_ready, adt_ready, acsd_ready, ea_ready, triadt_ready,
         dec_ready, mix_ready, xdd_ready, ygz_ready, gss_ready, gms_ready, grm_ready, ytok_ready) = (
             sem(n) for n in ("dtn_ready", "dte_ready", "dtu_ready", "dtl_ready", "nega_ready", "adt_ready",
                              "acsd_ready", "ea_ready", "triadt_ready", "dec_ready", "mix_ready", "xdd_ready",
                              "ygz_ready", "gss_ready", "gms_ready", "grm_ready", "ytok_ready"))
        (lss_ready, lms_ready, lrm_ready, cn_ready, qk_ready, score_ready, prob_ready, yT_ready) = (
            sem(n) for n in ("lss_ready", "lms_ready", "lrm_ready", "cn_ready", "qk_ready", "score_ready",
                             "prob_ready", "yT_ready"))
        (chosen_ready, dv_ready, ev_ready, flag_ready, sel_ready, selg_ready) = (sem(n) for n in (
            "chosen_ready", "dv_ready", "ev_ready", "flag_ready", "sel_ready", "selg_ready"))
        trig_arg, trig_ready = sem("trig_arg"), sem("trig_ready")
        dve_step = sem("dve_step")

        class Banks:

            def __init__(self):
                self.full = [sem(f"full{b}") for b in range(8)]
                self.free = [sem(f"free{b}") for b in range(8)]
                self.count = [0] * 8
                self.uses = {}

            def fill(self, pe, name, b):
                if self.count[b]:
                    pe.wait_ge(self.free[b], self.count[b])
                self.count[b] += 1
                self.uses[name] = (b, self.count[b])
                return psum[:, b, :]

            def is_full(self, name):
                return self.full[self.uses[name][0]]

            def filled(self, eng, name):
                b, n = self.uses[name]
                eng.wait_ge(self.full[b], n)
                return psum[:, b, :]

            def is_free(self, name):
                return self.free[self.uses[name][0]]

            def taken(self, name):
                b, n = self.uses[name]
                return self.free[b], n

        banks = Banks()
        moe_full = [sem(f"moe_full{b}") for b in range(8)]
        moe_free = [sem(f"moe_free{b}") for b in range(8)]
        MOE_USED = 2 * NCB + DOWN_UNITS - 1
        MOE_FILLS = [NCB, NCB, NCB + 1, 2, 2, 1, 1, 2]

        def by_cols(w, c0, n=SEQ):
            return [(w.rearrange("(k p) n -> p k n", p=P)[:, :, c0:c0 + n], KT, n)]

        def by_rows(w, c0, n=512):
            v = w.rearrange("(k p) n -> p k n", p=P)
            return [(v[:, i * HALF_K:(i + 1) * HALF_K, c0:c0 + n], HALF_K, n) for i in range(2)]

        def whole_rows(w, i):
            return [(w.rearrange("(k p) n -> p k n", p=P)[:, 2 * i:2 * i + 2, :], 2, D)]

        def layer_front(L):
            wi, wo = w_in[L], w_out[L]
            return (sum((by_cols(wi, C_CONV + SEQ * i) for i in range(2)), [])
                    + sum((by_cols(wi, C_XBC + SEQ * i) for i in range(4)), [])
                    + by_rows(wi, C_SM, SMW) + by_rows(wi, C_Z) + by_rows(wo, 0) + by_rows(wo, 512))

        def layer_ple(L):
            return by_rows(ple_g[L], 0) + by_rows(ple_g[L], 512) + whole_rows(ple_p[L], 0)

        def swiglu_unit(g, u, d, c):
            if c < 4 * NCB:
                return by_rows(g if c % 4 < 2 else u, (c // 4) * FB)[c % 2]
            return whole_rows(d, c - 4 * NCB)[0]

        FRONT = layer_front(0)
        NF = len(FRONT)
        before_moe = FRONT + [swiglu_unit(dense_g[0], dense_u[0], dense_d[0], c)
                              for c in range(EXPERT_UNITS)] + layer_ple(0) + layer_front(1)
        after_moe = layer_ple(1)
        N0 = len(before_moe)
        sizes = [k * n for _, k, n in before_moe] + [UNIT] * (EXPERT_UNITS + len(after_moe))
        last_reader = []

        def raw(g, n=UNIT):
            return ring[:, (g % SLOTS) * UNIT:(g % SLOTS) * UNIT + n]

        def part(buf, g, n=UNIT):
            return buf[:, (g % SPLITS) * UNIT:(g % SPLITS) * UNIT + n]

        def landed(g, e=0):
            return e * (16 * EXPERT_UNITS // SLOTS) + 16 * (g // SLOTS + 1)

        used_before_moe = []
        block = ctx.enter_context(nc.Block())

        @block.tensor
        def _(pe):
            mm, tr = nc.tensor.matmul, nc.tensor.transpose
            used = [0]

            def unit():
                g = len(last_reader)
                pe.wait_ge(lo_ready, g + 1)
                k = before_moe[g][1]
                return tuple(part(b, g, sizes[g]).rearrange("p (k n) -> p k n", k=k) for b in (w_hi, w_lo))

            def unit_done(last=None, key=None):
                if key is None:
                    used[0] += 1
                    last.then_inc(unit_used, 1)
                    last_reader.append((unit_used, used[0]))
                else:
                    b, n = banks.uses[key]
                    last_reader.append((banks.full[b], n))

            def product(o, a, b, first, final):
                mm(o, a[0], b[0], start=first, stop=False)
                mm(o, a[0], b[1], start=False, stop=False)
                return mm(o, a[1], b[0], start=False, stop=final)

            def at(parts, *index):
                return tuple(x[index] for x in parts)

            ALLP = slice(None)
            xTp, pTp = (xT_hi, xT_lo), (pT_hi, pT_lo)

            def transpose_x(key):
                for b in range(4):
                    o = banks.fill(pe, (key, b), b)
                    for q in range(2):
                        for t in range(NT):
                            kt = 2 * b + q
                            last = tr(o[:, q * SEQ + t * P:q * SEQ + t * P + P], xs[:, t, kt * P:kt * P + P], ident)
                    last.then_inc(banks.is_full((key, b)), 1)

            def wait_xT(key):
                for b in range(4):
                    pe.wait_ge(*banks.taken((key, b)))

            def channels_by_tokens(key, b):
                w = unit()
                o = banks.fill(pe, key, b)
                for m in range(2):
                    for kt in range(KT):
                        last = product(o[:, m * SEQ:m * SEQ + SEQ], at(w, ALLP, kt, slice(m * P, m * P + P)),
                                       at(xTp, ALLP, kt), kt == 0, kt == KT - 1)
                last.then_inc(banks.is_full(key), 1)
                unit_done(key=key)

            def tokens_by_channels(keys, bs, n):
                for i in range(2):
                    w = unit()
                    for t in range(NT):
                        o = banks.fill(pe, keys[t], bs[t]) if i == 0 else psum[:, bs[t], :]
                        for q in range(HALF_K):
                            kt = HALF_K * i + q
                            last = product(o[:, 0:n], at(xTp, ALLP, kt, slice(t * P, t * P + P)), at(w, ALLP, q),
                                           kt == 0, kt == KT - 1)
                        if i:
                            last.then_inc(banks.is_full(keys[t]), 1)
                    if i == 0:
                        unit_done(last)
                unit_done(key=keys[1])

            def mixers(L):
                for j in range(2):
                    channels_by_tokens(("conv", L, j), 4 + j)
                for j in range(4):
                    channels_by_tokens(("xbc", L, j), [6, 7, 0, 1][j])
                tokens_by_channels([("sm", L, t) for t in range(NT)], (2, 3), SMW)
                tokens_by_channels([("z", L, t) for t in range(NT)], (6, 7), 512)
                pe.wait_ge(cn_ready, L + 1)
                o = banks.fill(pe, ("cqT", L), 4)
                for k in range(2):
                    for t in range(NT):
                        last = tr(o[:, k * SEQ + t * P:k * SEQ + t * P + P],
                                  sm[:, t, S_CQ + k * P:S_CQ + k * P + P], ident)
                last.then_inc(banks.is_full(("cqT", L)), 1)
                o = banks.fill(pe, ("ckvT", L), 5)
                for t in range(NT):
                    last = tr(o[:, t * P:t * P + P], sm[:, t, S_CKV:S_CKV + KVRANK], ident)
                last.then_inc(banks.is_full(("ckvT", L)), 1)
                pe.wait_ge(*banks.taken(("cqT", L)))
                pe.wait_ge(*banks.taken(("ckvT", L)))
                pe.wait_ge(wsmall_in, 16 * (2 * L + 3))
                for t in range(NT):
                    key = ("q", L, t)
                    o = banks.fill(pe, key, t)
                    for k in range(2):
                        last = mm(o[:, 0:MH * QD], cqT[:, k, t * P:t * P + P], wq[:, k, :], start=k == 0, stop=k == 1)
                    last.then_inc(banks.is_full(key), 1)
                for t in range(NT):
                    o = banks.fill(pe, ("kv", L, t), 2 + t)
                    mm(o, ckvT[:, t * P:t * P + P], wkv_b[:, :], start=True, stop=True).then_inc(
                        banks.is_full(("kv", L, t)), 1)
                pe.wait_ge(xbc_ready, XT * (L + 1))
                for t in range(NT):
                    o = banks.fill(pe, ("xtok", L, t), 4 + t)
                    for m in range(4):
                        last = tr(o[:, m * P:m * P + P], xbcT[:, m, t * P:t * P + P], ident)
                    last.then_inc(banks.is_full(("xtok", L, t)), 1)
                o = banks.fill(pe, ("btok", L), 6)
                for g in range(SG):
                    last = tr(o[:, g * P:g * P + P], xbcT[:, 4 + g, 0:P], ident)
                last.then_inc(banks.is_full(("btok", L)), 1)
                o = banks.fill(pe, ("cb", L), 7)
                for t in range(NT):
                    for g in range(SG):
                        c0 = (t * SG + g) * P
                        last = mm(o[:, c0:c0 + P], xbcT[:, 4 + g, t * P:t * P + P], xbcT[:, 6 + g, t * P:t * P + P],
                                  start=True, stop=True)
                last.then_inc(banks.is_full(("cb", L)), 1)
                pe.wait_ge(qk_ready, L + 1)
                for t in range(NT):
                    pe.wait_ge(*banks.taken(("kv", L, t)))
                for n, (buf, name) in enumerate(((qf, "qT"), (kf, "kT"))):
                    for t in range(NT):
                        o = banks.fill(pe, (name, L, t), 2 * n + t)
                        for hd in range(MH):
                            last = tr(o[0:QD, hd * P:hd * P + P], buf[:, t, hd, :], ident)
                        last.then_inc(banks.is_full((name, L, t)), 1)
                pe.wait_ge(adt_ready, L + 1)
                o = banks.fill(pe, ("acs", L), 6)
                for t in range(NT):
                    mm(o[:, t * SH:t * SH + SH], tri, adt[:, t * SH:t * SH + SH], start=True, stop=True)
                mm(o[:, 2 * SH:3 * SH], ones, adt[:, 0:SH], start=True, stop=True).then_inc(
                    banks.is_full(("acs", L)), 1)
                for t in range(NT):
                    for g in range(SG):
                        pe.wait_ge(triadt_ready, 4 * L + 2 * t + g + 1)
                        key = ("seg", L, t, g)
                        o = banks.fill(pe, key, [4, 5, 7, 6][2 * t + g])
                        mm(o, ones, dec[:, t, 4 * g:4 * g + 4, :].rearrange("p h l -> p (h l)"),
                           start=True, stop=True).then_inc(banks.is_full(key), 1)
                for name in ("qT", "kT"):
                    for t in range(NT):
                        pe.wait_ge(*banks.taken((name, L, t)))
                o = banks.fill(pe, ("sc", L, 0), 0)
                for hd in range(MH):
                    last = mm(o[:, hd * P:hd * P + P], qT[0:QD, hd, 0:P], kT[0:QD, hd, 0:P], start=True, stop=True)
                last.then_inc(banks.is_full(("sc", L, 0)), 1)
                for j in range(2):
                    key = ("sc", L, 1 + j)
                    o = banks.fill(pe, key, 1 + j)
                    for i in range(2):
                        hd = 2 * j + i
                        last = mm(o[:, i * SEQ:i * SEQ + SEQ], qT[0:QD, hd, P:SEQ], kT[0:QD, hd, :],
                                  start=True, stop=True)
                    last.then_inc(banks.is_full(key), 1)
                pe.wait_ge(conv_ready, L + 1)
                o = banks.fill(pe, ("mean", L), 3)
                mm(o, group, cacc.rearrange("p m s -> p (m s)"), start=True, stop=True).then_inc(
                    banks.is_full(("mean", L)), 1)
                pe.wait_ge(*banks.taken(("btok", L)))
                pe.wait_ge(xdd_ready, L + 1)
                o = banks.fill(pe, ("st", L), 4)
                for g in range(SG):
                    last = mm(o[:, g * SEQ:g * SEQ + SEQ], btok[:, g, :], xdd[:, g * SEQ:g * SEQ + SEQ],
                              start=True, stop=True)
                last.then_inc(banks.is_full(("st", L)), 1)
                pe.wait_ge(csq_ready, L + 1)
                o = banks.fill(pe, ("var", L), 3)
                mm(o, group, csq.rearrange("p m s -> p (m s)"), start=True, stop=True).then_inc(
                    banks.is_full(("var", L)), 1)
                for t in range(NT):
                    pe.wait_ge(*banks.taken(("xtok", L, t)))
                    key = ("yd", L, t)
                    o = banks.fill(pe, key, 5 + t)
                    for hd in range(SH):
                        if hd % 4 == 0:
                            pe.wait_ge(mix_ready, 4 * L + 2 * t + hd // 4 + 1)
                        last = mm(o[:, hd * SHD:hd * SHD + SHD], dec[:, t, hd, :], xd[:, t, hd * SHD:hd * SHD + SHD],
                                  start=True, stop=True)
                    last.then_inc(banks.is_full(key), 1)
                pe.wait_ge(*banks.taken(("st", L)))
                o = banks.fill(pe, ("yo", L), 7)
                for g in range(SG):
                    last = mm(o[:, g * SEQ:g * SEQ + SEQ], xbcT[:, 6 + g, P:SEQ], st[:, g * SEQ:g * SEQ + SEQ],
                              start=True, stop=True)
                last.then_inc(banks.is_full(("yo", L)), 1)
                pe.wait_ge(prob_ready, 8 * L + 4)
                o = banks.fill(pe, ("prT", L, 0), 0)
                for hd in range(MH):
                    last = tr(o[:, hd * P:hd * P + P], sc[0][:, hd, :], ident)
                last.then_inc(banks.is_full(("prT", L, 0)), 1)
                pe.wait_ge(prob_ready, 8 * L + 8)
                for j in range(2):
                    key = ("prT", L, 1 + j)
                    o = banks.fill(pe, key, 1 + j)
                    for i in range(2):
                        for b in range(2):
                            last = tr(o[:, (2 * i + b) * P:(2 * i + b) * P + P], sc[1][:, 2 * j + i, b * P:b * P + P],
                                      ident)
                    last.then_inc(banks.is_full(key), 1)
                for j in range(3):
                    pe.wait_ge(*banks.taken(("prT", L, j)))
                o = banks.fill(pe, ("pv", L), 4)
                for t in range(NT):
                    for hd in range(MH):
                        c0 = (t * MH + hd) * VD
                        for b in range(t + 1):
                            last = mm(o[:, c0:c0 + VD], prT[t][:, hd, b, :], vs[:, b, hd, :], start=b == 0, stop=b == t)
                last.then_inc(banks.is_full(("pv", L)), 1)
                pe.wait_ge(*banks.taken(("pv", L)))
                pe.wait_ge(ytok_ready, L + 1)
                for j in range(3):
                    key = ("yT", L, j)
                    o = banks.fill(pe, key, [0, 1, 2][j])
                    for q in range(2):
                        m = 2 * j + q
                        for t in range(NT):
                            last = tr(o[:, q * SEQ + t * P:q * SEQ + t * P + P], ytok[:, t, m * P:m * P + P], ident)
                    last.then_inc(banks.is_full(key), 1)
                pe.wait_ge(yT_ready, L + 1)
                for j in range(3):
                    pe.wait_ge(*banks.taken(("yT", L, j)))
                for half in range(2):
                    tokens_by_channels([("o", L, half, t) for t in range(NT)], (4 + 2 * half, 5 + 2 * half), 512)

            def hidden_T(cb):
                for t in range(NT):
                    key = ("hT", cb, t)
                    pe.wait_ge(*banks.taken(("u", cb, t)))
                    o = banks.fill(pe, key, 4 + t)
                    for q in range(4):
                        last = tr(o[:, q * P:q * P + P], dhs[:, t, q * P:q * P + P], ident)
                    last.then_inc(banks.is_full(key), 1)

            def dense():
                for cb in range(NCB):
                    tokens_by_channels([("g", cb, t) for t in range(NT)], (0, 1), FB)
                    if cb:
                        hidden_T(cb - 1)
                    tokens_by_channels([("u", cb, t) for t in range(NT)], (2, 3), FB)
                keys = [(t, half) for t in range(NT) for half in range(2)]
                acc = {key: banks.fill(pe, ("d", *key), b) for key, b in zip(keys, (6, 7, 0, 1))}
                for j in range(DOWN_UNITS):
                    w = unit()
                    if j == 1:
                        hidden_T(NCB - 1)
                    for t in range(NT):
                        pe.wait_ge(*banks.taken(("hT", j // 2, t)))
                    for t, half in keys:
                        for q in range(2):
                            kt = 2 * j + q
                            last = product(acc[t, half], at((hT_hi, hT_lo), ALLP, kt, slice(t * P, t * P + P)),
                                           at(w, ALLP, q, slice(half * 512, half * 512 + 512)),
                                           kt == 0, kt == FKT - 1)
                        if j == DOWN_UNITS - 1:
                            last.then_inc(banks.is_full(("d", t, half)), 1)
                    if j < DOWN_UNITS - 1:
                        unit_done(last)
                unit_done(key=("d", 1, 1))

            def ple_front(L):
                pe.wait_ge(ptok_in, 16 * (L + 1))
                o = banks.fill(pe, ("pT", L), 7)
                for k in range(2):
                    for t in range(NT):
                        last = tr(o[:, k * SEQ + t * P:k * SEQ + t * P + P], ptok[:, t, k * P:k * P + P], ident)
                last.then_inc(banks.is_full(("pT", L)), 1)
                pe.wait_ge(xs_ready, 2 * (3 * L + 3))
                transpose_x(("n", 3 * L + 2))
                wait_xT(("n", 3 * L + 2))

            def ple_projection(L, w):
                pe.wait_ge(*banks.taken(("pT", L)))
                for half in range(2):
                    for t in range(NT):
                        key = ("pp", L, half, t)
                        o = banks.fill(pe, key, [6, 7, 2, 3][2 * half + t])
                        for k in range(2):
                            last = product(o, at(pTp, ALLP, k, slice(t * P, t * P + P)),
                                           at(w, ALLP, k, slice(half * 512, half * 512 + 512)), k == 0, k == 1)
                        last.then_inc(banks.is_full(key), 1)

            def ple(L):
                ple_front(L)
                for half in range(2):
                    tokens_by_channels([("pg", L, half, t) for t in range(NT)], ((4, 5), (0, 1))[half], 512)
                ple_projection(L, unit())
                unit_done(key=("pp", L, 1, 1))

            pe.wait_ge(params_in, 16)
            for L in range(DEPTH):
                pe.wait_ge(xs_ready, 2 * (3 * L + 1))
                transpose_x(("n", 3 * L))
                wait_xT(("n", 3 * L))
                mixers(L)
                pe.wait_ge(xs_ready, 2 * (3 * L + 2))
                transpose_x(("n", 3 * L + 1))
                wait_xT(("n", 3 * L + 1))
                if L == 0:
                    dense()
                    ple(0)

            for t in range(NT):
                o = banks.fill(pe, ("lg", t), 4 + t)
                if t == 0:
                    pe.wait_ge(rt_ready, 1)
                for kt in range(KT):
                    last = product(o[:, 0:NE], at(xTp, ALLP, kt, slice(t * P, t * P + P)),
                                   at((rt_hi, rt_lo), ALLP, kt), kt == 0, kt == KT - 1)
                last.then_inc(banks.is_full(("lg", t)), 1)
            pe.wait_ge(chosen_ready, 1)
            o = banks.fill(pe, ("rank",), 6)
            mm(o[:, 0:NE], tri, chosen[:, 0:NE], start=True, stop=True)
            mm(o[:, NE:2 * NE], tri, chosen[:, NE:2 * NE], start=True, stop=False)
            mm(o[:, NE:2 * NE], ones, chosen[:, 0:NE], start=False, stop=True)
            mm(o[:, 2 * NE:3 * NE], ones, chosen[:, 0:NE], start=True, stop=False)
            mm(o[:, 2 * NE:3 * NE], ones, chosen[:, NE:2 * NE], start=False, stop=True).then_inc(
                banks.is_full(("rank",)), 1)

            for b in range(8):
                pe.wait_ge(banks.free[b], banks.count[b])
            pe.wait_ge(flag_ready, 1)
            n_steps = pe.value_load(flag[0:1, 0:1], min_val=NE, max_val=2 * NE)

            def gather(step):
                pe.wait_ge(sel_ready, step + 1)
                for half in range(2):
                    pe.wait_ge(moe_free[5 + half], step + 1)
                    o = psum[:, 5 + half, :]
                    for q in range(4):
                        kt = 4 * half + q
                        for t in range(NT):
                            last = mm(o[:, q * P:q * P + P], xs[:, t, kt * P:kt * P + P], sel[:, t, :],
                                      start=t == 0, stop=t == NT - 1)
                    last.then_inc(moe_full[5 + half], 1)

            for b in range(8):
                pe.sem_inc(moe_free[b], 1)
            gather(0)
            with pe.Fori(0, n_steps) as e:
                def moe_unit(c, k):
                    pe.wait_ge(lo_ready, e * EXPERT_UNITS + N0 + c + 1)
                    return tuple(part(b, N0 + c).rearrange("p (k n) -> p k n", k=k) for b in (w_hi, w_lo))

                def hidden(cb):
                    pe.wait_ge(moe_free[1], e * NCB + cb + 2)
                    pe.wait_ge(moe_free[2], e * (NCB + 1) + cb + 2)
                    for q in range(4):
                        last = tr(psum[:, 2, q * P:q * P + P], hs[:, cb % 2, q * P:q * P + P], ident)
                    last.then_inc(moe_full[2], 1)

                pe.wait_ge(moe_free[5], e + 2)
                pe.wait_ge(moe_free[6], e + 2)
                for cb in range(NCB):
                    for u in range(2):
                        for i in range(2):
                            w = moe_unit(4 * cb + 2 * u + i, HALF_K)
                            if i == 0:
                                pe.wait_ge(moe_free[u], e * NCB + cb + 1)
                            for q in range(HALF_K):
                                kt = HALF_K * i + q
                                last = product(psum[:, u, :], at((xg_hi, xg_lo), ALLP, kt), at(w, ALLP, q),
                                               kt == 0, kt == KT - 1)
                            last.then_inc(moe_full[u] if i else unit_used, 1)
                        if u == 0 and cb == 0:
                            pe.wait_ge(selg_ready, e + 1)
                            pe.wait_ge(moe_free[2], e * (NCB + 1) + 1)
                            for t in range(NT):
                                last = tr(psum[:, 2, t * P:t * P + P], selg[:, t, :], ident)
                            last.then_inc(moe_full[2], 1)
                        elif u == 0:
                            hidden(cb - 1)
                for half in range(2):
                    pe.wait_ge(moe_free[3 + half], e * 2 + 1)
                for j in range(DOWN_UNITS):
                    w = moe_unit(4 * NCB + j, 2)
                    if j == 1:
                        hidden(NCB - 1)
                    pe.wait_ge(moe_free[2], e * (NCB + 1) + j // 2 + 3)
                    for half in range(2):
                        for q in range(2):
                            kt = 2 * j + q
                            last = product(psum[:, 3 + half, :], at((ehT_hi, ehT_lo), ALLP, kt),
                                           at(w, ALLP, q, slice(half * 512, half * 512 + 512)),
                                           kt == 0, kt == FKT - 1)
                        if j == DOWN_UNITS - 1:
                            last.then_inc(moe_full[3 + half], 1)
                    if j < DOWN_UNITS - 1:
                        last.then_inc(unit_used, 1)
                gather(e + 1)
                pe.wait_ge(moe_free[3], e * 2 + 2)
                pe.wait_ge(moe_free[4], e * 2 + 2)
                for i, (b, n) in enumerate(((7, 0), (3, 1), (4, 1), (7, 1))):
                    t, half = divmod(i, 2)
                    pe.wait_ge(moe_free[b], e * 2 + n + 1)
                    mm(psum[:, b, :], selgT[:, t, :], ysb[:, half * 512:half * 512 + 512],
                       start=True, stop=True).then_inc(moe_full[b], 1)
            for b in range(8):
                extra = 2 if b in (5, 6) else 1
                pe.wait_ge(moe_free[b], n_steps * MOE_FILLS[b] + extra)

            ple_front(1)
            for half in range(2):
                keys, bs = [("pg", 1, half, t) for t in range(NT)], ((4, 5), (0, 1))[half]
                for i in range(2):
                    c = 2 * half + i
                    pe.wait_ge(lo_ready, n_steps * EXPERT_UNITS + N0 + c + 1)
                    w = tuple(part(b, N0 + c).rearrange("p (k n) -> p k n", k=HALF_K) for b in (w_hi, w_lo))
                    for t in range(NT):
                        o = banks.fill(pe, keys[t], bs[t]) if i == 0 else psum[:, bs[t], :]
                        for q in range(HALF_K):
                            kt = HALF_K * i + q
                            last = product(o, at(xTp, ALLP, kt, slice(t * P, t * P + P)), at(w, ALLP, q),
                                           kt == 0, kt == KT - 1)
                        if i:
                            last.then_inc(banks.is_full(keys[t]), 1)
                    if i == 0:
                        last.then_inc(unit_used, 1)
            pe.wait_ge(lo_ready, n_steps * EXPERT_UNITS + N0 + 5)
            ple_projection(1, tuple(part(b, N0 + 4).rearrange("p (k n) -> p k n", k=2) for b in (w_hi, w_lo)))
            used_before_moe.append(used[0])

        def moe_reader(c, e):
            if c < 4 * NCB:
                cb, r = divmod(c, 4)
                if r % 2:
                    return moe_full[r // 2], e * NCB + cb + 1
                return unit_used, e * MOE_USED + used_before_moe[0] + 2 * cb + r // 2 + 1
            j = c - 4 * NCB
            if j < DOWN_UNITS - 1:
                return unit_used, e * MOE_USED + used_before_moe[0] + 2 * NCB + j + 1
            return moe_full[4], e * 2 + 1

        def after_reader(c, n_steps):
            if c % 2:
                b, n = banks.uses[("pg", 1, c // 2, 1)]
                return banks.full[b], n
            return unit_used, n_steps * MOE_USED + used_before_moe[0] + c // 2 + 1

        @block.sync
        def _(sp):
            def load(g, src, k, n):
                sp.dma_start(raw(g, k * n).rearrange("p (k n) -> p k n", k=k), src).then_inc(loaded[g % SLOTS], 16)

            sp.dma_start(h, x[0].rearrange("(t p) d -> p t d", p=P)).then_inc(x_in, 16)
            for g, u in enumerate(before_moe):
                if g >= SLOTS:
                    sp.wait_ge(lo_ready, g - SLOTS + 1)
                load(g, *u)

            def expert(e, weights):
                for c in range(EXPERT_UNITS):
                    sp.wait_ge(lo_ready, e * EXPERT_UNITS + N0 + c - SLOTS + 1)
                    load(N0 + c, *swiglu_unit(*weights, c))

            expert(0, (moe_g[0, 0], moe_u[0, 0], moe_d[0, 0]))
            sp.wait_ge(flag_ready, 1)
            n_steps = sp.value_load(flag[0:1, 0:1], min_val=NE, max_val=2 * NE)
            with sp.Fori(1, n_steps) as e:
                ex = sp.snap(e % NE)

                def pick(w):
                    return w[0, bass.ds(ex, 1)].rearrange("a k n -> (a k) n")
                expert(e, (pick(moe_g), pick(moe_u), pick(moe_d)))
            for c, u in enumerate(after_moe):
                sp.wait_ge(lo_ready, n_steps * EXPERT_UNITS + N0 + c - SLOTS + 1)
                load(N0 + c, *u)
            for t in range(NT):
                sp.wait_ge(out_ready, t + 1)
                sp.dma_start(out[0, t * P:t * P + P, :], xs[:, t, :]).then_inc(out_done, 16)
            sp.wait_ge(out_done, 16 * NT)

        @block.gpsimd
        def _(pool):
            pool.dma_start(par[:, :], params).then_inc(params_in, 16)
            pool.dma_start(pos_i[:, :], positions).then_inc(pos_in, 16)
            for L in range(DEPTH):
                if L:
                    banks.filled(pool, ("kv", L - 1, 1))
                pool.dma_start(wq, w_uq[L].rearrange("(k p) n -> p k n", p=P)).then_inc(wsmall_in, 16)
                pool.dma_start(wkv_b[:, :], w_ukv[L]).then_inc(wsmall_in, 16)
                if L == 0:
                    pool.dma_start(rt_v, router[0].rearrange("(k p) n -> p k n", p=P)).then_inc(wsmall_in, 16)
                pool.wait_ge(*banks.taken(("o", L, 1, 1)))
                pool.dma_start(ptok, p[L, 0].rearrange("(t p) c -> p t c", p=P)).then_inc(ptok_in, 16)
            pool.wait_ge(*banks.taken(("pT", DEPTH - 1)))
            pool.dma_start(gfin, final_g.rearrange("(a n) -> a n", a=1).to_broadcast([P, D])).then_inc(gfin_in, 16)

        @block.scalar
        def _(act):
            A = nc.scalar.activation

            def split(g, e=0, wait=None):
                act.wait_ge(loaded[g % SLOTS], landed(g, e))
                if wait is not None:
                    act.wait_ge(*wait)
                elif g >= SPLITS:
                    act.wait_ge(*last_reader[g - SPLITS])
                A(part(w_hi, g, sizes[g]), raw(g, sizes[g]), ACT.Copy).then_inc(hi_ready, 1)
            def norm(k, h_done):
                act.wait_ge(*h_done)
                for t in range(NT):
                    A(xs[:, t, :], h[:, t, :], ACT.Square, accum_out=ss[:, t:t + 1]).then_inc(sumsq, 1)
                act.wait_ge(ms_ready, k + 1)
                A(rms, ms, ACT.Sqrt).then_inc(rms_ready, 1)

            def take_xT(k, L, gain):
                for b in range(4):
                    o = banks.filled(act, (("n", k), b))
                    for q in range(2):
                        kt = 2 * b + q
                        last = A(xT_hi[:, kt, :], o[:, q * SEQ:q * SEQ + SEQ], ACT.Copy, scale=lp(L, gain, kt))
                    last.then_inc(x_hi_ready, 1)

            def mixers(L):
                f = L * (N0 - NF)
                split(f + 3)
                o = banks.filled(act, ("conv", L, 1))
                A(csq.rearrange("p m s -> p (m s)"), o, ACT.Sigmoid).then_inc(banks.is_free(("conv", L, 1)), 1)
                split(f + 4)
                act.wait_ge(pads_ready, L + 1)
                for j in range(4):
                    split(f + 5 + j)
                    o = banks.filled(act, ("xbc", L, j))
                    A(xpad[:, 2 * j:2 * j + 2, SCONV - 1:], o.rearrange("p (m s) -> p m s", m=2), ACT.Copy).then_inc(
                        banks.is_free(("xbc", L, j)), 1)
                split(f + 9)
                split(f + 10)
                for t in range(NT):
                    o = banks.filled(act, ("sm", L, t))
                    A(sm[:, t, :], o[:, 0:SMW], ACT.Copy).then_inc(banks.is_free(("sm", L, t)), 1)
                    act.wait_ge(*banks.taken(("sm", L, t)))
                    A(sq_junk(QRANK), sm[:, t, S_CQ:S_CQ + QRANK], ACT.Square, accum_out=lss[:, t:t + 1]).then_inc(lss_ready, 1)
                    act.wait_ge(lss_ready, 4 * L + 2 * t + 1)
                    A(sq_junk(KVRANK), sm[:, t, S_CKV:S_CKV + KVRANK], ACT.Square,
                      accum_out=lss[:, 2 + t:3 + t]).then_inc(lss_ready, 1)
                    act.wait_ge(lss_ready, 4 * L + 2 * t + 2)
                act.wait_ge(lms_ready, L + 1)
                A(lrm, lms, ACT.Sqrt).then_inc(lrm_ready, 1)
                act.wait_ge(dtn_ready, L + 1)
                A(dte, dtn, ACT.Exp).then_inc(dte_ready, 1)
                A(nega, lp(L, "alog", 0, SH), ACT.Exp).then_inc(nega_ready, 1)
                act.wait_ge(dtu_ready, L + 1)
                A(dtl, dtu, ACT.Ln).then_inc(dtl_ready, 1)
                for m in range(XT):
                    act.wait_ge(xtap_ready, XT * L + m + 1)
                    A(xbcT[:, m, :], xbcT[:, m, :], ACT.Silu, bias=lp(L, "sb", m)).then_inc(xbc_ready, 1)
                for t in range(NT):
                    o = banks.filled(act, ("z", L, t))
                    A(z[:, t, :], o, ACT.Silu).then_inc(banks.is_free(("z", L, t)), 1)
                split(f + 11)
                split(f + 12)
                o = banks.filled(act, ("cqT", L))
                for k in range(2):
                    last = A(cqT[:, k, :], o[:, k * SEQ:k * SEQ + SEQ], ACT.Copy, scale=lp(L, "qg", k))
                last.then_inc(banks.is_free(("cqT", L)), 1)
                o = banks.filled(act, ("ckvT", L))
                A(ckvT, o[:, 0:SEQ], ACT.Copy, scale=lp(L, "kvg")).then_inc(banks.is_free(("ckvT", L)), 1)
                for t in range(NT):
                    o = banks.filled(act, ("q", L, t))
                    A(qf[:, t, :, :], o[:, 0:MH * QD].rearrange("p (h d) -> p h d", h=MH), ACT.Copy).then_inc(
                        banks.is_free(("q", L, t)), 1)
                for t in range(NT):
                    o = banks.filled(act, ("kv", L, t)).rearrange("p (h d) -> p h d", h=MH)
                    A(kf[:, t, :, 0:NOPE], o[:, :, 0:NOPE], ACT.Copy)
                    A(vs[:, t, :, :], o[:, :, NOPE:], ACT.Copy).then_inc(banks.is_free(("kv", L, t)), 1)
                o = banks.filled(act, ("btok", L))
                A(btok.rearrange("p g n -> p (g n)"), o[:, 0:SG * SN], ACT.Copy).then_inc(
                    banks.is_free(("btok", L)), 1)
                for name, buf in (("qT", qT), ("kT", kT)):
                    for t in range(NT):
                        o = banks.filled(act, (name, L, t))
                        A(buf[0:QD, :, t * P:t * P + P], o[0:QD, :].rearrange("p (h s) -> p h s", h=MH),
                          ACT.Copy).then_inc(banks.is_free((name, L, t)), 1)
                act.wait_ge(acsd_ready, L + 1)
                A(dst, dst, ACT.Exp)
                A(ea, acs[:, SH:2 * SH], ACT.Exp).then_inc(ea_ready, 1)
                for t in range(NT):
                    for g in range(SG):
                        act.wait_ge(*banks.taken(("seg", L, t, g)))
                        v = dec[:, t, 4 * g:4 * g + 4, :].rearrange("p h l -> p (h l)")
                        A(v, v, ACT.Exp).then_inc(dec_ready, 1)
                for t in range(NT):
                    act.wait_ge(score_ready, 2 * L + t + 1)
                    for hd in range(MH):
                        i = t * MH + hd
                        A(sc[t][:, hd, :], sc[t][:, hd, :], ACT.Exp, bias=nm[:, i:i + 1],
                          accum_out=den[:, i:i + 1]).then_inc(prob_ready, 1)
                act.wait_ge(*banks.taken(("mean", L)))
                A(csq.rearrange("p m s -> p (m s)"), cacc.rearrange("p m s -> p (m s)"), ACT.Square).then_inc(
                    csq_ready, 1)
                o = banks.filled(act, ("st", L))
                A(st, o, ACT.Copy).then_inc(banks.is_free(("st", L)), 1)
                act.wait_ge(*banks.taken(("var", L)))
                c2 = csq.rearrange("p m s -> p (m s)")
                A(c2, c2, ACT.Sqrt).then_inc(crms_ready, 1)
                for j in range(3):
                    o = banks.filled(act, ("prT", L, j))
                    A(prT_f[:, j * 512:(j + 1) * 512], o, ACT.Copy).then_inc(banks.is_free(("prT", L, j)), 1)
                act.wait_ge(chn_ready, L + 1)
                for m in range(2):
                    last = A(csq[:, m, :], cacc[:, m, :], ACT.Silu, scale=lp(L, "lng", m), bias=lp(L, "lnb", m))
                last.then_inc(conv_hi_ready, 1)
                act.wait_ge(conv_hi_ready, 2 * L + 1)
                A(yT_hi[:, 0:2, :], csq, ACT.Copy).then_inc(conv_hi_ready, 1)
                act.wait_ge(ygz_ready, L + 1)
                for t in range(NT):
                    for g in range(SG):
                        A(dx[:, t, g * SEQ:g * SEQ + SEQ], ytok[:, t, g * SEQ:g * SEQ + SEQ], ACT.Square,
                          accum_out=gss[:, 2 * t + g:2 * t + g + 1]).then_inc(gss_ready, 1)
                act.wait_ge(gms_ready, L + 1)
                A(grm, gms, ACT.Sqrt).then_inc(grm_ready, 1)
                for j in range(3):
                    o = banks.filled(act, ("yT", L, j))
                    for q in range(2):
                        m = 2 * j + q
                        last = A(yT_hi[:, 2 + m, :], o[:, q * SEQ:q * SEQ + SEQ], ACT.Copy,
                                 scale=lp(L, "sng", m) if j < 2 else 1.0)
                    last.then_inc(y_hi_ready, 1)
                for i in range(13, 17):
                    split(f + i)

            def sq_junk(n):
                return xd.rearrange("p t c -> p (t c)")[:, 0:n]

            act.wait_ge(trig_arg, 1)
            A(sin_t, tr0, ACT.Sin)
            A(cos_t, tr1, ACT.Sin).then_inc(trig_ready, 1)
            for g in range(SPLITS):
                split(g)
            for L in range(DEPTH):
                f = NF + L * (N0 - NF)
                norm(3 * L, (h_ready, L) if L else (x_in, 16))
                take_xT(3 * L, L, "g_attn")
                mixers(L)
                norm(3 * L + 1, banks.taken(("o", L, 1, 1)))
                take_xT(3 * L + 1, L, "g_ffn")
                if L == 0:
                    h_done = banks.taken(("d", 1, 1))
                    for c in range(EXPERT_UNITS):
                        cb = c // 4
                        if c < 4 * NCB and c % 4 == 1:
                            for t in range(NT):
                                o = banks.filled(act, ("g", cb, t))
                                if cb:
                                    act.wait_ge(*banks.taken(("u", cb - 1, t)))
                                A(dsg[:, t, :], o, ACT.Silu).then_inc(banks.is_free(("g", cb, t)), 1)
                        split(f + c + SPLITS)
                        if (4 < c < 4 * NCB and c % 4 == 1) or c == 4 * NCB:
                            for t in range(NT):
                                o = banks.filled(act, ("hT", cb - 1, t))
                                A(hT_hi[:, 4 * cb - 4:4 * cb, t * P:t * P + P],
                                  o.rearrange("p (k s) -> p k s", k=4), ACT.Copy).then_inc(h_hi_ready, 1)
                else:
                    act.wait_ge(dv_ready, 1)
                    A(ev, dv, ACT.Exp).then_inc(ev_ready, 1)
                    act.wait_ge(flag_ready, 1)
                    n_steps = act.value_load(flag[0:1, 0:1], min_val=NE, max_val=2 * NE)

                    def take_xg(stepno):
                        for half in range(2):
                            act.wait_ge(moe_full[5 + half], stepno + 1)
                            for q in range(4):
                                kt = 4 * half + q
                                last = A(xg_hi[:, kt, :], psum[:, 5 + half, q * P:q * P + P], ACT.Copy,
                                         scale=lp(1, "g_ffn", kt))
                            last.then_inc(moe_x_hi, 1)

                    take_xg(0)
                    with act.Fori(0, n_steps) as e:
                        for c in range(EXPERT_UNITS):
                            cb = c // 4
                            if c < 4 * NCB and c % 4 == 1:
                                act.wait_ge(moe_full[0], e * NCB + cb + 1)
                                A(sg[:, cb % 2, :], psum[:, 0, :], ACT.Silu).then_inc(moe_free[0], 1)
                            split(N0 + c + SPLITS, e, moe_reader(c, e))
                            if c == 1:
                                act.wait_ge(moe_full[2], e * (NCB + 1) + 1)
                                A(selgT.rearrange("p t s -> p (t s)"), psum[:, 2, 0:NT * P], ACT.Copy).then_inc(
                                    moe_free[2], 1)
                            elif (c < 4 * NCB and c % 4 == 1) or c == 4 * NCB:
                                act.wait_ge(moe_full[2], e * (NCB + 1) + cb + 1)
                                A(ehT_hi[:, 4 * cb - 4:4 * cb, :], psum[:, 2, :].rearrange("p (k s) -> p k s", k=4),
                                  ACT.Copy).then_inc(moe_h_hi, 1)
                        for half in range(2):
                            act.wait_ge(moe_full[3 + half], e * 2 + 1)
                            A(ysb[:, half * 512:half * 512 + 512], psum[:, 3 + half, :], ACT.Copy).then_inc(
                                moe_free[3 + half], 1)
                        take_xg(e + 1)
                    h_done = (moe_free[7], n_steps * MOE_FILLS[7] + 1)
                o = banks.filled(act, ("pT", L))
                A(pT_hi, o.rearrange("p (k s) -> p k s", k=2), ACT.Copy).then_inc(p_hi_ready, 1)
                norm(3 * L + 2, h_done)
                take_xT(3 * L + 2, L, "g_ple")

                def gates(half):
                    for t in range(NT):
                        o = banks.filled(act, ("pg", L, half, t))
                        buf = sg if half == 0 else hs
                        A(buf[:, t, :], o, ACT.Sigmoid).then_inc(banks.is_free(("pg", L, half, t)), 1)

                f = NF + EXPERT_UNITS
                if L == 0:
                    split(f + 3)
                    gates(0)
                    split(f + 4)
                    split(f + 5)
                    gates(1)
                    split(f + 6)
                    split(f + 7)
                else:
                    split(N0 + 3, n_steps, after_reader(0, n_steps))
                    gates(0)
                    split(N0 + 4, n_steps, after_reader(1, n_steps))
                    gates(1)
            norm(3 * DEPTH, (h_ready, DEPTH))

        @block.vector
        def _(dve):
            V = nc.vector
            steps = [0]

            def step(ins):
                steps[0] += 1
                ins.then_inc(dve_step, 1)
                dve.wait_ge(dve_step, steps[0])

            def norm(k):
                dve.wait_ge(sumsq, NT * (k + 1))
                V.tensor_scalar(ms, ss, 1.0 / D, RMS_EPS, ALU.mult, ALU.add).then_inc(ms_ready, 1)
                dve.wait_ge(rms_ready, k + 1)
                step(V.reciprocal(rstd, rms))
                for t in range(NT):
                    V.tensor_scalar(xs[:, t, :], h[:, t, :], rstd[:, t:t + 1], None, ALU.mult).then_inc(xs_ready, 1)

            def f32(v):
                return v.bitcast(F32)

            def split(g, e=0):
                dve.wait_ge(hi_ready, e * EXPERT_UNITS + g + 1)
                V.tensor_tensor(part(w_lo, g, sizes[g]), raw(g, sizes[g]), f32(part(w_hi, g, sizes[g])),
                                ALU.subtract).then_inc(lo_ready, 1)

            def rest(lo, exact, hi, gain=None):
                if gain is None:
                    return V.tensor_tensor(lo, exact, f32(hi), ALU.subtract)
                return V.scalar_tensor_tensor(out=lo, in0=exact, scalar=gain, in1=f32(hi), op0=ALU.mult,
                                              op1=ALU.subtract)

            def take_xT(k, L, gain):
                for b in range(4):
                    dve.wait_ge(x_hi_ready, 4 * k + b + 1)
                    o = banks.filled(dve, (("n", k), b))
                    for q in range(2):
                        kt = 2 * b + q
                        last = rest(xT_lo[:, kt, :], o[:, q * SEQ:q * SEQ + SEQ], xT_hi[:, kt, :], lp(L, gain, kt))
                    last.then_inc(banks.is_free((("n", k), b)), 1)

            def bc(v, n):
                return v.unsqueeze(len(v.shape)).to_broadcast(list(v.shape) + [n])

            def heads(v, n=SH):
                return v.rearrange("p (h d) -> p h d", h=n)

            def rotate(x1, x2, c, s, t1, t2, t3, t4):
                V.tensor_tensor(t1, x1, c, ALU.mult)
                V.tensor_tensor(t2, x2, s, ALU.mult)
                V.tensor_tensor(t3, x1, s, ALU.mult)
                step(V.tensor_tensor(t4, x2, c, ALU.mult))
                V.tensor_tensor(x1, t1, t2, ALU.subtract)
                return V.tensor_tensor(x2, t3, t4, ALU.add)

            def mixers(L):
                V.memset(cpad[:, :, 0:CK - 1], 0.0)
                V.memset(xpad[:, :, 0:SCONV - 1], 0.0).then_inc(pads_ready, 1)
                dve.wait_ge(pads_ready, L + 1)
                f = L * (N0 - NF)
                split(f + 3)
                dve.wait_ge(*banks.taken(("conv", L, 1)))
                o = banks.filled(dve, ("conv", L, 0))
                V.tensor_tensor(cpad[:, :, CK - 1:], o.rearrange("p (m s) -> p m s", m=2),
                                csq, ALU.mult).then_inc(banks.is_free(("conv", L, 0)), 1)
                dve.wait_ge(*banks.taken(("conv", L, 0)))

                def conv_taps(j0, j1):
                    for j in range(j0, j1):
                        for m in range(2):
                            src, w = cpad[:, m, j:j + SEQ], lp(L, "cw", m * CK + j)
                            if j == 0:
                                ins = V.tensor_scalar(cacc[:, m, :], src, w, lp(L, "cb", m), ALU.mult, ALU.add)
                            else:
                                ins = V.scalar_tensor_tensor(out=cacc[:, m, :], in0=src, scalar=w,
                                                             in1=cacc[:, m, :], op0=ALU.mult, op1=ALU.add)
                            if j == CK - 1 and m == 1:
                                ins.then_inc(conv_ready, 1)
                            elif m == 1:
                                step(ins)

                split(f + 4)
                conv_taps(0, 2)
                for j in range(4):
                    split(f + 5 + j)
                    dve.wait_ge(*banks.taken(("xbc", L, j)))
                    for i in range(SCONV):
                        for m in (2 * j, 2 * j + 1):
                            src, w = xpad[:, m, i:i + SEQ], lp(L, "sw", m * SCONV + i)
                            if i == 0:
                                ins = V.tensor_scalar(xbcT[:, m, :], src, w, None, ALU.mult)
                            else:
                                ins = V.scalar_tensor_tensor(out=xbcT[:, m, :], in0=src, scalar=w,
                                                             in1=xbcT[:, m, :], op0=ALU.mult, op1=ALU.add)
                            if i == SCONV - 1:
                                ins.then_inc(xtap_ready, 1)
                            elif m % 2:
                                step(ins)
                split(f + 9)
                split(f + 10)
                dve.wait_ge(lss_ready, 4 * (L + 1))
                V.tensor_scalar(lms[:, 0:2], lss[:, 0:2], 1.0 / QRANK, RMS_EPS, ALU.mult, ALU.add)
                V.tensor_scalar(lms[:, 2:4], lss[:, 2:4], 1.0 / KVRANK, RMS_EPS, ALU.mult, ALU.add).then_inc(
                    lms_ready, 1)
                for t in range(NT):
                    ins = V.tensor_tensor(dtx[:, t * SH:t * SH + SH], sm[:, t, 0:SH], lp(L, "dtb", 0, SH), ALU.add)
                step(ins)
                V.scalar_tensor_tensor(out=dtn, in0=dtx, scalar=-1.0, in1=dtx, op0=ALU.mult, op1=ALU.min).then_inc(
                    dtn_ready, 1)
                dve.wait_ge(dte_ready, L + 1)
                V.tensor_scalar(dtu, dte, 1.0, None, ALU.add).then_inc(dtu_ready, 1)
                dve.wait_ge(lrm_ready, L + 1)
                step(V.reciprocal(lrs, lrm))
                for t in range(NT):
                    V.tensor_scalar(sm[:, t, S_CQ:S_CQ + QRANK], sm[:, t, S_CQ:S_CQ + QRANK], lrs[:, t:t + 1],
                                    None, ALU.mult)
                    last = V.tensor_scalar(sm[:, t, S_CKV:S_CKV + KVRANK], sm[:, t, S_CKV:S_CKV + KVRANK],
                                           lrs[:, 2 + t:3 + t], None, ALU.mult)
                last.then_inc(cn_ready, 1)
                step(V.scalar_tensor_tensor(out=dtc, in0=dtu, scalar=-1.0, in1=dte, op0=ALU.add, op1=ALU.subtract))
                step(V.reciprocal(dtn, dtu))
                step(V.tensor_tensor(dtc, dtc, dtn, ALU.mult))
                dve.wait_ge(dtl_ready, L + 1)
                step(V.tensor_tensor(dtc, dtl, dtc, ALU.subtract))
                step(V.scalar_tensor_tensor(out=dt, in0=dtx, scalar=0.0, in1=dtc, op0=ALU.max, op1=ALU.add))
                dve.wait_ge(nega_ready, L + 1)
                for t in range(NT):
                    last = V.scalar_tensor_tensor(out=adt[:, t * SH:t * SH + SH], in0=dt[:, t * SH:t * SH + SH],
                                                  scalar=-1.0, in1=nega, op0=ALU.mult, op1=ALU.mult)
                last.then_inc(adt_ready, 1)
                dve.wait_ge(adt_ready, L + 1)
                dve.wait_ge(xtap_ready, XT * (L + 1))
                for t in range(NT):
                    for g in range(SG):
                        for hd in range(4 * g, 4 * g + 4):
                            last = V.tensor_scalar(dec[:, t, hd, :], tri, adt[:, t * SH + hd:t * SH + hd + 1], None,
                                                   ALU.mult)
                        last.then_inc(triadt_ready, 1)
                split(f + 11)
                split(f + 12)
                conv_taps(2, CK)
                if L == 0:
                    dve.wait_ge(trig_ready, 1)
                c3 = cos_t.rearrange("p (t r) -> p t r", t=NT)
                s3 = sin_t.rearrange("p (t r) -> p t r", t=NT)
                tmp = [ctmp[:, i * NT * HR:(i + 1) * NT * HR].rearrange("p (t r) -> p t r", t=NT) for i in range(4)]
                step(rotate(sm[:, :, S_KR:S_KR + HR], sm[:, :, S_KR + HR:S_KR + ROPE], c3, s3, *tmp))
                for t in range(NT):
                    for hd in range(MH):
                        V.tensor_copy(kf[:, t, hd, NOPE:], sm[:, t, S_KR:S_KR + ROPE])
                for t in range(NT):
                    dve.wait_ge(*banks.taken(("q", L, t)))
                    ct = c3[:, t:t + 1, :].to_broadcast([P, MH, HR])
                    s_ = s3[:, t:t + 1, :].to_broadcast([P, MH, HR])
                    tmp = [xdd[:, i * MH * HR:(i + 1) * MH * HR].rearrange("p (h r) -> p h r", h=MH)
                           for i in range(4)]
                    last = rotate(qf[:, t, :, NOPE:NOPE + HR], qf[:, t, :, NOPE + HR:], ct, s_, *tmp)
                    if t < NT - 1:
                        step(last)
                last.then_inc(qk_ready, 1)
                for t in range(NT):
                    o = banks.filled(dve, ("xtok", L, t))
                    V.tensor_tensor(heads(xd[:, t, :]), heads(o), bc(dt[:, t * SH:t * SH + SH], SHD), ALU.mult)
                    V.tensor_tensor(heads(dx[:, t, :]), heads(o), bc(lp(L, "dskip", 0, SH), SHD),
                                    ALU.mult).then_inc(banks.is_free(("xtok", L, t)), 1)
                    dve.wait_ge(*banks.taken(("xtok", L, t)))
                o = banks.filled(dve, ("acs", L))
                V.tensor_copy(acs, o[:, 0:3 * SH]).then_inc(banks.is_free(("acs", L)), 1)
                dve.wait_ge(*banks.taken(("acs", L)))
                V.tensor_tensor(dst, acs[:, 2 * SH:], acs[:, 0:SH], ALU.subtract).then_inc(acsd_ready, 1)
                o = banks.filled(dve, ("cb", L))
                V.tensor_tensor(cbm.rearrange("p t g l -> p (t g) l"), o.rearrange("p (a l) -> p a l", l=P),
                                tri.unsqueeze(1).to_broadcast([P, NT * SG, P]), ALU.mult).then_inc(
                                    banks.is_free(("cb", L)), 1)
                for t in range(NT):
                    for g in range(SG):
                        o = banks.filled(dve, ("seg", L, t, g))
                        for i in range(4):
                            hd = 4 * g + i
                            c = t * SH + hd
                            last = V.tensor_scalar(dec[:, t, hd, :], o[:, i * P:i * P + P], acs[:, c:c + 1], 0.0,
                                                   ALU.subtract, ALU.min)
                        last.then_inc(banks.is_free(("seg", L, t, g)), 1)
                dve.wait_ge(ea_ready, L + 1)
                V.tensor_tensor(heads(xdd), heads(xd[:, 0, :]), bc(dst, SHD), ALU.mult).then_inc(xdd_ready, 1)
                scale = float(QD) ** -0.5
                o = banks.filled(dve, ("sc", L, 0))
                step(V.scalar_tensor_tensor(out=sc[0], in0=heads(o, MH), scalar=scale,
                                            in1=mask[:, P:].unsqueeze(1).to_broadcast([P, MH, P]),
                                            op0=ALU.mult, op1=ALU.add))
                V.tensor_reduce(rden[:, 0:4], sc[0], AX.X, ALU.max).then_inc(banks.is_free(("sc", L, 0)), 1)
                dve.wait_ge(*banks.taken(("sc", L, 0)))
                V.tensor_scalar(nm[:, 0:4], rden[:, 0:4], -1.0, None, ALU.mult).then_inc(score_ready, 1)
                for j in range(2):
                    o = banks.filled(dve, ("sc", L, 1 + j))
                    v = sc[1][:, 2 * j:2 * j + 2, :]
                    step(V.scalar_tensor_tensor(out=v, in0=heads(o, 2), scalar=scale,
                                                in1=mask.unsqueeze(1).to_broadcast([P, 2, SEQ]),
                                                op0=ALU.mult, op1=ALU.add))
                    V.tensor_reduce(rden[:, 4 + 2 * j:6 + 2 * j], v, AX.X, ALU.max).then_inc(
                        banks.is_free(("sc", L, 1 + j)), 1)
                    dve.wait_ge(*banks.taken(("sc", L, 1 + j)))
                V.tensor_scalar(nm[:, 4:8], rden[:, 4:8], -1.0, None, ALU.mult).then_inc(score_ready, 1)
                o = banks.filled(dve, ("mean", L))
                c2 = cacc.rearrange("p m s -> p (m s)")
                q2 = csq.rearrange("p m s -> p (m s)")
                V.tensor_tensor(c2, c2, o, ALU.subtract).then_inc(banks.is_free(("mean", L)), 1)
                for t in range(NT):
                    for g in range(SG):
                        dve.wait_ge(dec_ready, 4 * L + 2 * t + g + 1)
                        v = dec[:, t, 4 * g:4 * g + 4, :]
                        V.tensor_tensor(v, v, cbm[:, t, g:g + 1, :].to_broadcast([P, 4, P]), ALU.mult).then_inc(
                            mix_ready, 1)
                o = banks.filled(dve, ("var", L))
                V.tensor_scalar(q2, o, LN_EPS, None, ALU.add).then_inc(banks.is_free(("var", L)), 1)
                dve.wait_ge(crms_ready, L + 1)
                step(V.reciprocal(q2, q2))
                V.tensor_tensor(c2, c2, q2, ALU.mult).then_inc(chn_ready, 1)
                o0 = banks.filled(dve, ("yd", L, 0))
                V.tensor_tensor(ytok[:, 0, 0:SSDW], o0, dx[:, 0, :], ALU.add).then_inc(banks.is_free(("yd", L, 0)), 1)
                o1_ = banks.filled(dve, ("yd", L, 1))
                V.tensor_tensor(ytok[:, 1, 0:SSDW], o1_, dx[:, 1, :], ALU.add).then_inc(banks.is_free(("yd", L, 1)), 1)
                oo = banks.filled(dve, ("yo", L))
                V.tensor_tensor(heads(xdd), heads(oo), bc(ea, SHD), ALU.mult).then_inc(banks.is_free(("yo", L)), 1)
                dve.wait_ge(*banks.taken(("yo", L)))
                step(V.tensor_tensor(ytok[:, 1, 0:SSDW], ytok[:, 1, 0:SSDW], xdd, ALU.add))
                for t in range(NT):
                    dve.wait_ge(*banks.taken(("z", L, t)))
                V.tensor_tensor(ytok[:, :, 0:SSDW], ytok[:, :, 0:SSDW], z, ALU.mult).then_inc(ygz_ready, 1)
                dve.wait_ge(prob_ready, 8 * (L + 1))
                step(V.reciprocal(rden, den))
                o = banks.filled(dve, ("pv", L))
                for t in range(NT):
                    last = V.tensor_tensor(heads(ytok[:, t, SSDW:], MH), heads(o[:, t * 256:t * 256 + 256], MH),
                                           bc(rden[:, 4 * t:4 * t + 4], VD), ALU.mult)
                last.then_inc(banks.is_free(("pv", L)), 1)
                dve.wait_ge(gss_ready, 4 * (L + 1))
                V.tensor_scalar(gms, gss, SG / SSDW, RMS_EPS, ALU.mult, ALU.add).then_inc(gms_ready, 1)
                dve.wait_ge(grm_ready, L + 1)
                step(V.reciprocal(grs, grm))
                for t in range(NT):
                    for g in range(SG):
                        v = ytok[:, t, g * SEQ:g * SEQ + SEQ]
                        last = V.tensor_scalar(v, v, grs[:, 2 * t + g:2 * t + g + 1], None, ALU.mult)
                last.then_inc(ytok_ready, 1)
                dve.wait_ge(conv_hi_ready, 2 * L + 2)
                rest(yT_lo[:, 0:2, :], csq, yT_hi[:, 0:2, :]).then_inc(yT_ready, 1)
                for j in range(3):
                    dve.wait_ge(y_hi_ready, 3 * L + j + 1)
                    o = banks.filled(dve, ("yT", L, j))
                    for q in range(2):
                        m = 2 * j + q
                        last = rest(yT_lo[:, 2 + m, :], o[:, q * SEQ:q * SEQ + SEQ], yT_hi[:, 2 + m, :],
                                    lp(L, "sng", m) if j < 2 else None)
                    last.then_inc(banks.is_free(("yT", L, j)), 1)
                split(f + 13)
                for half in range(2):
                    split(f + 14 + 2 * half)
                    if half == 0:
                        split(f + 15)
                    for t in range(NT):
                        o = banks.filled(dve, ("o", L, half, t))
                        v = h[:, t, half * 512:half * 512 + 512]
                        V.tensor_tensor(v, v, o, ALU.add).then_inc(banks.is_free(("o", L, half, t)), 1)

            def embed(L, n_steps):
                f = NF + EXPERT_UNITS
                if L == 0:
                    for i in range(3, 7):
                        split(f + i)
                else:
                    for i in range(3, 5):
                        split(N0 + i, n_steps)
                for half in range(2):
                    buf = sg if half == 0 else hs
                    for t in range(NT):
                        dve.wait_ge(*banks.taken(("pg", L, half, t)))
                        o = banks.filled(dve, ("pp", L, half, t))
                        V.tensor_tensor(buf[:, t, :], o, buf[:, t, :], ALU.mult).then_inc(
                            banks.is_free(("pp", L, half, t)), 1)
                        dve.wait_ge(*banks.taken(("pp", L, half, t)))
                        v = h[:, t, half * 512:half * 512 + 512]
                        last = V.tensor_tensor(v, v, buf[:, t, :], ALU.add)
                last.then_inc(h_ready, 1)
                if L == 0:
                    split(f + 7)

            def experts():
                for t in range(NT):
                    o = banks.filled(dve, ("lg", t))
                    V.tensor_copy(logits[:, t * NE:t * NE + NE], o[:, 0:NE]).then_inc(banks.is_free(("lg", t)), 1)
                    dve.wait_ge(*banks.taken(("lg", t)))
                    lt, tt = logits[:, t * NE:t * NE + NE], top[:, t * 8:t * 8 + 8]
                    step(V.max(out=tt, in_=lt))
                    step(V.max_index(out=tinyi[:, t * 8:t * 8 + 8], in_max=tt, in_values=lt))
                    V.tensor_copy(topi[:, 2 * t:2 * t + 2], tinyi[:, t * 8:t * 8 + 2])
                    step(V.tensor_tensor(dv[:, t:t + 1], tt[:, 1:2], tt[:, 0:1], ALU.subtract))
                V.tensor_copy(g2, dv).then_inc(dv_ready, 1)
                dve.wait_ge(ev_ready, 1)
                step(V.tensor_scalar(g1, ev, 1.0, None, ALU.add))
                step(V.reciprocal(g1, g1))
                step(V.tensor_tensor(g2, ev, g1, ALU.mult))
                for t in range(NT):
                    c = slice(t * NE, t * NE + NE)
                    V.tensor_scalar(o1[:, c], iota[:, 0:NE], topi[:, 2 * t:2 * t + 1], None, ALU.is_equal)
                    step(V.tensor_scalar(o2[:, c], iota[:, 0:NE], topi[:, 2 * t + 1:2 * t + 2], None, ALU.is_equal))
                V.tensor_tensor(chosen, o1, o2, ALU.add).then_inc(chosen_ready, 1)
                for t in range(NT):
                    c = slice(t * NE, t * NE + NE)
                    step(V.tensor_scalar(gate_of[:, t, 0:NE], o1[:, c], g1[:, t:t + 1], None, ALU.mult))
                    step(V.scalar_tensor_tensor(out=gate_of[:, t, 0:NE], in0=o2[:, c], scalar=g2[:, t:t + 1],
                                                in1=gate_of[:, t, 0:NE], op0=ALU.mult, op1=ALU.add))
                    V.tensor_copy(gate_of[:, t, NE:2 * NE], gate_of[:, t, 0:NE])
                V.memset(slot_of[:, :, STEPS:], -1.0)
                step(V.memset(gate_of[:, :, STEPS:], 0.0))
                o = banks.filled(dve, ("rank",))
                V.tensor_copy(cnt, o[:, 2 * NE:3 * NE])
                V.tensor_tensor(rank, o[:, 0:NT * NE], chosen, ALU.mult).then_inc(banks.is_free(("rank",)), 1)
                dve.wait_ge(*banks.taken(("rank",)))
                r3 = rank.rearrange("p (t e) -> p t e", t=NT)
                V.tensor_scalar(slot_of[:, :, 0:NE], r3, -1.0, None, ALU.add)
                V.tensor_scalar(slot_of[:, :, NE:2 * NE], r3, -1.0 - P, None, ALU.add)
                step(V.tensor_reduce(mx, cnt, AX.X, ALU.max))
                step(V.tensor_scalar(mx, mx, P + 0.5, float(NE), ALU.is_gt, ALU.mult))
                V.tensor_scalar(flag[:, :], mx, float(NE), None, ALU.add).then_inc(flag_ready, 1)
                dve.wait_ge(flag_ready, 1)
                n_steps = dve.value_load(flag[0:1, 0:1], min_val=NE, max_val=2 * NE)

                def build_sel(stepno):
                    for t in range(NT):
                        col = slot_of[:, t, bass.ds(stepno, 1)] if not isinstance(stepno, int) else slot_of[:, t, 0:1]
                        last = V.tensor_scalar(sel[:, t, :], iota, col, None, ALU.is_equal)
                    last.then_inc(sel_ready, 1)

                def take_xg(stepno):
                    for half in range(2):
                        dve.wait_ge(moe_x_hi, stepno * 2 + half + 1)
                        for q in range(4):
                            kt = 4 * half + q
                            last = rest(xg_lo[:, kt, :], psum[:, 5 + half, q * P:q * P + P], xg_hi[:, kt, :],
                                        lp(1, "g_ffn", kt))
                        last.then_inc(moe_free[5 + half], 1)

                build_sel(0)
                take_xg(0)
                with dve.Fori(0, n_steps) as e:
                    for c in range(EXPERT_UNITS):
                        cb = c // 4
                        split(N0 + c + SPLITS, e)
                        if c == 0:
                            for t in range(NT):
                                last = V.tensor_scalar(selg[:, t, :], iota, slot_of[:, t, bass.ds(e, 1)],
                                                       gate_of[:, t, bass.ds(e, 1)], ALU.is_equal, ALU.mult)
                            last.then_inc(selg_ready, 1)
                            dve.wait_ge(moe_full[6], e + 1)
                            build_sel(e + 1)
                        if c < 4 * NCB and c % 4 == 3:
                            dve.wait_ge(moe_free[0], e * NCB + cb + 2)
                            dve.wait_ge(moe_full[1], e * NCB + cb + 1)
                            V.tensor_tensor(hs[:, cb % 2, :], psum[:, 1, :], sg[:, cb % 2, :], ALU.mult).then_inc(
                                moe_free[1], 1)
                        if (4 < c < 4 * NCB and c % 4 == 1) or c == 4 * NCB:
                            dve.wait_ge(moe_h_hi, e * NCB + cb)
                            rest(ehT_lo[:, 4 * cb - 4:4 * cb, :], psum[:, 2, :].rearrange("p (k s) -> p k s", k=4),
                                 ehT_hi[:, 4 * cb - 4:4 * cb, :]).then_inc(moe_free[2], 1)
                    take_xg(e + 1)
                    for i, (b, n) in enumerate(((7, 1), (3, 2), (4, 2), (7, 2))):
                        t, half = divmod(i, 2)
                        dve.wait_ge(moe_full[b], e * 2 + n)
                        v = h[:, t, half * 512:half * 512 + 512]
                        V.tensor_tensor(v, v, psum[:, b, :], ALU.add).then_inc(moe_free[b], 1)
                dve.wait_ge(moe_free[7], n_steps * MOE_FILLS[7] + 1)
                return n_steps

            dve.wait_ge(params_in, 16)
            dve.wait_ge(pos_in, 16)
            step(V.tensor_copy(posf, pos_i[:, :]))
            for t in range(NT):
                last = V.tensor_scalar(tr0[:, t * HR:t * HR + HR], const("inv", HR), posf[:, t:t + 1], None, ALU.mult)
            step(last)
            two_pi = 2 * np.pi
            big = 1.5 * 2 ** 23
            step(V.tensor_scalar(tr1, tr0, 1 / two_pi, big, ALU.mult, ALU.add))
            step(V.tensor_scalar(tr1, tr1, -big, None, ALU.add))
            c1 = 6.28125
            c2 = float(np.floor((two_pi - c1) * 2 ** 17) / 2 ** 17)
            c3 = float(np.floor((two_pi - c1 - c2) * 2 ** 28) / 2 ** 28)
            c4 = float(np.float32(two_pi - c1 - c2 - c3))
            for c in (c1, c2, c3, c4):
                step(V.scalar_tensor_tensor(out=tr0, in0=tr1, scalar=-c, in1=tr0, op0=ALU.mult, op1=ALU.add))
            pi = 3.1415925
            step(V.tensor_scalar(tr0, tr0, pi, -pi, ALU.min, ALU.max))
            step(V.scalar_tensor_tensor(out=tr2, in0=tr0, scalar=-1.0, in1=tr0, op0=ALU.mult, op1=ALU.min))
            V.tensor_scalar(tr1, tr2, float(np.pi / 2), None, ALU.add).then_inc(trig_arg, 1)

            dve.wait_ge(wsmall_in, 48)
            step(V.tensor_copy(rt_hi, rt_v))
            rest(rt_lo, rt_v, rt_hi).then_inc(rt_ready, 1)
            for g in range(SPLITS):
                split(g)
            n_steps = None
            for L in range(DEPTH):
                f = NF + L * (N0 - NF)
                if L == 0:
                    dve.wait_ge(x_in, 16)
                norm(3 * L)
                take_xT(3 * L, L, "g_attn")
                mixers(L)
                norm(3 * L + 1)
                take_xT(3 * L + 1, L, "g_ffn")
                if L == 0:
                    for c in range(EXPERT_UNITS):
                        cb = c // 4
                        split(f + c + SPLITS)
                        if c < 4 * NCB and c % 4 == 3:
                            for t in range(NT):
                                dve.wait_ge(*banks.taken(("g", cb, t)))
                                o = banks.filled(dve, ("u", cb, t))
                                V.tensor_tensor(dhs[:, t, :], o, dsg[:, t, :], ALU.mult).then_inc(
                                    banks.is_free(("u", cb, t)), 1)
                        if (4 < c < 4 * NCB and c % 4 == 1) or c == 4 * NCB:
                            for t in range(NT):
                                dve.wait_ge(h_hi_ready, NT * (cb - 1) + t + 1)
                                o = banks.filled(dve, ("hT", cb - 1, t))
                                w = (slice(None), slice(4 * cb - 4, 4 * cb), slice(t * P, t * P + P))
                                rest(hT_lo[w], o.rearrange("p (k s) -> p k s", k=4), hT_hi[w]).then_inc(
                                    banks.is_free(("hT", cb - 1, t)), 1)
                    for t in range(NT):
                        for half in range(2):
                            o = banks.filled(dve, ("d", t, half))
                            v = h[:, t, half * 512:half * 512 + 512]
                            V.tensor_tensor(v, v, o, ALU.add).then_inc(banks.is_free(("d", t, half)), 1)
                else:
                    n_steps = experts()
                dve.wait_ge(p_hi_ready, L + 1)
                o = banks.filled(dve, ("pT", L))
                rest(pT_lo, o.rearrange("p (k s) -> p k s", k=2), pT_hi).then_inc(banks.is_free(("pT", L)), 1)
                norm(3 * L + 2)
                take_xT(3 * L + 2, L, "g_ple")
                embed(L, n_steps)
            k = 3 * DEPTH
            dve.wait_ge(sumsq, NT * (k + 1))
            V.tensor_scalar(ms, ss, 1.0 / D, RMS_EPS, ALU.mult, ALU.add).then_inc(ms_ready, 1)
            dve.wait_ge(rms_ready, k + 1)
            step(V.reciprocal(rstd, rms))
            dve.wait_ge(gfin_in, 16)
            for t in range(NT):
                V.scalar_tensor_tensor(out=xs[:, t, :], in0=h[:, t, :], scalar=rstd[:, t:t + 1], in1=gfin,
                                       op0=ALU.mult, op1=ALU.mult).then_inc(out_ready, 1)


def _constants():
    i = np.arange(P)
    group = (i[:, None] // 64 == i[None, :] // 64) / np.float32(64)
    mask = np.zeros((P, 2 * P))
    mask[:, P:] = np.where(i[:, None] >= i[None, :], 0.0, NEG)
    inv = np.float32(10000.0) ** (-np.arange(0, ROPE, 2, dtype=np.float32) / np.float32(ROPE))
    parts = [np.eye(P), i[:, None] <= i[None, :], np.ones((P, P)), group, np.tile(i, (P, 1)), mask,
             np.tile(inv, (P, 1))]
    return [a.astype(np.float32) for a in parts]


def _by_partition(a):
    a = np.asarray(a)
    return np.moveaxis(a.reshape(a.shape[:-1] + (-1, P)), -1, 0)


def _spread(a):
    return np.broadcast_to(np.asarray(a)[None], (P,) + np.asarray(a).shape)


def kernel(**inputs):
    import concourse.bacc as bacc
    from concourse.bass_utils import run_bass_kernel_spmd

    v = {k: np.asarray(a) for k, a in inputs.items()}
    parts = _constants()
    for L in range(DEPTH):
        parts += [_by_partition(v["attn_norm_g"][L]), _by_partition(v["ffn_norm_g"][L]),
                  _by_partition(v["ple_norm_g"][L]),
                  _by_partition(v["conv_dw_w"][L]).transpose(0, 2, 1).reshape(P, -1),
                  _by_partition(v["conv_dw_b"][L]), _by_partition(v["conv_ln_g"][L]),
                  _by_partition(v["conv_ln_b"][L]),
                  _by_partition(v["ssd_conv_w"][L]).transpose(0, 2, 1).reshape(P, -1),
                  _by_partition(v["ssd_conv_b"][L]), _spread(v["ssd_dt_bias"][L]), _spread(v["ssd_a_log"][L]),
                  _spread(v["ssd_d"][L]), _by_partition(v["ssd_norm_g"][L]), _by_partition(v["mla_q_norm_g"][L]),
                  _by_partition(v["mla_kv_norm_g"][L])]
    params = np.ascontiguousarray(np.concatenate(parts, axis=1))
    v["positions"] = v["positions"].reshape(NT, P).T
    names = ["x", "p", "positions", "w_in", "mla_w_uq", "mla_w_ukv", "w_out", "dense_w_gate", "dense_w_up",
             "dense_w_down", "moe_router", "moe_w_gate", "moe_w_up", "moe_w_down", "ple_w_gate", "ple_w_proj",
             "final_norm_g"]
    arrays = {"params": params, **{n: np.ascontiguousarray(v[n]) for n in names}}
    nc = bacc.Bacc("TRN2", target_bir_lowering=False, num_devices=1)
    args = [nc.dram_tensor("in_" + n, a.shape, mybir.dt.from_np(a.dtype), kind="ExternalInput").ap()
            for n, a in arrays.items()]
    out = nc.dram_tensor("out", (1, SEQ, D), F32, kind="ExternalOutput").ap()
    trunk(nc, *args, out)
    r = run_bass_kernel_spmd(nc, [{"in_" + n: a for n, a in arrays.items()}], core_ids=[0])
    return r.results[0]["out"]
```

```python
from contextlib import ExitStack

import numpy as np
import concourse.bass as bass
from concourse import mybir

F32 = mybir.dt.float32
F32R = mybir.dt.float32r
I32 = mybir.dt.int32
U32 = mybir.dt.uint32
ALU = mybir.AluOpType
ACT = mybir.ActivationFunctionType
AX = mybir.AxisListType

P = 128
D = 1024
KT = D // P
SEQ = 256
NT = SEQ // P
DEPTH = 2
PLE = 256
CONVW = 256
CK = 31
SSDW = 512
SH = 8
SHD = SSDW // SH
SG = 2
SN = 128
SCONV = 4
XBC = SSDW + 2 * SG * SN
XT = XBC // P
MH = 4
NOPE = 64
ROPE = 32
HR = ROPE // 2
VD = 64
QD = NOPE + ROPE
QRANK = 256
KVRANK = 128
FF = 3584
FB = 512
NCB = FF // FB
FKT = FF // P
NE = 8
RMS_EPS = 1e-6
LN_EPS = 1e-5
C_CONV, C_Z, C_XBC = 0, 2 * CONVW, 2 * CONVW + SSDW
C_SM = C_XBC + XBC
SMW = SH + QRANK + KVRANK + ROPE
S_CQ, S_CKV, S_KR = SH, SH + QRANK, SH + QRANK + KVRANK
B_SIZE = NT * SMW + 2 * NT * SSDW + 2 * NT * MH * QD + NT * MH * VD + 2 * MH * SEQ + 3 * SEQ
SLOTS = 7
UNIT = 2048
SPLITS = 3
HALF_K = KT // 2
OUT_ORDER = (3, 0, 1, 2)
EXPERT_UNITS = 6 * NCB
DOWN_UNITS = 2 * NCB
assert EXPERT_UNITS % SLOTS == 0 and EXPERT_UNITS % SPLITS == 0
NEG = -1e30
POOL_TAPS = 21
EARLY_TAPS = 10


def layout(parts):
    at, out = 0, {}
    for name, n in parts:
        out[name] = at
        at += n
    return out, at


CONST_PARTS = [("ident", P), ("tri", P), ("ones", P), ("group", P), ("iota", P), ("mask", 2 * P), ("inv", HR)]
LAYER_PARTS = [("g_attn", KT), ("g_ffn", KT), ("g_ple", KT), ("cw", 2 * CK), ("cb", 2), ("lng", 2), ("lnb", 2),
               ("sw", XT * SCONV), ("sb", XT), ("dtb", SH), ("alog", SH), ("dskip", SH), ("sng", SSDW // P),
               ("qg", 2), ("kvg", 1)]
CONST_AT, CONST_N = layout(CONST_PARTS)
LAYER_AT, LAYER_N = layout(LAYER_PARTS)


def trunk(nc, params, x, p, positions, w_in, w_uq, w_ukv, w_out, dense_g, dense_u, dense_d, router,
          moe_g, moe_u, moe_d, ple_g, ple_p, final_g, out):
    with ExitStack() as ctx:
        def sb(name, n, dt=F32):
            return ctx.enter_context(nc.sbuf_tensor(name, [P, n], dt))

        def sem(name):
            return ctx.enter_context(nc.semaphore(name))

        def shared(name, n, over, n_over):
            at = -(-nc.sbuf_base // 32) * 32
            buf = sb(name, n)
            return buf, nc.alloc_sbuf_tensor_at(over, [P, n_over], F32R, offset=at)

        ring = sb("ring", SLOTS * UNIT)
        w_hi = sb("w_hi", SPLITS * UNIT, F32R)
        w_lo = sb("w_lo", SPLITS * UNIT, F32R)
        h_b = sb("h", NT * D)
        xs_b = sb("xs", NT * D)
        xT_b, xT_r = shared("xT", 2 * NT * D, "xT_parts", 2 * NT * D)
        arena_a, arena_a_r = shared("arena_a", FKT * SEQ, "hidden_a", FKT * SEQ)
        arena_b, arena_b_r = shared("arena_b", B_SIZE, "hidden_b", FKT * SEQ)
        par = sb("par", CONST_N + DEPTH * LAYER_N)
        wq_b = sb("wq", 2 * MH * QD)
        wkv_b = sb("wkv", MH * (NOPE + VD))
        rt = sb("rt", KT * NE)
        rt_r = sb("rt_parts", 2 * KT * NE, F32R)
        pos_i = sb("pos_i", NT, I32)
        trig = sb("trig", 5 * NT * HR)
        tiny = sb("tiny", 434)
        tinyi = sb("tinyi", 2 * 8, U32)
        flag = sb("flag", 1, I32)
        psum = ctx.enter_context(nc.psum_tensor("psum", [P, 8, 512], F32))

        h = h_b[:, :].rearrange("p (t d) -> p t d", t=NT)
        xs = xs_b[:, :].rearrange("p (t d) -> p t d", t=NT)
        xT_hi = xT_r[:, 0:NT * D].rearrange("p (k s) -> p k s", k=KT)
        xT_lo = xT_r[:, NT * D:].rearrange("p (k s) -> p k s", k=KT)

        def const(name, n=P):
            return par[:, CONST_AT[name]:CONST_AT[name] + n]

        def lp(L, name, i=0, n=1):
            a = CONST_N + L * LAYER_N + LAYER_AT[name] + i
            return par[:, a:a + n]

        ident, tri, ones, group, iota = (const(n) for n in ("ident", "tri", "ones", "group", "iota"))
        mask = const("mask", 2 * P)

        class View:

            def __init__(self, buf, at, end):
                self.buf, self.at, self.end = buf, at, end

            def __call__(self, n):
                a, self.at = self.at, self.at + n
                assert self.at <= self.end, (self.at, self.end)
                return self.buf[:, a:a + n]

        va = View(arena_a, 0, FKT * SEQ)
        cpad = va(2 * (CK - 1 + SEQ)).rearrange("p (m s) -> p m s", m=2)
        xpad_f = va(XT * (SCONV - 1 + SEQ))
        xpad = xpad_f.rearrange("p (m s) -> p m s", m=XT)
        xbcT = va(XT * SEQ).rearrange("p (m s) -> p m s", m=XT)
        z = va(NT * SSDW).rearrange("p (t c) -> p t c", t=NT)
        cacc = va(2 * SEQ).rearrange("p (m s) -> p m s", m=2)
        csq = va(2 * SEQ).rearrange("p (m s) -> p m s", m=2)
        ctmp = va(4 * NT * HR)
        hT_hi = arena_a_r[:, :].rearrange("p (k s) -> p k s", k=FKT)
        hT_lo = arena_b_r[:, :].rearrange("p (k s) -> p k s", k=FKT)
        ehT_hi = arena_a_r[:, 0:FKT * P].rearrange("p (k s) -> p k s", k=FKT)
        ehT_lo = arena_a_r[:, FKT * P:].rearrange("p (k s) -> p k s", k=FKT)
        dec = xpad_f[:, 0:NT * SH * P].rearrange("p (t h l) -> p t h l", t=NT, h=SH)
        vb = View(arena_b, 0, B_SIZE)
        sm_f = vb(NT * SMW)
        sm = sm_f.rearrange("p (t c) -> p t c", t=NT)
        xd = vb(NT * SSDW).rearrange("p (t c) -> p t c", t=NT)
        dx = vb(NT * SSDW).rearrange("p (t c) -> p t c", t=NT)
        tap_parts = [b.rearrange("p t c -> p (t c)")[:, a:a + 2 * SEQ].rearrange("p (m s) -> p m s", m=2)
                     for b, a in ((dx, 0), (dx, SSDW), (xd, SSDW))]
        st = sm_f[:, 0:SSDW]
        qk_f = vb(2 * NT * MH * QD)
        qf = qk_f[:, 0:NT * MH * QD].rearrange("p (t h d) -> p t h d", t=NT, h=MH)
        kf = qk_f[:, NT * MH * QD:].rearrange("p (t h d) -> p t h d", t=NT, h=MH)
        sc = [s.rearrange("p (h k) -> p h k", h=MH) for s in (qk_f[:, 0:MH * P], qk_f[:, MH * P:3 * MH * P])]
        vs = vb(NT * MH * VD).rearrange("p (t h d) -> p t h d", t=NT, h=MH)
        qkT_f = vb(2 * MH * SEQ)
        qT = qkT_f[:, 0:MH * SEQ].rearrange("p (h s) -> p h s", h=MH)
        kT = qkT_f[:, MH * SEQ:].rearrange("p (h s) -> p h s", h=MH)
        prT_f = qkT_f[:, 0:3 * MH * P]
        cqT = vb(2 * SEQ).rearrange("p (k s) -> p k s", k=2)
        ckvT = vb(SEQ)
        cbm = cqT.rearrange("p k s -> p (k s)").rearrange("p (t g l) -> p t g l", t=NT, g=SG)
        btok = ckvT.rearrange("p (g n) -> p g n", g=SG)
        prT = [prT_f[:, 0:MH * P].rearrange("p (h b q) -> p h b q", h=MH, b=1),
               prT_f[:, MH * P:].rearrange("p (h b q) -> p h b q", h=MH, b=2)]
        YW = SSDW + MH * VD
        ytok = xs_b[:, 0:NT * YW].rearrange("p (t c) -> p t c", t=NT)
        xdd = xs_b[:, NT * YW:NT * YW + SSDW]
        conv_parts = [ytok[:, t, SSDW:] for t in range(NT)]
        yT_hi, yT_lo = xT_hi, xT_lo
        squares = [xs_b[:, i * 512:i * 512 + 512] for i in range(3)]
        diag = xs_b[:, 3 * 512:3 * 512 + NT * P].rearrange("p (t s) -> p t s", t=NT)
        dsg = xs_b[:, 0:NT * FB].rearrange("p (t c) -> p t c", t=NT)
        dhs = xs_b[:, NT * FB:].rearrange("p (t c) -> p t c", t=NT)
        xg_hi = arena_b_r[:, 0:KT * P].rearrange("p (k s) -> p k s", k=KT)
        xg_lo = arena_b_r[:, KT * P:2 * KT * P].rearrange("p (k s) -> p k s", k=KT)
        vf = View(arena_b, 2 * KT * P, B_SIZE)
        sg = vf(2 * FB).rearrange("p (t c) -> p t c", t=2)
        hs = vf(2 * FB).rearrange("p (t c) -> p t c", t=2)
        ysb = vf(D)
        sel = vf(NT * P).rearrange("p (t s) -> p t s", t=NT)
        selg = vf(NT * P).rearrange("p (t s) -> p t s", t=NT)
        selgT = vf(NT * P).rearrange("p (t s) -> p t s", t=NT)
        logitsT = sg.rearrange("p t c -> p (t c)")[0:NE, 0:SEQ]
        ptok = arena_b[:, FKT * SEQ:FKT * SEQ + NT * PLE].rearrange("p (t c) -> p t c", t=NT)
        pT_hi = arena_a_r[:, 0:2 * SEQ].rearrange("p (k s) -> p k s", k=2)
        pT_lo = arena_a_r[:, 2 * SEQ:4 * SEQ].rearrange("p (k s) -> p k s", k=2)
        gfin = arena_a[:, 4 * SEQ:4 * SEQ + D]
        wq = wq_b[:, :].rearrange("p (k n) -> p k n", k=2)
        rt_v = rt[:, :].rearrange("p (k n) -> p k n", k=KT)
        rt_hi = rt_r[:, 0:KT * NE].rearrange("p (k n) -> p k n", k=KT)
        rt_lo = rt_r[:, KT * NE:].rearrange("p (k n) -> p k n", k=KT)

        cos_t, sin_t, tr0, tr1, tr2 = (trig[:, i * NT * HR:(i + 1) * NT * HR] for i in range(5))

        vt = View(tiny, 0, 434)
        ss = vt(2 * NT)
        ms = vt(2)
        warm = vt(1)
        rms = vt(2)
        rstd = vt(2)
        dtx, dtn, dte, dtu, dtl, dtc, dt, adt = (vt(NT * SH) for _ in range(8))
        nega = vt(SH)
        acs = vt(3 * SH)
        ea, dst = vt(SH), vt(SH)
        lss, lrm, lrs = (vt(4) for _ in range(3))
        gss, grm, grs = (vt(4) for _ in range(3))
        nm, den, rden = vt(8), vt(8), vt(8)
        posf = vt(NT)
        logits = vt(NT * NE)
        top = vt(NT * 8)
        topi = vt(NT * 2)
        dv, ev, g1, g2 = (vt(NT) for _ in range(4))
        o1, o2 = vt(NT * NE), vt(NT * NE)
        chosen = vt(NT * NE)
        rank = vt(NT * NE)
        STEPS = 2 * NE
        slot_of = vt(NT * (STEPS + 1)).rearrange("p (t e) -> p t e", t=NT)
        gate_of = vt(NT * (STEPS + 1)).rearrange("p (t e) -> p t e", t=NT)
        cnt = vt(NE)
        mx = vt(1)
        eps_rms, eps_ln = vt(1), vt(1)

        loaded = [sem(f"loaded{s}") for s in range(SLOTS)]
        hi_ready, lo_ready, unit_used = sem("hi_ready"), sem("lo_ready"), sem("unit_used")
        x_hi_ready, y_hi_ready, conv_hi_ready, h_hi_ready, p_hi_ready, rt_ready = (sem(n) for n in (
            "x_hi_ready", "y_hi_ready", "conv_hi_ready", "h_hi_ready", "p_hi_ready", "rt_ready"))
        moe_x_hi, moe_h_hi = sem("moe_x_hi"), sem("moe_h_hi")
        params_in, pos_in, wsmall_in = (sem(n) for n in ("params_in", "pos_in", "wsmall_in"))
        x_in = [sem(f"x_in{t}") for t in range(NT)]
        ptok_in, gfin_in, out_ready, out_done = (sem(n) for n in ("ptok_in", "gfin_in", "out_ready", "out_done"))
        table_in, eps_ready = sem("table_in"), sem("eps_ready")
        h_ready, sumsq, ms_ready, rms_ready, xs_ready = (sem(n) for n in (
            "h_ready", "sumsq", "ms_ready", "rms_ready", "xs_ready"))
        conv_ready, csq_ready, chn_ready = (sem(n) for n in (
            "conv_ready", "csq_ready", "chn_ready"))
        (xtap_ready, xbc_ready, pads_ready) = (sem(n) for n in ("xtap_ready", "xbc_ready", "pads_ready"))
        (dtn_ready, dte_ready, dtu_ready, dtl_ready, nega_ready, adt_ready, acsd_ready, ea_ready, triadt_ready,
         dec_ready, mix_ready, xdd_ready, ygz_ready, gss_ready, grm_ready, ytok_ready) = (
             sem(n) for n in ("dtn_ready", "dte_ready", "dtu_ready", "dtl_ready", "nega_ready", "adt_ready",
                              "acsd_ready", "ea_ready", "triadt_ready", "dec_ready", "mix_ready", "xdd_ready",
                              "ygz_ready", "gss_ready", "grm_ready", "ytok_ready"))
        (lss_ready, lrm_ready, qk_ready, score_ready, prob_ready, yT_ready) = (
            sem(n) for n in ("lss_ready", "lrm_ready", "qk_ready", "score_ready",
                             "prob_ready", "yT_ready"))
        (chosen_ready, dv_ready, ev_ready, flag_ready, sel_ready, selg_ready) = (sem(n) for n in (
            "chosen_ready", "dv_ready", "ev_ready", "flag_ready", "sel_ready", "selg_ready"))
        trig_arg, trig_ready = sem("trig_arg"), sem("trig_ready")
        dve_step, tap_product, tap_done = sem("dve_step"), sem("tap_product"), sem("tap_done")
        conv_product, conv_sum = sem("conv_product"), sem("conv_sum")

        class Banks:

            def __init__(self):
                self.full = [sem(f"full{b}") for b in range(8)]
                self.free = [sem(f"free{b}") for b in range(8)]
                self.count = [0] * 8
                self.uses = {}

            def fill(self, pe, name, b):
                if self.count[b]:
                    pe.wait_ge(self.free[b], self.count[b])
                self.count[b] += 1
                self.uses[name] = (b, self.count[b])
                return psum[:, b, :]

            def is_full(self, name):
                return self.full[self.uses[name][0]]

            def filled(self, eng, name):
                b, n = self.uses[name]
                eng.wait_ge(self.full[b], n)
                return psum[:, b, :]

            def is_free(self, name):
                return self.free[self.uses[name][0]]

            def taken(self, name):
                b, n = self.uses[name]
                return self.free[b], n

        banks = Banks()
        moe_full = [sem(f"moe_full{b}") for b in range(8)]
        moe_free = [sem(f"moe_free{b}") for b in range(8)]
        MOE_USED = 2 * NCB + DOWN_UNITS - 1
        MOE_FILLS = [NCB, NCB, NCB + 2, 2, 2, 1, 1, 1]

        SCATTER = ((7, 1), (3, 2), (4, 2), (2, NCB + 2))

        def by_cols(w, c0, n=SEQ):
            return [(w.rearrange("(k p) n -> p k n", p=P)[:, :, c0:c0 + n], KT, n)]

        def by_rows(w, c0, n=512):
            v = w.rearrange("(k p) n -> p k n", p=P)
            return [(v[:, i * HALF_K:(i + 1) * HALF_K, c0:c0 + n], HALF_K, n) for i in range(2)]

        def whole_rows(w, i):
            return [(w.rearrange("(k p) n -> p k n", p=P)[:, 2 * i:2 * i + 2, :], 2, D)]

        def layer_front(L):
            wi, wo = w_in[L], w_out[L]
            return (sum((by_cols(wi, C_CONV + SEQ * i) for i in range(2)), []) + by_rows(wi, C_SM, SMW)
                    + sum((by_cols(wi, C_XBC + SEQ * i) for i in range(4)), []) + by_rows(wi, C_Z)
                    + sum((whole_rows(wo, i) for i in OUT_ORDER), []))

        def layer_ple(L):
            return whole_rows(ple_p[L], 0) + by_rows(ple_g[L], 0) + by_rows(ple_g[L], 512)

        def swiglu_unit(g, u, d, c):
            if c < 4 * NCB:
                return by_rows(g if c % 4 < 2 else u, (c // 4) * FB)[c % 2]
            return whole_rows(d, c - 4 * NCB)[0]

        FRONT = layer_front(0)
        NF = len(FRONT)
        before_moe = FRONT + [swiglu_unit(dense_g[0], dense_u[0], dense_d[0], c)
                              for c in range(EXPERT_UNITS)] + layer_ple(0) + layer_front(1)
        after_moe = layer_ple(1)
        N0 = len(before_moe)
        sizes = [k * n for _, k, n in before_moe] + [UNIT] * (EXPERT_UNITS + len(after_moe))
        last_reader = []

        def raw(g, n=UNIT):
            return ring[:, (g % SLOTS) * UNIT:(g % SLOTS) * UNIT + n]

        def part(buf, g, n=UNIT):
            return buf[:, (g % SPLITS) * UNIT:(g % SPLITS) * UNIT + n]

        def landed(g, e=0):
            return e * (16 * EXPERT_UNITS // SLOTS) + 16 * (g // SLOTS + 1)

        used_before_moe = []
        block = ctx.enter_context(nc.Block())

        @block.tensor
        def _(pe):
            mm, tr = nc.tensor.matmul, nc.tensor.transpose
            used = [0]

            def unit():
                g = len(last_reader)
                pe.wait_ge(lo_ready, g + 1)
                k = before_moe[g][1]
                return tuple(part(b, g, sizes[g]).rearrange("p (k n) -> p k n", k=k) for b in (w_hi, w_lo))

            def unit_done(last=None, key=None):
                if key is None:
                    used[0] += 1
                    last.then_inc(unit_used, 1)
                    last_reader.append((unit_used, used[0]))
                else:
                    b, n = banks.uses[key]
                    last_reader.append((banks.full[b], n))

            def product(o, a, b, first, final):
                mm(o, a[0], b[0], start=first, stop=False)
                mm(o, a[0], b[1], start=False, stop=False)
                return mm(o, a[1], b[0], start=False, stop=final)

            def at(parts, *index):
                return tuple(x[index] for x in parts)

            ALLP = slice(None)
            xTp, pTp = (xT_hi, xT_lo), (pT_hi, pT_lo)

            def transpose_x(key):
                for b in range(4):
                    o = banks.fill(pe, (key, b), b)
                    for q in range(2):
                        for t in range(NT):
                            kt = 2 * b + q
                            c = q * SEQ + t * P
                            last = mm(o[:, c:c + P], h[:, t, kt * P:kt * P + P], diag[:, t, :], start=True, stop=True)
                    last.then_inc(banks.is_full((key, b)), 1)
                    xT_banks[b] = banks.taken((key, b))

            xT_banks = {}

            def wait_xT(kt):
                if kt // 2 in xT_banks:
                    pe.wait_ge(*xT_banks.pop(kt // 2))

            def channels_by_tokens(key, b):
                w = unit()
                o = banks.fill(pe, key, b)
                for m in range(2):
                    for kt in range(KT):
                        wait_xT(kt)
                        last = product(o[:, m * SEQ:m * SEQ + SEQ], at(w, ALLP, kt, slice(m * P, m * P + P)),
                                       at(xTp, ALLP, kt), kt == 0, kt == KT - 1)
                last.then_inc(banks.is_full(key), 1)
                unit_done(key=key)

            def half_product(keys, bs, n, i):
                w = unit()
                for t in range(NT):
                    o = banks.fill(pe, keys[t], bs[t]) if i == 0 else psum[:, bs[t], :]
                    for q in range(HALF_K):
                        kt = HALF_K * i + q
                        wait_xT(kt)
                        last = product(o[:, 0:n], at(xTp, ALLP, kt, slice(t * P, t * P + P)), at(w, ALLP, q),
                                       kt == 0, kt == KT - 1)
                    if i:
                        last.then_inc(banks.is_full(keys[t]), 1)
                if i:
                    unit_done(key=keys[1])
                else:
                    unit_done(last)

            def tokens_by_channels(keys, bs, n):
                for i in range(2):
                    half_product(keys, bs, n, i)

            def mixers(L):
                for j in range(2):
                    channels_by_tokens(("conv", L, j), 4 + j)
                tokens_by_channels([("sm", L, t) for t in range(NT)], (2, 3), SMW)
                for j in range(2):
                    channels_by_tokens(("xbc", L, j), 6 + j)
                for t in range(NT):
                    pe.wait_ge(*banks.taken(("sm", L, t)))
                o = banks.fill(pe, ("cqT", L), 4)
                for k in range(2):
                    for t in range(NT):
                        last = tr(o[:, k * SEQ + t * P:k * SEQ + t * P + P],
                                  sm[:, t, S_CQ + k * P:S_CQ + k * P + P], ident)
                last.then_inc(banks.is_full(("cqT", L)), 1)
                o = banks.fill(pe, ("ckvT", L), 5)
                for t in range(NT):
                    last = tr(o[:, t * P:t * P + P], sm[:, t, S_CKV:S_CKV + KVRANK], ident)
                last.then_inc(banks.is_full(("ckvT", L)), 1)
                channels_by_tokens(("xbc", L, 2), 0)
                pe.wait_ge(*banks.taken(("cqT", L)))
                pe.wait_ge(*banks.taken(("ckvT", L)))
                pe.wait_ge(wsmall_in, 16 * (2 * L + 3))
                for t in range(NT):
                    key = ("q", L, t)
                    o = banks.fill(pe, key, 2 + t)
                    for k in range(2):
                        last = mm(o[:, 0:MH * QD], cqT[:, k, t * P:t * P + P], wq[:, k, :], start=k == 0, stop=k == 1)
                    last.then_inc(banks.is_full(key), 1)
                for t in range(NT):
                    o = banks.fill(pe, ("kv", L, t), 4 + t)
                    mm(o, ckvT[:, t * P:t * P + P], wkv_b[:, :], start=True, stop=True).then_inc(
                        banks.is_full(("kv", L, t)), 1)
                channels_by_tokens(("xbc", L, 3), 1)
                zk = [("z", L, t) for t in range(NT)]
                half_product(zk, (6, 7), 512, 0)
                pe.wait_ge(qk_ready, L + 1)
                for t in range(NT):
                    pe.wait_ge(*banks.taken(("kv", L, t)))
                for n, (buf, name) in enumerate(((qf, "qT"), (kf, "kT"))):
                    for t in range(NT):
                        o = banks.fill(pe, (name, L, t), 2 * n + t)
                        for hd in range(MH):
                            last = tr(o[0:QD, hd * P:hd * P + P], buf[:, t, hd, :], ident)
                        last.then_inc(banks.is_full((name, L, t)), 1)
                pe.wait_ge(adt_ready, L + 1)
                o = banks.fill(pe, ("acs", L), 4)
                for t in range(NT):
                    mm(o[:, t * SH:t * SH + SH], tri, adt[:, t * SH:t * SH + SH], start=True, stop=True)
                mm(o[:, 2 * SH:3 * SH], ones, adt[:, 0:SH], start=True, stop=True).then_inc(
                    banks.is_full(("acs", L)), 1)
                for name in ("qT", "kT"):
                    for t in range(NT):
                        pe.wait_ge(*banks.taken((name, L, t)))
                o = banks.fill(pe, ("sc", L, 0), 0)
                for hd in range(MH):
                    last = mm(o[:, hd * P:hd * P + P], qT[0:QD, hd, 0:P], kT[0:QD, hd, 0:P], start=True, stop=True)
                last.then_inc(banks.is_full(("sc", L, 0)), 1)
                for j in range(2):
                    key = ("sc", L, 1 + j)
                    o = banks.fill(pe, key, 1 + j)
                    for i in range(2):
                        hd = 2 * j + i
                        last = mm(o[:, i * SEQ:i * SEQ + SEQ], qT[0:QD, hd, P:SEQ], kT[0:QD, hd, :],
                                  start=True, stop=True)
                    last.then_inc(banks.is_full(key), 1)
                for t in range(NT):
                    o = banks.fill(pe, ("xtok", L, t), (5, 3)[t])
                    for m in range(4):
                        if t == 0:
                            pe.wait_ge(xbc_ready, XT * L + m + 1)
                        last = tr(o[:, m * P:m * P + P], xbcT[:, m, t * P:t * P + P], ident)
                    last.then_inc(banks.is_full(("xtok", L, t)), 1)
                half_product(zk, (6, 7), 512, 1)
                pe.wait_ge(xbc_ready, XT * (L + 1))
                o = banks.fill(pe, ("cb", L), 4)
                for t in range(NT):
                    for g in range(SG):
                        c0 = (t * SG + g) * P
                        last = mm(o[:, c0:c0 + P], xbcT[:, 4 + g, t * P:t * P + P], xbcT[:, 6 + g, t * P:t * P + P],
                                  start=True, stop=True)
                last.then_inc(banks.is_full(("cb", L)), 1)
                o = banks.fill(pe, ("btok", L), 1)
                for g in range(SG):
                    last = tr(o[:, g * P:g * P + P], xbcT[:, 4 + g, 0:P], ident)
                last.then_inc(banks.is_full(("btok", L)), 1)
                for t in range(NT):
                    for g in range(SG):
                        pe.wait_ge(triadt_ready, 4 * L + 2 * t + g + 1)
                        key = ("seg", L, t, g)
                        o = banks.fill(pe, key, [5, 3, 4, 0][2 * t + g])
                        mm(o, ones, dec[:, t, 4 * g:4 * g + 4, :].rearrange("p h l -> p (h l)"),
                           start=True, stop=True).then_inc(banks.is_full(key), 1)
                pe.wait_ge(prob_ready, 8 * L + 4)
                o = banks.fill(pe, ("prT", L, 0), 1)
                for hd in range(MH):
                    last = tr(o[:, hd * P:hd * P + P], sc[0][:, hd, :], ident)
                last.then_inc(banks.is_full(("prT", L, 0)), 1)
                pe.wait_ge(prob_ready, 8 * L + 8)
                for j in range(2):
                    key = ("prT", L, 1 + j)
                    o = banks.fill(pe, key, (2, 0)[j])
                    for i in range(2):
                        for b in range(2):
                            last = tr(o[:, (2 * i + b) * P:(2 * i + b) * P + P], sc[1][:, 2 * j + i, b * P:b * P + P],
                                      ident)
                    last.then_inc(banks.is_full(key), 1)
                pe.wait_ge(*banks.taken(("btok", L)))
                pe.wait_ge(xdd_ready, L + 1)
                o = banks.fill(pe, ("st", L), 5)
                for g in range(SG):
                    last = mm(o[:, g * SEQ:g * SEQ + SEQ], btok[:, g, :], xdd[:, g * SEQ:g * SEQ + SEQ],
                              start=True, stop=True)
                last.then_inc(banks.is_full(("st", L)), 1)
                for t in range(NT):
                    pe.wait_ge(*banks.taken(("xtok", L, t)))
                    key = ("yd", L, t)
                    o = banks.fill(pe, key, 3 + t)
                    for hd in range(SH):
                        if hd % 4 == 0:
                            pe.wait_ge(mix_ready, 4 * L + 2 * t + hd // 4 + 1)
                        last = mm(o[:, hd * SHD:hd * SHD + SHD], dec[:, t, hd, :], xd[:, t, hd * SHD:hd * SHD + SHD],
                                  start=True, stop=True)
                    last.then_inc(banks.is_full(key), 1)
                pe.wait_ge(*banks.taken(("st", L)))
                o = banks.fill(pe, ("yo", L), 6)
                for g in range(SG):
                    last = mm(o[:, g * SEQ:g * SEQ + SEQ], xbcT[:, 6 + g, P:SEQ], st[:, g * SEQ:g * SEQ + SEQ],
                              start=True, stop=True)
                last.then_inc(banks.is_full(("yo", L)), 1)
                pe.wait_ge(conv_ready, L + 1)
                o = banks.fill(pe, ("mean", L), 5)
                mm(o, group, cacc.rearrange("p m s -> p (m s)"), start=True, stop=True).then_inc(
                    banks.is_full(("mean", L)), 1)
                for j in range(3):
                    pe.wait_ge(*banks.taken(("prT", L, j)))
                o = banks.fill(pe, ("pv", L), 7)
                for t in range(NT):
                    for hd in range(MH):
                        c0 = (t * MH + hd) * VD
                        for b in range(t + 1):
                            last = mm(o[:, c0:c0 + VD], prT[t][:, hd, b, :], vs[:, b, hd, :], start=b == 0, stop=b == t)
                last.then_inc(banks.is_full(("pv", L)), 1)
                def y_transposed(j, b):
                    key = ("yT", L, j)
                    o = banks.fill(pe, key, b)
                    for q in range(2):
                        m = 2 * j + q
                        for t in range(NT):
                            last = tr(o[:, q * SEQ + t * P:q * SEQ + t * P + P], ytok[:, t, m * P:m * P + P], ident)
                    last.then_inc(banks.is_full(key), 1)

                pe.wait_ge(*banks.taken(("pv", L)))
                y_transposed(2, 0)
                pe.wait_ge(csq_ready, L + 1)
                o = banks.fill(pe, ("var", L), 5)
                mm(o, group, csq.rearrange("p m s -> p (m s)"), start=True, stop=True).then_inc(
                    banks.is_full(("var", L)), 1)
                keys = [("o", L, t, half) for t in range(NT) for half in range(2)]
                acc = {}
                for i, pair in enumerate(OUT_ORDER):
                    w = unit()
                    if i == 0:
                        pe.wait_ge(*banks.taken(("yT", L, 2)))
                    elif i == 1:
                        for j in range(2):
                            pe.wait_ge(ytok_ready, 2 * L + j + 1)
                            y_transposed(j, 1 + j)
                        pe.wait_ge(yT_ready, L + 1)
                    if i > 1:
                        pe.wait_ge(*banks.taken(("yT", L, i - 2)))
                    for n, key in enumerate(keys):
                        t, half = divmod(n, 2)
                        if i == 0:
                            acc[key] = banks.fill(pe, key, (7, 4, 5, 6)[n])
                        for q in range(2):
                            last = product(acc[key], at((yT_hi, yT_lo), ALLP, 2 * pair + q, slice(t * P, t * P + P)),
                                           at(w, ALLP, q, slice(half * 512, half * 512 + 512)),
                                           i == 0 and q == 0, i == 3 and q == 1)
                        if i == 3:
                            last.then_inc(banks.is_full(key), 1)
                    if i < 3:
                        unit_done(last)
                unit_done(key=keys[-1])

            def hidden_T(cb):
                for t in range(NT):
                    key = ("hT", cb, t)
                    pe.wait_ge(*banks.taken(("u", cb, t)))
                    o = banks.fill(pe, key, 4 + t)
                    for q in range(4):
                        last = tr(o[:, q * P:q * P + P], dhs[:, t, q * P:q * P + P], ident)
                    last.then_inc(banks.is_full(key), 1)

            def dense():
                for cb in range(NCB):
                    tokens_by_channels([("g", cb, t) for t in range(NT)], (0, 1), FB)
                    if cb:
                        hidden_T(cb - 1)
                    tokens_by_channels([("u", cb, t) for t in range(NT)], (2, 3), FB)
                keys = [(t, half) for t in range(NT) for half in range(2)]
                acc = {key: banks.fill(pe, ("d", *key), b) for key, b in zip(keys, (6, 7, 0, 1))}
                for j in range(DOWN_UNITS):
                    w = unit()
                    if j == 1:
                        hidden_T(NCB - 1)
                    for t in range(NT):
                        pe.wait_ge(*banks.taken(("hT", j // 2, t)))
                    for t, half in keys:
                        for q in range(2):
                            kt = 2 * j + q
                            last = product(acc[t, half], at((hT_hi, hT_lo), ALLP, kt, slice(t * P, t * P + P)),
                                           at(w, ALLP, q, slice(half * 512, half * 512 + 512)),
                                           kt == 0, kt == FKT - 1)
                        if j == DOWN_UNITS - 1:
                            last.then_inc(banks.is_full(("d", t, half)), 1)
                    if j < DOWN_UNITS - 1:
                        unit_done(last)
                unit_done(key=("d", 1, 1))

            def ple_p(L, w):
                pe.wait_ge(ptok_in, 16 * (L + 1))
                o = banks.fill(pe, ("pT", L), 3)
                for k in range(2):
                    for t in range(NT):
                        last = tr(o[:, k * SEQ + t * P:k * SEQ + t * P + P], ptok[:, t, k * P:k * P + P], ident)
                last.then_inc(banks.is_full(("pT", L)), 1)
                if L:
                    for b in (4, 5, 6, 7, 0, 1, 2):
                        moe_done(b)
                pe.wait_ge(*banks.taken(("pT", L)))
                w = w()
                for half in range(2):
                    for t in range(NT):
                        key = ("pp", L, half, t)
                        o = banks.fill(pe, key, 4 + 2 * half + t)
                        for k in range(2):
                            last = product(o, at(pTp, ALLP, k, slice(t * P, t * P + P)),
                                           at(w, ALLP, k, slice(half * 512, half * 512 + 512)), k == 0, k == 1)
                        last.then_inc(banks.is_full(key), 1)

            def ple_x(L):
                pe.wait_ge(xs_ready, 2 * (3 * L + 3))
                transpose_x(("n", 3 * L + 2))

            def ple(L):
                ple_p(L, unit)
                unit_done(key=("pp", L, 1, 1))
                ple_x(L)
                for half in range(2):
                    tokens_by_channels([("pg", L, half, t) for t in range(NT)], ((0, 1), (2, 3))[half], 512)

            pe.wait_ge(params_in, 16)
            for L in range(DEPTH):
                pe.wait_ge(xs_ready, 2 * (3 * L + 1))
                transpose_x(("n", 3 * L))
                mixers(L)
                pe.wait_ge(xs_ready, 2 * (3 * L + 2))
                transpose_x(("n", 3 * L + 1))
                if L == 0:
                    dense()
                    ple(0)

            pe.wait_ge(rt_ready, 1)
            o = banks.fill(pe, ("lgT",), 4)
            for kt in range(KT):
                wait_xT(kt)
                last = product(o[0:NE, 0:SEQ], at((rt_hi, rt_lo), ALLP, kt), at(xTp, ALLP, kt), kt == 0, kt == KT - 1)
            last.then_inc(banks.is_full(("lgT",)), 1)
            pe.wait_ge(*banks.taken(("lgT",)))
            o = banks.fill(pe, ("lg",), 5)
            for t in range(NT):
                last = tr(o[:, t * NE:t * NE + NE], logitsT[:, t * P:t * P + P], ident[0:NE, 0:NE])
            last.then_inc(banks.is_full(("lg",)), 1)
            pe.wait_ge(chosen_ready, 1)
            o = banks.fill(pe, ("rank",), 6)
            mm(o[:, 0:NE], tri, chosen[:, 0:NE], start=True, stop=True)
            mm(o[:, NE:2 * NE], tri, chosen[:, NE:2 * NE], start=True, stop=False)
            mm(o[:, NE:2 * NE], ones, chosen[:, 0:NE], start=False, stop=True)
            mm(o[:, 2 * NE:3 * NE], ones, chosen[:, 0:NE], start=True, stop=False)
            mm(o[:, 2 * NE:3 * NE], ones, chosen[:, NE:2 * NE], start=False, stop=True).then_inc(
                banks.is_full(("rank",)), 1)

            for b in range(8):
                pe.wait_ge(banks.free[b], banks.count[b])

            def gather(step):
                pe.wait_ge(sel_ready, step + 1)
                for half in range(2):
                    pe.wait_ge(moe_free[5 + half], step + 1)
                    o = psum[:, 5 + half, :]
                    for q in range(4):
                        kt = 4 * half + q
                        for t in range(NT):
                            last = mm(o[:, q * P:q * P + P], xs[:, t, kt * P:kt * P + P], sel[:, t, :],
                                      start=t == 0, stop=t == NT - 1)
                    last.then_inc(moe_full[5 + half], 1)

            for b in range(8):
                pe.sem_inc(moe_free[b], 1)
            gather(0)
            pe.wait_ge(flag_ready, 1)
            n_steps = pe.value_load(flag[0:1, 0:1], min_val=NE, max_val=2 * NE)
            with pe.Fori(0, n_steps) as e:
                def moe_unit(c, k):
                    pe.wait_ge(lo_ready, e * EXPERT_UNITS + N0 + c + 1)
                    return tuple(part(b, N0 + c).rearrange("p (k n) -> p k n", k=k) for b in (w_hi, w_lo))

                def hidden(cb):
                    pe.wait_ge(moe_free[1], e * NCB + cb + 2)
                    pe.wait_ge(moe_free[2], e * (NCB + 2) + cb + 2)
                    for q in range(4):
                        last = tr(psum[:, 2, q * P:q * P + P], hs[:, cb % 2, q * P:q * P + P], ident)
                    last.then_inc(moe_full[2], 1)

                for cb in range(NCB):
                    for u in range(2):
                        for i in range(2):
                            w = moe_unit(4 * cb + 2 * u + i, HALF_K)
                            if i == 0:
                                pe.wait_ge(moe_free[u], e * NCB + cb + 1)
                            if cb == 0 and u == 0:
                                pe.wait_ge(moe_free[5 + i], e + 2)
                            for q in range(HALF_K):
                                kt = HALF_K * i + q
                                last = product(psum[:, u, :], at((xg_hi, xg_lo), ALLP, kt), at(w, ALLP, q),
                                               kt == 0, kt == KT - 1)
                            last.then_inc(moe_full[u] if i else unit_used, 1)
                        if u == 0 and cb == 0:
                            pe.wait_ge(selg_ready, e + 1)
                            pe.wait_ge(moe_free[2], e * (NCB + 2) + 1)
                            for t in range(NT):
                                last = tr(psum[:, 2, t * P:t * P + P], selg[:, t, :], ident)
                            last.then_inc(moe_full[2], 1)
                        elif u == 0:
                            hidden(cb - 1)
                for half in range(2):
                    pe.wait_ge(moe_free[3 + half], e * 2 + 1)
                for j in range(DOWN_UNITS):
                    w = moe_unit(4 * NCB + j, 2)
                    if j == 3:
                        hidden(NCB - 1)
                    pe.wait_ge(moe_free[2], e * (NCB + 2) + j // 2 + 3)
                    for half in range(2):
                        for q in range(2):
                            kt = 2 * j + q
                            last = product(psum[:, 3 + half, :], at((ehT_hi, ehT_lo), ALLP, kt),
                                           at(w, ALLP, q, slice(half * 512, half * 512 + 512)),
                                           kt == 0, kt == FKT - 1)
                        if j == DOWN_UNITS - 1:
                            last.then_inc(moe_full[3 + half], 1)
                    if j < DOWN_UNITS - 1:
                        last.then_inc(unit_used, 1)
                gather(e + 1)
                pe.wait_ge(moe_free[3], e * 2 + 2)
                pe.wait_ge(moe_free[4], e * 2 + 2)
                for i, (b, n) in enumerate(SCATTER):
                    t, half = divmod(i, 2)
                    pe.wait_ge(moe_free[b], e * MOE_FILLS[b] + n)
                    mm(psum[:, b, :], selgT[:, t, :], ysb[:, half * 512:half * 512 + 512],
                       start=True, stop=True).then_inc(moe_full[b], 1)
            def moe_done(b):
                extra = 2 if b in (5, 6) else 1
                pe.wait_ge(moe_free[b], n_steps * MOE_FILLS[b] + extra)

            def after_unit(c, k):
                pe.wait_ge(lo_ready, n_steps * EXPERT_UNITS + N0 + c + 1)
                return tuple(part(b, N0 + c).rearrange("p (k n) -> p k n", k=k) for b in (w_hi, w_lo))

            moe_done(3)
            ple_p(1, lambda: after_unit(0, 2))
            ple_x(1)
            for half in range(2):
                keys, bs = [("pg", 1, half, t) for t in range(NT)], ((0, 1), (2, 3))[half]
                for i in range(2):
                    w = after_unit(1 + 2 * half + i, HALF_K)
                    for t in range(NT):
                        o = banks.fill(pe, keys[t], bs[t]) if i == 0 else psum[:, bs[t], :]
                        for q in range(HALF_K):
                            kt = HALF_K * i + q
                            wait_xT(kt)
                            last = product(o, at(xTp, ALLP, kt, slice(t * P, t * P + P)), at(w, ALLP, q),
                                           kt == 0, kt == KT - 1)
                        if i:
                            last.then_inc(banks.is_full(keys[t]), 1)
                    if i == 0:
                        last.then_inc(unit_used, 1)
            used_before_moe.append(used[0])

        def moe_reader(c, e):
            if c < 4 * NCB:
                cb, r = divmod(c, 4)
                if r % 2:
                    return moe_full[r // 2], e * NCB + cb + 1
                return unit_used, e * MOE_USED + used_before_moe[0] + 2 * cb + r // 2 + 1
            j = c - 4 * NCB
            if j < DOWN_UNITS - 1:
                return unit_used, e * MOE_USED + used_before_moe[0] + 2 * NCB + j + 1
            return moe_full[4], e * 2 + 1

        def after_reader(c, n_steps):
            if c == 0:
                b, n = banks.uses[("pp", 1, 1, 1)]
                return banks.full[b], n
            assert c == 1
            return unit_used, n_steps * MOE_USED + used_before_moe[0] + 1

        @block.sync
        def _(sp):
            def load(g, src, k, n):
                sp.dma_start(raw(g, k * n).rearrange("p (k n) -> p k n", k=k), src).then_inc(loaded[g % SLOTS], 16)

            for t in range(NT):
                sp.dma_start(h[:, t, :], x[0, t * P:t * P + P, :]).then_inc(x_in[t], 16)
            sp.dma_start(par[:, :], params).then_inc(params_in, 16)
            for g, u in enumerate(before_moe):
                if g >= SLOTS:
                    sp.wait_ge(lo_ready, g - SLOTS + 1)
                load(g, *u)

            def expert(e, weights):
                for c in range(EXPERT_UNITS):
                    sp.wait_ge(lo_ready, e * EXPERT_UNITS + N0 + c - SLOTS + 1)
                    load(N0 + c, *swiglu_unit(*weights, c))

            expert(0, (moe_g[0, 0], moe_u[0, 0], moe_d[0, 0]))
            sp.wait_ge(flag_ready, 1)
            n_steps = sp.value_load(flag[0:1, 0:1], min_val=NE, max_val=2 * NE)
            with sp.Fori(1, n_steps) as e:
                ex = sp.snap(e % NE)

                def pick(w):
                    return w[0, bass.ds(ex, 1)].rearrange("a k n -> (a k) n")
                expert(e, (pick(moe_g), pick(moe_u), pick(moe_d)))
            for c, u in enumerate(after_moe):
                sp.wait_ge(lo_ready, n_steps * EXPERT_UNITS + N0 + c - SLOTS + 1)
                load(N0 + c, *u)
            for t in range(NT):
                for half in range(2):
                    sp.wait_ge(out_ready, 2 * t + half + 1)
                    c = slice(half * 512, half * 512 + 512)
                    sp.dma_start(out[0, t * P:t * P + P, c], xs[:, t, c]).then_inc(out_done, 16)
            sp.wait_ge(out_done, 16 * 2 * NT)

        @block.gpsimd
        def _(pool):
            def xbc_taps(L, j):
                pool.wait_ge(*banks.taken(("xbc", L, j)))
                both = slice(2 * j, 2 * j + 2)
                if 4 * L + j:
                    pool.wait_ge(xtap_ready, 4 * L + j)
                weights = lp(L, "sw", 2 * j * SCONV, 2 * SCONV).rearrange("p (m i) -> p m i", m=2)
                for i in range(SCONV - 1):
                    nc.gpsimd.tensor_tensor(tap_parts[i], xpad[:, both, i:i + SEQ],
                                            weights[:, :, i:i + 1].to_broadcast([P, 2, SEQ]),
                                            ALU.mult).then_inc(tap_product, 1)
                for i in range(SCONV - 1):
                    pool.wait_ge(tap_product, (SCONV - 1) * (4 * L + j) + i + 1)
                    ins = nc.gpsimd.tensor_tensor(xbcT[:, both, :], xbcT[:, both, :], tap_parts[i], ALU.add)
                    if i < SCONV - 2:
                        tapped(ins)
                ins.then_inc(xtap_ready, 1)

            def conv_taps(L, j0, j1):
                def product(j):
                    if j == 0:
                        nc.gpsimd.tensor_scalar(cacc[:, 1, :], cpad[:, 1, 0:SEQ], lp(L, "cw", CK), lp(L, "cb", 1),
                                                ALU.mult, ALU.add).then_inc(conv_product, 1)
                        return
                    if j > 2:
                        pool.wait_ge(conv_sum, (POOL_TAPS - 1) * L + j - 2)
                    nc.gpsimd.tensor_tensor(conv_parts[j % 2], cpad[:, 1, j:j + SEQ],
                                            lp(L, "cw", CK + j).to_broadcast([P, SEQ]), ALU.mult).then_inc(
                                                conv_product, 1)
                product(j0)
                for j in range(j0, j1):
                    if j + 1 < j1:
                        product(j + 1)
                    if j:
                        pool.wait_ge(conv_product, POOL_TAPS * L + j + 1)
                        if j > 1:
                            pool.wait_ge(conv_sum, (POOL_TAPS - 1) * L + j - 1)
                        nc.gpsimd.tensor_tensor(cacc[:, 1, :], cacc[:, 1, :], conv_parts[j % 2],
                                                ALU.add).then_inc(conv_sum, 1)

            taps = [0]

            def tapped(ins):
                taps[0] += 1
                ins.then_inc(tap_done, 1)
                pool.wait_ge(tap_done, taps[0])

            pool.dma_start(pos_i[:, :], positions).then_inc(pos_in, 16)
            for L in range(DEPTH):
                if L:
                    banks.filled(pool, ("kv", L - 1, 1))
                pool.dma_start(wq, w_uq[L].rearrange("(k p) n -> p k n", p=P)).then_inc(wsmall_in, 16)
                pool.dma_start(wkv_b[:, :], w_ukv[L]).then_inc(wsmall_in, 16)
                if L == 0:
                    pool.dma_start(rt_v, router[0].rearrange("(k p) n -> p k n", p=P)).then_inc(wsmall_in, 16)
                pool.wait_ge(*banks.taken(("conv", L, 0)))
                conv_taps(L, 0, EARLY_TAPS)
                for j in range(4):
                    xbc_taps(L, j)
                pool.wait_ge(xtap_ready, 4 * (L + 1))
                pool.wait_ge(adt_ready, L + 1)
                for t in range(NT):
                    for g in range(SG):
                        c = t * SH + 4 * g
                        nc.gpsimd.tensor_tensor(dec[:, t, 4 * g:4 * g + 4, :],
                                                tri.unsqueeze(1).to_broadcast([P, 4, P]),
                                                adt[:, c:c + 4].unsqueeze(2).to_broadcast([P, 4, P]),
                                                ALU.mult).then_inc(triadt_ready, 1)
                conv_taps(L, EARLY_TAPS, POOL_TAPS)
                pool.wait_ge(banks.full[banks.uses[("o", L, 1, 1)][0]], banks.uses[("o", L, 1, 1)][1])
                pool.dma_start(ptok, p[L, 0].rearrange("(t p) c -> p t c", p=P)).then_inc(ptok_in, 16)
            pool.wait_ge(*banks.taken(("pT", DEPTH - 1)))
            pool.dma_start(gfin, final_g.rearrange("(a n) -> a n", a=1).to_broadcast([P, D])).then_inc(gfin_in, 16)

        @block.scalar
        def _(act):
            A = nc.scalar.activation

            def split(g, e=0, wait=None):
                act.wait_ge(loaded[g % SLOTS], landed(g, e))
                if wait is not None:
                    act.wait_ge(*wait)
                elif g >= SPLITS:
                    act.wait_ge(*last_reader[g - SPLITS])
                A(part(w_hi, g, sizes[g]), raw(g, sizes[g]), ACT.Copy).then_inc(hi_ready, 1)

            warmings = [0]

            def warm_up():
                warmings[0] += 1
                A(warm, const("ones", 1), ACT.Sqrt).then_inc(table_in, 1)

            def warmed():
                act.wait_ge(table_in, warmings[0])

            def square(k, i, quarters):
                t, half, there = quarters[i]
                act.wait_ge(*there)
                if i == 3:
                    act.wait_ge(sumsq, 4 * k + 1)
                A(squares[i % 3], h[:, t, half * 512:half * 512 + 512], ACT.Square,
                  accum_out=ss[:, 2 * t + half:2 * t + half + 1]).then_inc(sumsq, 1)

            def norm(k, quarters, warm_already=False, squared=0):
                if k and not warm_already:
                    warm_up()
                for i in range(squared, 4):
                    square(k, i, quarters)
                act.wait_ge(sumsq, 4 * (k + 1))
                if k:
                    warmed()
                act.wait_ge(ms_ready, 2 * (k + 1))
                for t in range(NT):
                    half = [b for a, b, _ in quarters if a == t][1]
                    A(rms[:, t:t + 1], ss[:, 2 * t + half:2 * t + half + 1], ACT.Sqrt, scale=1.0 / D,
                      bias=ms[:, t:t + 1]).then_inc(rms_ready, 1)

            def take_xT(k, L, gain):
                for b in range(4):
                    o = banks.filled(act, (("n", k), b))
                    for q in range(2):
                        kt = 2 * b + q
                        last = A(xT_hi[:, kt, :], o[:, q * SEQ:q * SEQ + SEQ], ACT.Copy, scale=lp(L, gain, kt))
                    last.then_inc(x_hi_ready, 1)

            def mixers(L):
                f = L * (N0 - NF)
                split(f + 3)
                o = banks.filled(act, ("conv", L, 1))
                A(csq.rearrange("p m s -> p (m s)"), o, ACT.Sigmoid).then_inc(banks.is_free(("conv", L, 1)), 1)
                split(f + 4)
                if L == 0:
                    act.wait_ge(trig_arg, 1)
                    A(sin_t, tr0, ACT.Sin)
                    A(cos_t, tr1, ACT.Sin).then_inc(trig_ready, 1)
                split(f + 5)
                warm_up()
                for t in range(NT):
                    o = banks.filled(act, ("sm", L, t))
                    for i, (c0, n) in enumerate(((S_CQ, QRANK), (S_CKV, KVRANK))):
                        A(xd[:, t, i * QRANK:i * QRANK + n], o[:, c0:c0 + n], ACT.Square,
                          accum_out=lss[:, 2 * i + t:2 * i + t + 1]).then_inc(lss_ready, 1)
                warmed()
                act.wait_ge(lss_ready, 4 * (L + 1))
                A(lrm[:, 0:2], lss[:, 0:2], ACT.Sqrt, scale=1.0 / QRANK, bias=eps_rms)
                A(lrm[:, 2:4], lss[:, 2:4], ACT.Sqrt, scale=1.0 / KVRANK, bias=eps_rms).then_inc(lrm_ready, 1)
                split(f + 6)

                def take_xbc(j):
                    o = banks.filled(act, ("xbc", L, j))
                    for q in range(2):
                        m = 2 * j + q
                        A(xbcT[:, m, :], o[:, q * SEQ:q * SEQ + SEQ], ACT.Copy,
                          scale=lp(L, "sw", m * SCONV + SCONV - 1))
                    A(xpad[:, 2 * j:2 * j + 2, SCONV - 1:], o.rearrange("p (m s) -> p m s", m=2), ACT.Copy).then_inc(
                        banks.is_free(("xbc", L, j)), 1)

                act.wait_ge(pads_ready, L + 1)
                take_xbc(0)
                act.wait_ge(dtn_ready, L + 1)
                A(dte, dtn, ACT.Exp).then_inc(dte_ready, 1)
                A(nega, lp(L, "alog", 0, SH), ACT.Exp).then_inc(nega_ready, 1)
                split(f + 7)
                o = banks.filled(act, ("cqT", L))
                for k in range(2):
                    last = A(cqT[:, k, :], o[:, k * SEQ:k * SEQ + SEQ], ACT.Copy, scale=lp(L, "qg", k))
                last.then_inc(banks.is_free(("cqT", L)), 1)
                o = banks.filled(act, ("ckvT", L))
                A(ckvT, o[:, 0:SEQ], ACT.Copy, scale=lp(L, "kvg")).then_inc(banks.is_free(("ckvT", L)), 1)
                act.wait_ge(dtu_ready, L + 1)
                A(dtl, dtu, ACT.Ln).then_inc(dtl_ready, 1)
                take_xbc(1)
                split(f + 8)
                take_xbc(2)
                split(f + 9)

                def silu_xbc(m0, m1):
                    for m in range(m0, m1):
                        if m % 2 == 0:
                            act.wait_ge(xtap_ready, 4 * L + m // 2 + 1)
                        A(xbcT[:, m, :], xbcT[:, m, :], ACT.Silu, bias=lp(L, "sb", m)).then_inc(xbc_ready, 1)

                for t in range(NT):
                    o = banks.filled(act, ("q", L, t))
                    A(qf[:, t, :, :], o[:, 0:MH * QD].rearrange("p (h d) -> p h d", h=MH), ACT.Copy).then_inc(
                        banks.is_free(("q", L, t)), 1)
                for t in range(NT):
                    o = banks.filled(act, ("kv", L, t)).rearrange("p (h d) -> p h d", h=MH)
                    A(kf[:, t, :, 0:NOPE], o[:, :, 0:NOPE], ACT.Copy)
                    A(vs[:, t, :, :], o[:, :, NOPE:], ACT.Copy).then_inc(banks.is_free(("kv", L, t)), 1)
                silu_xbc(0, 2)
                take_xbc(3)
                silu_xbc(2, 4)
                split(f + 10)
                for name, buf in (("qT", qT), ("kT", kT)):
                    for t in range(NT):
                        o = banks.filled(act, (name, L, t))
                        A(buf[0:QD, :, t * P:t * P + P], o[0:QD, :].rearrange("p (h s) -> p h s", h=MH),
                          ACT.Copy).then_inc(banks.is_free((name, L, t)), 1)
                silu_xbc(4, XT)
                for t in range(NT):
                    o = banks.filled(act, ("z", L, t))
                    A(z[:, t, :], o, ACT.Silu).then_inc(banks.is_free(("z", L, t)), 1)
                for t in range(NT):
                    act.wait_ge(score_ready, 2 * L + t + 1)
                    for hd in range(MH):
                        i = t * MH + hd
                        A(sc[t][:, hd, :], sc[t][:, hd, :], ACT.Exp, bias=nm[:, i:i + 1],
                          accum_out=den[:, i:i + 1]).then_inc(prob_ready, 1)
                o = banks.filled(act, ("btok", L))
                A(btok.rearrange("p g n -> p (g n)"), o[:, 0:SG * SN], ACT.Copy).then_inc(
                    banks.is_free(("btok", L)), 1)
                act.wait_ge(acsd_ready, L + 1)
                A(dst, dst, ACT.Exp)
                A(ea, acs[:, SH:2 * SH], ACT.Exp).then_inc(ea_ready, 1)
                for t in range(NT):
                    for g in range(SG):
                        act.wait_ge(*banks.taken(("seg", L, t, g)))
                        v = dec[:, t, 4 * g:4 * g + 4, :].rearrange("p h l -> p (h l)")
                        A(v, v, ACT.Exp).then_inc(dec_ready, 1)
                split(f + 11)
                for j in range(3):
                    o = banks.filled(act, ("prT", L, j))
                    A(prT_f[:, j * 512:(j + 1) * 512], o, ACT.Copy).then_inc(banks.is_free(("prT", L, j)), 1)
                o = banks.filled(act, ("st", L))
                A(st, o, ACT.Copy).then_inc(banks.is_free(("st", L)), 1)
                warm_up()
                act.wait_ge(*banks.taken(("mean", L)))
                A(csq.rearrange("p m s -> p (m s)"), cacc.rearrange("p m s -> p (m s)"), ACT.Square).then_inc(
                    csq_ready, 1)

                def take_yT(j):
                    o = banks.filled(act, ("yT", L, j))
                    for q in range(2):
                        m = 2 * j + q
                        last = A(yT_hi[:, 2 + m, :], o[:, q * SEQ:q * SEQ + SEQ], ACT.Copy,
                                 scale=lp(L, "sng", m) if j < 2 else 1.0)
                    last.then_inc(y_hi_ready, 1)

                take_yT(2)
                act.wait_ge(ygz_ready, L + 1)
                for t in range(NT):
                    for g in range(SG):
                        A(dx[:, t, g * SEQ:g * SEQ + SEQ], ytok[:, t, g * SEQ:g * SEQ + SEQ], ACT.Square,
                          accum_out=gss[:, 2 * t + g:2 * t + g + 1]).then_inc(gss_ready, 1)
                act.wait_ge(gss_ready, 4 * (L + 1))
                warmed()
                A(grm, gss, ACT.Sqrt, scale=SG / SSDW, bias=eps_rms).then_inc(grm_ready, 1)
                o = banks.filled(act, ("var", L))
                A(csq.rearrange("p m s -> p (m s)"), o, ACT.Sqrt, bias=eps_ln).then_inc(
                    banks.is_free(("var", L)), 1)
                split(f + 12)
                act.wait_ge(chn_ready, L + 1)
                for m in range(2):
                    last = A(csq[:, m, :], cacc[:, m, :], ACT.Silu, scale=lp(L, "lng", m), bias=lp(L, "lnb", m))
                last.then_inc(conv_hi_ready, 1)
                act.wait_ge(conv_hi_ready, 2 * L + 1)
                A(yT_hi[:, 0:2, :], csq, ACT.Copy).then_inc(conv_hi_ready, 1)
                for j in range(2):
                    take_yT(j)
                for i in range(13, 16):
                    split(f + i)

            act.wait_ge(params_in, 16)
            act.wait_ge(eps_ready, 1)
            quarters = [(t, half) for t in range(NT) for half in range(2)]
            for L in range(DEPTH):
                f = NF + L * (N0 - NF)
                if L == 0:
                    norm(0, [(t, half, (x_in[t], 16)) for t, half in quarters])
                    split(0)
                else:
                    norm(3 * L, h_added, squared=2)
                    split(f - NF + 1)
                take_xT(3 * L, L, "g_attn")
                if L == 0:
                    split(1)
                split(f - NF + 2)
                mixers(L)
                norm(3 * L + 1, [(t, half, banks.taken(("o", L, t, half))) for t, half in quarters])
                split(f + 2)
                take_xT(3 * L + 1, L, "g_ffn")
                if L == 0:
                    h_done = [(t, half, banks.taken(("d", t, half))) for t, half in quarters]
                    for c in range(EXPERT_UNITS):
                        cb = c // 4
                        if c < 4 * NCB and c % 4 == 1:
                            for t in range(NT):
                                o = banks.filled(act, ("g", cb, t))
                                if cb:
                                    act.wait_ge(*banks.taken(("u", cb - 1, t)))
                                A(dsg[:, t, :], o, ACT.Silu).then_inc(banks.is_free(("g", cb, t)), 1)
                        if c < EXPERT_UNITS - 1:
                            split(f + c + SPLITS)
                        if (4 < c < 4 * NCB and c % 4 == 1) or c == 4 * NCB:
                            for t in range(NT):
                                o = banks.filled(act, ("hT", cb - 1, t))
                                A(hT_hi[:, 4 * cb - 4:4 * cb, t * P:t * P + P],
                                  o.rearrange("p (k s) -> p k s", k=4), ACT.Copy).then_inc(h_hi_ready, 1)
                else:
                    act.wait_ge(dv_ready, 1)
                    A(ev, dv, ACT.Exp).then_inc(ev_ready, 1)
                    act.wait_ge(flag_ready, 1)
                    n_steps = act.value_load(flag[0:1, 0:1], min_val=NE, max_val=2 * NE)

                    def take_xg(stepno):
                        for half in range(2):
                            act.wait_ge(moe_full[5 + half], stepno + 1)
                            for q in range(4):
                                kt = 4 * half + q
                                last = A(xg_hi[:, kt, :], psum[:, 5 + half, q * P:q * P + P], ACT.Copy,
                                         scale=lp(1, "g_ffn", kt))
                            last.then_inc(moe_x_hi, 1)

                    take_xg(0)
                    with act.Fori(0, n_steps) as e:
                        for c in range(EXPERT_UNITS):
                            cb = c // 4
                            if c < 4 * NCB and c % 4 == 1:
                                act.wait_ge(moe_full[0], e * NCB + cb + 1)
                                A(sg[:, cb % 2, :], psum[:, 0, :], ACT.Silu).then_inc(moe_free[0], 1)
                            split(N0 + c + SPLITS, e, moe_reader(c, e))
                            if c == 1:
                                act.wait_ge(moe_full[2], e * (NCB + 2) + 1)
                                A(selgT.rearrange("p t s -> p (t s)"), psum[:, 2, 0:NT * P], ACT.Copy).then_inc(
                                    moe_free[2], 1)
                            elif (c < 4 * NCB and c % 4 == 1) or c == 4 * NCB + 2:
                                act.wait_ge(moe_full[2], e * (NCB + 2) + cb + 1)
                                A(ehT_hi[:, 4 * cb - 4:4 * cb, :], psum[:, 2, :].rearrange("p (k s) -> p k s", k=4),
                                  ACT.Copy).then_inc(moe_h_hi, 1)
                        for half in range(2):
                            act.wait_ge(moe_full[3 + half], e * 2 + 1)
                            A(ysb[:, half * 512:half * 512 + 512], psum[:, 3 + half, :], ACT.Copy).then_inc(
                                moe_free[3 + half], 1)
                        take_xg(e + 1)
                    h_done = [(*divmod(i, 2), (moe_free[b], n_steps * MOE_FILLS[b] + 1))
                              for i, (b, _) in enumerate(SCATTER)]
                warm_up()
                o = banks.filled(act, ("pT", L))
                A(pT_hi, o.rearrange("p (k s) -> p k s", k=2), ACT.Copy).then_inc(p_hi_ready, 1)
                norm(3 * L + 2, h_done, warm_already=True)
                if L == 0:
                    split(f + EXPERT_UNITS + 2)
                take_xT(3 * L + 2, L, "g_ple")

                h_added = [(t, half, (h_ready, 4 * L + 2 * half + t + 1)) for half in range(2) for t in range(NT)]

                def first_half_squares():
                    for i in range(2):
                        square(3 * L + 3, i, h_added)

                def gates(half):
                    for t in range(NT):
                        o = banks.filled(act, ("pg", L, half, t))
                        buf = sg if half == 0 else hs
                        A(buf[:, t, :], o, ACT.Sigmoid).then_inc(banks.is_free(("pg", L, half, t)), 1)

                f = NF + EXPERT_UNITS
                if L == 0:
                    split(f + 3)
                    gates(0)
                    split(f + 4)
                    split(f + 5)
                    first_half_squares()
                    gates(1)
                else:
                    split(N0 + 3, n_steps, after_reader(0, n_steps))
                    split(N0 + 4, n_steps, after_reader(1, n_steps))
                    gates(0)
                    first_half_squares()
                    gates(1)
            norm(3 * DEPTH, h_added, squared=2)

        @block.vector
        def _(dve):
            V = nc.vector
            steps = [0]

            def step(ins):
                steps[0] += 1
                ins.then_inc(dve_step, 1)
                dve.wait_ge(dve_step, steps[0])

            def rms_of(k, by_half):
                for t in range(NT):
                    i = t if by_half else 2 * t
                    dve.wait_ge(sumsq, 4 * k + i + 1)
                    V.tensor_scalar(ms[:, t:t + 1], ss[:, 2 * t:2 * t + 1], 1.0 / D, RMS_EPS, ALU.mult,
                                    ALU.add).then_inc(ms_ready, 1)
                dve.wait_ge(rms_ready, NT * (k + 1))
                step(V.reciprocal(rstd, rms))

            def norm(k, by_half=False):
                rms_of(k, by_half)
                for t in range(NT):
                    V.tensor_scalar(diag[:, t, :], ident, rstd[:, t:t + 1], None, ALU.mult).then_inc(xs_ready, 1)

            def f32(v):
                return v.bitcast(F32)

            def split(g, e=0):
                dve.wait_ge(hi_ready, e * EXPERT_UNITS + g + 1)
                V.tensor_tensor(part(w_lo, g, sizes[g]), raw(g, sizes[g]), f32(part(w_hi, g, sizes[g])),
                                ALU.subtract).then_inc(lo_ready, 1)

            def rest(lo, exact, hi, gain=None):
                if gain is None:
                    return V.tensor_tensor(lo, exact, f32(hi), ALU.subtract)
                return V.scalar_tensor_tensor(out=lo, in0=exact, scalar=gain, in1=f32(hi), op0=ALU.mult,
                                              op1=ALU.subtract)

            def take_xT(k, L, gain):
                for b in range(4):
                    dve.wait_ge(x_hi_ready, 4 * k + b + 1)
                    o = banks.filled(dve, (("n", k), b))
                    for q in range(2):
                        kt = 2 * b + q
                        last = rest(xT_lo[:, kt, :], o[:, q * SEQ:q * SEQ + SEQ], xT_hi[:, kt, :], lp(L, gain, kt))
                    last.then_inc(banks.is_free((("n", k), b)), 1)

            def bc(v, n):
                return v.unsqueeze(len(v.shape)).to_broadcast(list(v.shape) + [n])

            def heads(v, n=SH):
                return v.rearrange("p (h d) -> p h d", h=n)

            def rotate(x1, x2, c, s, t1, t2, t3, t4):
                V.tensor_tensor(t1, x1, c, ALU.mult)
                V.tensor_tensor(t2, x2, s, ALU.mult)
                V.tensor_tensor(t3, x1, s, ALU.mult)
                step(V.tensor_tensor(t4, x2, c, ALU.mult))
                V.tensor_tensor(x1, t1, t2, ALU.subtract)
                return V.tensor_tensor(x2, t3, t4, ALU.add)

            def angles():
                dve.wait_ge(pos_in, 16)
                step(V.tensor_copy(posf, pos_i[:, :]))
                for t in range(NT):
                    last = V.tensor_scalar(tr0[:, t * HR:t * HR + HR], const("inv", HR), posf[:, t:t + 1], None,
                                           ALU.mult)
                step(last)
                two_pi = 2 * np.pi
                big = 1.5 * 2 ** 23
                step(V.tensor_scalar(tr1, tr0, 1 / two_pi, big, ALU.mult, ALU.add))
                step(V.tensor_scalar(tr1, tr1, -big, None, ALU.add))
                c1 = 6.28125
                c2 = float(np.floor((two_pi - c1) * 2 ** 17) / 2 ** 17)
                c3 = float(np.floor((two_pi - c1 - c2) * 2 ** 28) / 2 ** 28)
                c4 = float(np.float32(two_pi - c1 - c2 - c3))
                for c in (c1, c2, c3, c4):
                    step(V.scalar_tensor_tensor(out=tr0, in0=tr1, scalar=-c, in1=tr0, op0=ALU.mult, op1=ALU.add))
                pi = 3.1415925
                step(V.tensor_scalar(tr0, tr0, pi, -pi, ALU.min, ALU.max))
                step(V.scalar_tensor_tensor(out=tr2, in0=tr0, scalar=-1.0, in1=tr0, op0=ALU.mult, op1=ALU.min))
                V.tensor_scalar(tr1, tr2, float(np.pi / 2), None, ALU.add).then_inc(trig_arg, 1)

            def mixers(L):
                V.memset(cpad[:, :, 0:CK - 1], 0.0)
                V.memset(xpad[:, :, 0:SCONV - 1], 0.0).then_inc(pads_ready, 1)
                dve.wait_ge(pads_ready, L + 1)
                f = L * (N0 - NF)

                def conv_taps(j0, j1, m=0):
                    for j in range(j0, j1):
                        src, w = cpad[:, m, j:j + SEQ], lp(L, "cw", m * CK + j)
                        o = csq[:, 1, :] if m else cacc[:, 0, :]
                        if j == (POOL_TAPS if m else 0):
                            ins = V.tensor_scalar(o, src, w, 0.0 if m else lp(L, "cb"), ALU.mult, ALU.add)
                        else:
                            ins = V.scalar_tensor_tensor(out=o, in0=src, scalar=w, in1=o, op0=ALU.mult, op1=ALU.add)
                        step(ins)

                if L == 0:
                    angles()
                split(f + 3)
                dve.wait_ge(*banks.taken(("conv", L, 1)))
                o = banks.filled(dve, ("conv", L, 0))
                V.tensor_tensor(cpad[:, :, CK - 1:], o.rearrange("p (m s) -> p m s", m=2),
                                csq, ALU.mult).then_inc(banks.is_free(("conv", L, 0)), 1)
                dve.wait_ge(*banks.taken(("conv", L, 0)))
                split(f + 4)
                conv_taps(0, 3)
                split(f + 5)
                conv_taps(3, 8)
                dve.wait_ge(lss_ready, 4 * (L + 1))
                so = [banks.filled(dve, ("sm", L, t)) for t in range(NT)]
                for t in range(NT):
                    ins = V.tensor_tensor(dtx[:, t * SH:t * SH + SH], so[t][:, 0:SH], lp(L, "dtb", 0, SH), ALU.add)
                step(ins)
                V.scalar_tensor_tensor(out=dtn, in0=dtx, scalar=-1.0, in1=dtx, op0=ALU.mult, op1=ALU.min).then_inc(
                    dtn_ready, 1)
                for t in range(NT):
                    V.tensor_copy(sm[:, t, S_KR:S_KR + ROPE], so[t][:, S_KR:S_KR + ROPE])
                dve.wait_ge(lrm_ready, L + 1)
                step(V.reciprocal(lrs, lrm))
                for t in range(NT):
                    V.tensor_scalar(sm[:, t, S_CQ:S_CQ + QRANK], so[t][:, S_CQ:S_CQ + QRANK], lrs[:, t:t + 1],
                                    None, ALU.mult)
                    V.tensor_scalar(sm[:, t, S_CKV:S_CKV + KVRANK], so[t][:, S_CKV:S_CKV + KVRANK],
                                    lrs[:, 2 + t:3 + t], None, ALU.mult).then_inc(banks.is_free(("sm", L, t)), 1)
                split(f + 6)
                dve.wait_ge(dte_ready, L + 1)
                V.tensor_scalar(dtu, dte, 1.0, None, ALU.add).then_inc(dtu_ready, 1)
                dve.wait_ge(dtu_ready, L + 1)
                conv_taps(8, 12)
                step(V.scalar_tensor_tensor(out=dtc, in0=dtu, scalar=-1.0, in1=dte, op0=ALU.add, op1=ALU.subtract))
                step(V.reciprocal(dtn, dtu))
                step(V.tensor_tensor(dtc, dtc, dtn, ALU.mult))
                split(f + 7)
                conv_taps(12, 15)
                dve.wait_ge(dtl_ready, L + 1)
                step(V.tensor_tensor(dtc, dtl, dtc, ALU.subtract))
                step(V.scalar_tensor_tensor(out=dt, in0=dtx, scalar=0.0, in1=dtc, op0=ALU.max, op1=ALU.add))
                dve.wait_ge(nega_ready, L + 1)
                for t in range(NT):
                    last = V.scalar_tensor_tensor(out=adt[:, t * SH:t * SH + SH], in0=dt[:, t * SH:t * SH + SH],
                                                  scalar=-1.0, in1=nega, op0=ALU.mult, op1=ALU.mult)
                last.then_inc(adt_ready, 1)
                if L == 0:
                    dve.wait_ge(trig_ready, 1)
                c3 = cos_t.rearrange("p (t r) -> p t r", t=NT)
                s3 = sin_t.rearrange("p (t r) -> p t r", t=NT)
                tmp = [ctmp[:, i * NT * HR:(i + 1) * NT * HR].rearrange("p (t r) -> p t r", t=NT) for i in range(4)]
                step(rotate(sm[:, :, S_KR:S_KR + HR], sm[:, :, S_KR + HR:S_KR + ROPE], c3, s3, *tmp))
                for t in range(NT):
                    V.tensor_copy(kf[:, t, :, NOPE:],
                                  sm[:, t, S_KR:S_KR + ROPE].unsqueeze(1).to_broadcast([P, MH, ROPE]))
                split(f + 8)
                conv_taps(15, 23)
                for t in range(NT):
                    dve.wait_ge(*banks.taken(("q", L, t)))
                    ct = c3[:, t:t + 1, :].to_broadcast([P, MH, HR])
                    s_ = s3[:, t:t + 1, :].to_broadcast([P, MH, HR])
                    tmp = [xdd[:, i * MH * HR:(i + 1) * MH * HR].rearrange("p (h r) -> p h r", h=MH)
                           for i in range(4)]
                    last = rotate(qf[:, t, :, NOPE:NOPE + HR], qf[:, t, :, NOPE + HR:], ct, s_, *tmp)
                    if t < NT - 1:
                        step(last)
                last.then_inc(qk_ready, 1)
                split(f + 9)
                conv_taps(23, CK)
                split(f + 10)
                conv_taps(POOL_TAPS, POOL_TAPS + 5, 1)
                o = banks.filled(dve, ("acs", L))
                V.tensor_copy(acs, o[:, 0:3 * SH]).then_inc(banks.is_free(("acs", L)), 1)
                dve.wait_ge(*banks.taken(("acs", L)))
                V.tensor_tensor(dst, acs[:, 2 * SH:], acs[:, 0:SH], ALU.subtract).then_inc(acsd_ready, 1)
                dve.wait_ge(xtap_ready, 4 * (L + 1))
                for t in range(NT):
                    o = banks.filled(dve, ("xtok", L, t))
                    V.tensor_tensor(heads(xd[:, t, :]), heads(o), bc(dt[:, t * SH:t * SH + SH], SHD), ALU.mult)
                    V.tensor_tensor(heads(dx[:, t, :]), heads(o), bc(lp(L, "dskip", 0, SH), SHD),
                                    ALU.mult).then_inc(banks.is_free(("xtok", L, t)), 1)
                    dve.wait_ge(*banks.taken(("xtok", L, t)))
                scale = float(QD) ** -0.5
                o = banks.filled(dve, ("sc", L, 0))
                step(V.scalar_tensor_tensor(out=sc[0], in0=heads(o, MH), scalar=scale,
                                            in1=mask[:, P:].unsqueeze(1).to_broadcast([P, MH, P]),
                                            op0=ALU.mult, op1=ALU.add))
                V.tensor_reduce(rden[:, 0:4], sc[0], AX.X, ALU.max).then_inc(banks.is_free(("sc", L, 0)), 1)
                dve.wait_ge(*banks.taken(("sc", L, 0)))
                V.tensor_scalar(nm[:, 0:4], rden[:, 0:4], -1.0, None, ALU.mult).then_inc(score_ready, 1)
                for j in range(2):
                    o = banks.filled(dve, ("sc", L, 1 + j))
                    v = sc[1][:, 2 * j:2 * j + 2, :]
                    step(V.scalar_tensor_tensor(out=v, in0=heads(o, 2), scalar=scale,
                                                in1=mask.unsqueeze(1).to_broadcast([P, 2, SEQ]),
                                                op0=ALU.mult, op1=ALU.add))
                    V.tensor_reduce(rden[:, 4 + 2 * j:6 + 2 * j], v, AX.X, ALU.max).then_inc(
                        banks.is_free(("sc", L, 1 + j)), 1)
                    dve.wait_ge(*banks.taken(("sc", L, 1 + j)))
                V.tensor_scalar(nm[:, 4:8], rden[:, 4:8], -1.0, None, ALU.mult).then_inc(score_ready, 1)
                o = banks.filled(dve, ("cb", L))
                V.tensor_tensor(cbm.rearrange("p t g l -> p (t g) l"), o.rearrange("p (a l) -> p a l", l=P),
                                tri.unsqueeze(1).to_broadcast([P, NT * SG, P]), ALU.mult).then_inc(
                                    banks.is_free(("cb", L)), 1)
                for t in range(NT):
                    for g in range(SG):
                        o = banks.filled(dve, ("seg", L, t, g))
                        for i in range(4):
                            hd = 4 * g + i
                            c = t * SH + hd
                            last = V.tensor_scalar(dec[:, t, hd, :], o[:, i * P:i * P + P], acs[:, c:c + 1], 0.0,
                                                   ALU.subtract, ALU.min)
                        last.then_inc(banks.is_free(("seg", L, t, g)), 1)
                dve.wait_ge(ea_ready, L + 1)
                V.tensor_tensor(heads(xdd), heads(xd[:, 0, :]), bc(dst, SHD), ALU.mult).then_inc(xdd_ready, 1)
                for t in range(NT):
                    for g in range(SG):
                        dve.wait_ge(dec_ready, 4 * L + 2 * t + g + 1)
                        v = dec[:, t, 4 * g:4 * g + 4, :]
                        V.tensor_tensor(v, v, cbm[:, t, g:g + 1, :].to_broadcast([P, 4, P]), ALU.mult).then_inc(
                            mix_ready, 1)
                conv_taps(POOL_TAPS + 5, CK, 1)
                dve.wait_ge(conv_sum, (POOL_TAPS - 1) * (L + 1))
                V.tensor_tensor(cacc[:, 1, :], cacc[:, 1, :], csq[:, 1, :], ALU.add).then_inc(conv_ready, 1)
                for t in range(NT):
                    o = banks.filled(dve, ("yd", L, t))
                    V.tensor_tensor(ytok[:, t, 0:SSDW], o, dx[:, t, :], ALU.add).then_inc(
                        banks.is_free(("yd", L, t)), 1)
                o = banks.filled(dve, ("yo", L))
                V.tensor_tensor(heads(xdd), heads(o), bc(ea, SHD), ALU.mult).then_inc(banks.is_free(("yo", L)), 1)
                dve.wait_ge(*banks.taken(("yo", L)))
                step(V.tensor_tensor(ytok[:, 1, 0:SSDW], ytok[:, 1, 0:SSDW], xdd, ALU.add))
                for t in range(NT):
                    dve.wait_ge(*banks.taken(("z", L, t)))
                V.tensor_tensor(ytok[:, :, 0:SSDW], ytok[:, :, 0:SSDW], z, ALU.mult).then_inc(ygz_ready, 1)
                o = banks.filled(dve, ("mean", L))
                c2 = cacc.rearrange("p m s -> p (m s)")
                q2 = csq.rearrange("p m s -> p (m s)")
                V.tensor_tensor(c2, c2, o, ALU.subtract).then_inc(banks.is_free(("mean", L)), 1)
                dve.wait_ge(prob_ready, 8 * (L + 1))
                step(V.reciprocal(rden, den))
                o = banks.filled(dve, ("pv", L))
                for t in range(NT):
                    last = V.tensor_tensor(heads(ytok[:, t, SSDW:], MH), heads(o[:, t * 256:t * 256 + 256], MH),
                                           bc(rden[:, 4 * t:4 * t + 4], VD), ALU.mult)
                last.then_inc(banks.is_free(("pv", L)), 1)
                split(f + 11)

                def take_yT(j, n):
                    dve.wait_ge(y_hi_ready, 3 * L + n)
                    o = banks.filled(dve, ("yT", L, j))
                    for q in range(2):
                        m = 2 * j + q
                        last = rest(yT_lo[:, 2 + m, :], o[:, q * SEQ:q * SEQ + SEQ], yT_hi[:, 2 + m, :],
                                    lp(L, "sng", m) if j < 2 else None)
                    last.then_inc(banks.is_free(("yT", L, j)), 1)

                take_yT(2, 1)
                dve.wait_ge(grm_ready, L + 1)
                step(V.reciprocal(grs, grm))
                for g in range(SG):
                    for t in range(NT):
                        v = ytok[:, t, g * SEQ:g * SEQ + SEQ]
                        last = V.tensor_scalar(v, v, grs[:, 2 * t + g:2 * t + g + 1], None, ALU.mult)
                    last.then_inc(ytok_ready, 1)
                dve.wait_ge(*banks.taken(("var", L)))
                step(V.reciprocal(q2, q2))
                V.tensor_tensor(c2, c2, q2, ALU.mult).then_inc(chn_ready, 1)
                dve.wait_ge(conv_hi_ready, 2 * L + 2)
                rest(yT_lo[:, 0:2, :], csq, yT_hi[:, 0:2, :]).then_inc(yT_ready, 1)
                split(f + 12)
                for j in range(2):
                    take_yT(j, 2 + j)
                for i in range(13, 16):
                    split(f + i)
                for t in range(NT):
                    for half in range(2):
                        o = banks.filled(dve, ("o", L, t, half))
                        v = h[:, t, half * 512:half * 512 + 512]
                        V.tensor_tensor(v, v, o, ALU.add).then_inc(banks.is_free(("o", L, t, half)), 1)

            def embed(L, n_steps):
                f = NF + EXPERT_UNITS
                if L == 0:
                    split(f + 3)
                else:
                    split(N0 + 3, n_steps)
                    split(N0 + 4, n_steps)
                for half in range(2):
                    buf = sg if half == 0 else hs
                    for t in range(NT):
                        dve.wait_ge(*banks.taken(("pg", L, half, t)))
                        o = banks.filled(dve, ("pp", L, half, t))
                        V.tensor_tensor(buf[:, t, :], o, buf[:, t, :], ALU.mult).then_inc(
                            banks.is_free(("pp", L, half, t)), 1)
                        dve.wait_ge(*banks.taken(("pp", L, half, t)))
                        v = h[:, t, half * 512:half * 512 + 512]
                        V.tensor_tensor(v, v, buf[:, t, :], ALU.add).then_inc(h_ready, 1)
                    if L == 0 and half == 0:
                        split(f + 4)
                        split(f + 5)

            def experts():
                for t in range(NT):
                    V.tensor_scalar(xs[:, t, :], h[:, t, :], rstd[:, t:t + 1], None, ALU.mult)
                V.memset(slot_of[:, :, STEPS:], -1.0)
                V.memset(gate_of[:, :, STEPS:], 0.0)
                o = banks.filled(dve, ("lgT",))
                V.tensor_copy(logitsT, o[0:NE, 0:SEQ]).then_inc(banks.is_free(("lgT",)), 1)
                o = banks.filled(dve, ("lg",))
                V.tensor_copy(logits, o[:, 0:NT * NE]).then_inc(banks.is_free(("lg",)), 1)
                dve.wait_ge(*banks.taken(("lg",)))
                blocks = [slice(t * 8, t * 8 + 8) for t in range(NT)]
                for c in blocks:
                    last = V.max(out=top[:, c], in_=logits[:, c])
                step(last)
                for c in blocks:
                    last = V.max_index(out=tinyi[:, c], in_max=top[:, c], in_values=logits[:, c])
                step(last)

                def pairs(v):
                    return v.rearrange("p (t e) -> p t e", t=NT)

                def each(v):
                    return v.unsqueeze(2).to_broadcast([P, NT, NE])

                tops = pairs(top)
                V.tensor_tensor(dv.unsqueeze(2), tops[:, :, 1:2], tops[:, :, 0:1], ALU.subtract).then_inc(dv_ready, 1)
                step(V.tensor_copy(pairs(topi), pairs(tinyi[:, :])[:, :, 0:2]))
                numbers = iota[:, 0:NE].unsqueeze(1).to_broadcast([P, NT, NE])
                V.tensor_tensor(pairs(o1), numbers, pairs(topi)[:, :, 0:1].to_broadcast([P, NT, NE]), ALU.is_equal)
                step(V.tensor_tensor(pairs(o2), numbers, pairs(topi)[:, :, 1:2].to_broadcast([P, NT, NE]),
                                     ALU.is_equal))
                V.tensor_tensor(chosen, o1, o2, ALU.add).then_inc(chosen_ready, 1)
                dve.wait_ge(ev_ready, 1)
                step(V.tensor_scalar(g1, ev, 1.0, None, ALU.add))
                step(V.reciprocal(g1, g1))
                step(V.tensor_tensor(g2, ev, g1, ALU.mult))
                V.tensor_tensor(pairs(o1), pairs(o1), each(g1), ALU.mult)
                step(V.tensor_tensor(pairs(o2), pairs(o2), each(g2), ALU.mult))
                V.tensor_tensor(gate_of[:, :, 0:NE], pairs(o1), pairs(o2), ALU.add)
                V.tensor_tensor(gate_of[:, :, NE:2 * NE], pairs(o1), pairs(o2), ALU.add)
                dve.wait_ge(chosen_ready, 1)
                o = banks.filled(dve, ("rank",))
                step(V.tensor_tensor(rank, o[:, 0:NT * NE], chosen, ALU.mult))
                V.tensor_copy(cnt, o[:, 2 * NE:3 * NE]).then_inc(banks.is_free(("rank",)), 1)
                V.tensor_scalar(slot_of[:, :, NE:2 * NE], pairs(rank), -1.0 - P, None, ALU.add)
                step(V.tensor_scalar(slot_of[:, :, 0:NE], pairs(rank), -1.0, None, ALU.add))

                def build_sel(stepno):
                    for t in range(NT):
                        col = slot_of[:, t, bass.ds(stepno, 1)] if not isinstance(stepno, int) else slot_of[:, t, 0:1]
                        last = V.tensor_scalar(sel[:, t, :], iota, col, None, ALU.is_equal)
                    last.then_inc(sel_ready, 1)

                def take_xg(stepno):
                    for half in range(2):
                        dve.wait_ge(moe_x_hi, stepno * 2 + half + 1)
                        for q in range(4):
                            kt = 4 * half + q
                            last = rest(xg_lo[:, kt, :], psum[:, 5 + half, q * P:q * P + P], xg_hi[:, kt, :],
                                        lp(1, "g_ffn", kt))
                        last.then_inc(moe_free[5 + half], 1)

                build_sel(0)
                dve.wait_ge(*banks.taken(("rank",)))
                step(V.tensor_reduce(mx, cnt, AX.X, ALU.max))
                step(V.tensor_scalar(mx, mx, P + 0.5, float(NE), ALU.is_gt, ALU.mult))
                V.tensor_scalar(flag[:, :], mx, float(NE), None, ALU.add).then_inc(flag_ready, 1)
                dve.wait_ge(flag_ready, 1)
                n_steps = dve.value_load(flag[0:1, 0:1], min_val=NE, max_val=2 * NE)
                take_xg(0)
                with dve.Fori(0, n_steps) as e:
                    for c in range(EXPERT_UNITS):
                        cb = c // 4
                        if c == 0:
                            for t in range(NT):
                                last = V.tensor_scalar(selg[:, t, :], iota, slot_of[:, t, bass.ds(e, 1)],
                                                       gate_of[:, t, bass.ds(e, 1)], ALU.is_equal, ALU.mult)
                            last.then_inc(selg_ready, 1)
                            dve.wait_ge(moe_full[6], e + 1)
                            build_sel(e + 1)
                        split(N0 + c + SPLITS, e)
                        if c < 4 * NCB and c % 4 == 3:
                            dve.wait_ge(moe_free[0], e * NCB + cb + 2)
                            dve.wait_ge(moe_full[1], e * NCB + cb + 1)
                            V.tensor_tensor(hs[:, cb % 2, :], psum[:, 1, :], sg[:, cb % 2, :], ALU.mult).then_inc(
                                moe_free[1], 1)
                        if (4 < c < 4 * NCB and c % 4 == 1) or c == 4 * NCB + 2:
                            dve.wait_ge(moe_h_hi, e * NCB + cb)
                            rest(ehT_lo[:, 4 * cb - 4:4 * cb, :], psum[:, 2, :].rearrange("p (k s) -> p k s", k=4),
                                 ehT_hi[:, 4 * cb - 4:4 * cb, :]).then_inc(moe_free[2], 1)
                    take_xg(e + 1)
                    for i, (b, n) in enumerate(SCATTER):
                        t, half = divmod(i, 2)
                        dve.wait_ge(moe_full[b], e * MOE_FILLS[b] + n)
                        v = h[:, t, half * 512:half * 512 + 512]
                        V.tensor_tensor(v, v, psum[:, b, :], ALU.add).then_inc(moe_free[b], 1)
                dve.wait_ge(moe_free[2], n_steps * MOE_FILLS[2] + 1)
                return n_steps

            V.memset(eps_rms, RMS_EPS)
            V.memset(eps_ln, LN_EPS).then_inc(eps_ready, 1)
            dve.wait_ge(params_in, 16)
            n_steps = None
            for L in range(DEPTH):
                f = NF + L * (N0 - NF)
                norm(3 * L, by_half=L > 0)
                split(0 if L == 0 else f - NF + 1)
                take_xT(3 * L, L, "g_attn")
                if L == 0:
                    split(1)
                split(f - NF + 2)
                mixers(L)
                norm(3 * L + 1)
                split(f + 2)
                take_xT(3 * L + 1, L, "g_ffn")
                if L == 0:
                    dve.wait_ge(wsmall_in, 48)
                    step(V.tensor_copy(rt_hi, rt_v))
                    rest(rt_lo, rt_v, rt_hi).then_inc(rt_ready, 1)
                    for c in range(EXPERT_UNITS):
                        cb = c // 4
                        if c < EXPERT_UNITS - 1:
                            split(f + c + SPLITS)
                        if c < 4 * NCB and c % 4 == 3:
                            for t in range(NT):
                                dve.wait_ge(*banks.taken(("g", cb, t)))
                                o = banks.filled(dve, ("u", cb, t))
                                V.tensor_tensor(dhs[:, t, :], o, dsg[:, t, :], ALU.mult).then_inc(
                                    banks.is_free(("u", cb, t)), 1)
                        if (4 < c < 4 * NCB and c % 4 == 1) or c == 4 * NCB:
                            for t in range(NT):
                                dve.wait_ge(h_hi_ready, NT * (cb - 1) + t + 1)
                                o = banks.filled(dve, ("hT", cb - 1, t))
                                w = (slice(None), slice(4 * cb - 4, 4 * cb), slice(t * P, t * P + P))
                                rest(hT_lo[w], o.rearrange("p (k s) -> p k s", k=4), hT_hi[w]).then_inc(
                                    banks.is_free(("hT", cb - 1, t)), 1)
                    for t in range(NT):
                        for half in range(2):
                            o = banks.filled(dve, ("d", t, half))
                            v = h[:, t, half * 512:half * 512 + 512]
                            V.tensor_tensor(v, v, o, ALU.add).then_inc(banks.is_free(("d", t, half)), 1)
                else:
                    n_steps = experts()
                dve.wait_ge(p_hi_ready, L + 1)
                o = banks.filled(dve, ("pT", L))
                rest(pT_lo, o.rearrange("p (k s) -> p k s", k=2), pT_hi).then_inc(banks.is_free(("pT", L)), 1)
                norm(3 * L + 2)
                if L == 0:
                    split(f + EXPERT_UNITS + 2)
                take_xT(3 * L + 2, L, "g_ple")
                embed(L, n_steps)
            k = 3 * DEPTH
            rms_of(k, by_half=True)
            dve.wait_ge(gfin_in, 16)
            for t in range(NT):
                for c in (slice(0, 512), slice(512, D)):
                    V.scalar_tensor_tensor(out=xs[:, t, c], in0=h[:, t, c], scalar=rstd[:, t:t + 1], in1=gfin[:, c],
                                           op0=ALU.mult, op1=ALU.mult).then_inc(out_ready, 1)


def _constants():
    i = np.arange(P)
    group = (i[:, None] // 64 == i[None, :] // 64) / np.float32(64)
    mask = np.zeros((P, 2 * P))
    mask[:, P:] = np.where(i[:, None] >= i[None, :], 0.0, NEG)
    inv = np.float32(10000.0) ** (-np.arange(0, ROPE, 2, dtype=np.float32) / np.float32(ROPE))
    parts = [np.eye(P), i[:, None] <= i[None, :], np.ones((P, P)), group, np.tile(i, (P, 1)), mask,
             np.tile(inv, (P, 1))]
    return [a.astype(np.float32) for a in parts]


def _by_partition(a):
    a = np.asarray(a)
    return np.moveaxis(a.reshape(a.shape[:-1] + (-1, P)), -1, 0)


def _spread(a):
    return np.broadcast_to(np.asarray(a)[None], (P,) + np.asarray(a).shape)


def kernel(**inputs):
    import concourse.bacc as bacc
    from concourse.bass_utils import run_bass_kernel_spmd

    v = {k: np.asarray(a) for k, a in inputs.items()}
    parts = _constants()
    for L in range(DEPTH):
        parts += [_by_partition(v["attn_norm_g"][L]), _by_partition(v["ffn_norm_g"][L]),
                  _by_partition(v["ple_norm_g"][L]),
                  _by_partition(v["conv_dw_w"][L]).transpose(0, 2, 1).reshape(P, -1),
                  _by_partition(v["conv_dw_b"][L]), _by_partition(v["conv_ln_g"][L]),
                  _by_partition(v["conv_ln_b"][L]),
                  _by_partition(v["ssd_conv_w"][L]).transpose(0, 2, 1).reshape(P, -1),
                  _by_partition(v["ssd_conv_b"][L]), _spread(v["ssd_dt_bias"][L]), _spread(v["ssd_a_log"][L]),
                  _spread(v["ssd_d"][L]), _by_partition(v["ssd_norm_g"][L]), _by_partition(v["mla_q_norm_g"][L]),
                  _by_partition(v["mla_kv_norm_g"][L])]
    params = np.ascontiguousarray(np.concatenate(parts, axis=1))
    v["positions"] = v["positions"].reshape(NT, P).T
    names = ["x", "p", "positions", "w_in", "mla_w_uq", "mla_w_ukv", "w_out", "dense_w_gate", "dense_w_up",
             "dense_w_down", "moe_router", "moe_w_gate", "moe_w_up", "moe_w_down", "ple_w_gate", "ple_w_proj",
             "final_norm_g"]
    arrays = {"params": params, **{n: np.ascontiguousarray(v[n]) for n in names}}
    nc = bacc.Bacc("TRN2", target_bir_lowering=False, num_devices=1)
    args = [nc.dram_tensor("in_" + n, a.shape, mybir.dt.from_np(a.dtype), kind="ExternalInput").ap()
            for n, a in arrays.items()]
    out = nc.dram_tensor("out", (1, SEQ, D), F32, kind="ExternalOutput").ap()
    trunk(nc, *args, out)
    r = run_bass_kernel_spmd(nc, [{"in_" + n: a for n, a in arrays.items()}], core_ids=[0])
    return r.results[0]["out"]
```
